# Optimizing a Trainium2 kernel written in Bass

```python
import math
import jax
import jax.numpy as jnp
from jax import lax
import numpy as np
import jax, jax.numpy as jnp

D_MODEL = 1024
BATCH = 1
SEQ = 256
DEPTH = 2

A_HEADS = 4
A_DK = 128
A_DV = 256
A_QK = A_HEADS * A_DK
A_V = A_HEADS * A_DV
GATE_SOFT_CAP = 15.0
B_HEADS = 8
B_DK = 128
B_DV = 128
B_WIDTH = B_HEADS * B_DK
CONV_K = 4
CHUNK = 64
D_FF = ((8 * D_MODEL // 3 + 255) // 256) * 256
DEEPNORM_ALPHA = (2.0 * DEPTH) ** 0.25
DEEPNORM_BETA = (8.0 * DEPTH) ** -0.25
LN_EPS = 1e-5
RMS_EPS = 1e-6
IN_SIZES = (A_QK, A_QK, A_V, A_V, A_HEADS, A_HEADS, 3 * B_WIDTH, B_WIDTH, B_HEADS, B_HEADS, D_MODEL, D_MODEL)
N_IN = sum(IN_SIZES)
SPLIT_POINTS = tuple(int(v) for v in np.cumsum(IN_SIZES)[:-1])


def _layernorm(x, g, b):
    xf = x.astype(jnp.float32)
    mu = jnp.mean(xf, -1, keepdims=True)
    var = jnp.mean(jnp.square(xf - mu), -1, keepdims=True)
    y = (xf - mu) * lax.rsqrt(var + LN_EPS) * g.astype(jnp.float32) + b.astype(jnp.float32)
    return y.astype(x.dtype)

def _head_rmsnorm(h, g):
    return h * lax.rsqrt(jnp.mean(jnp.square(h), -1, keepdims=True) + RMS_EPS) * g.astype(jnp.float32)

def _soft_cap(x):
    return GATE_SOFT_CAP * jnp.tanh(x / GATE_SOFT_CAP)

def _to_chunks(t):
    bsz, s, h = t.shape[:3]
    t = t.reshape((bsz, s // CHUNK, CHUNK, h) + t.shape[3:])
    perm = (1, 0, 3, 2) + tuple(range(4, t.ndim))
    return t.transpose(perm)

def _from_chunks(t):
    nc, bsz, h, l, d = t.shape
    return t.transpose(1, 0, 3, 2, 4).reshape(bsz, nc * l, h, d)

def _causal_conv(u, w):
    k, c = w.shape
    return lax.conv_general_dilated(u, w.astype(u.dtype)[:, None, :], window_strides=(1,), padding=[(k - 1, 0)],
                                    dimension_numbers=('NWC', 'WIO', 'NWC'), feature_group_count=c)

def _mlstm_chunked(q, k, v, i_pre, f_pre):
    bsz, _, h, dk = q.shape
    dv = v.shape[-1]
    q = q * (dk ** -0.5)
    li = _soft_cap(i_pre)
    lf = jax.nn.log_sigmoid(_soft_cap(f_pre))
    xs = (_to_chunks(q), _to_chunks(k), _to_chunks(v), _to_chunks(li), _to_chunks(lf))
    causal = jnp.tril(jnp.ones((CHUNK, CHUNK), dtype=bool))

    def step(carry, chunk):
        c_st, n_st, m_st = carry
        qc, kc, vc, lic, lfc = chunk
        g = jnp.cumsum(lfc, -1)
        dmat = jnp.where(causal, g[..., :, None] - g[..., None, :] + lic[..., None, :], -jnp.inf)
        inter = g + m_st[..., None]
        m_t = jnp.maximum(inter, jnp.max(dmat, -1))
        w = jnp.exp(dmat - m_t[..., None])
        s = jnp.einsum('bhtd,bhsd->bhts', qc, kc) * w
        sc = jnp.exp(inter - m_t)
        num = jnp.einsum('bhts,bhsv->bhtv', s, vc) + sc[..., None] * jnp.einsum('bhtd,bhdv->bhtv', qc, c_st)
        den = jnp.sum(s, -1) + sc * jnp.einsum('bhtd,bhd->bht', qc, n_st)
        h_out = num / jnp.maximum(jnp.abs(den), jnp.exp(-m_t))[..., None]
        g_end = g[..., -1]
        dec = g_end[..., None] - g + lic
        m_new = jnp.maximum(g_end + m_st, jnp.max(dec, -1))
        wk = jnp.exp(dec - m_new[..., None])
        carry_scale = jnp.exp(g_end + m_st - m_new)
        c_new = carry_scale[..., None, None] * c_st + jnp.einsum('bhs,bhsd,bhsv->bhdv', wk, kc, vc)
        n_new = carry_scale[..., None] * n_st + jnp.einsum('bhs,bhsd->bhd', wk, kc)
        return (c_new, n_new, m_new), h_out

    init = (jnp.zeros((bsz, h, dk, dv), jnp.float32), jnp.zeros((bsz, h, dk), jnp.float32),
            jnp.zeros((bsz, h), jnp.float32))
    _, hs = lax.scan(step, init, xs)
    return _from_chunks(hs)

def _l2norm(t):
    return t * lax.rsqrt(jnp.sum(jnp.square(t), -1, keepdims=True) + RMS_EPS)

def _gated_delta_chunked(q, k, v, beta, g):
    bsz, _, h, dk = q.shape
    dv = v.shape[-1]
    q = _l2norm(q) * (dk ** -0.5)
    k = _l2norm(k)
    qc, kc, vc = _to_chunks(q), _to_chunks(k), _to_chunks(v)
    bc, gc = _to_chunks(beta), _to_chunks(g)
    gcum = jnp.cumsum(gc, -1)
    incl = jnp.tril(jnp.ones((CHUNK, CHUNK), dtype=bool))
    strict = jnp.tril(jnp.ones((CHUNK, CHUNK), dtype=bool), -1)
    diff = gcum[..., :, None] - gcum[..., None, :]
    decay_mat = jnp.where(incl, jnp.exp(jnp.where(incl, diff, 0.0)), 0.0)
    kk = jnp.einsum('nbhid,nbhjd->nbhij', kc, kc)
    a_low = jnp.where(strict, bc[..., :, None] * kk * decay_mat, 0.0)
    rhs = jnp.concatenate([vc * bc[..., None], kc * (bc * jnp.exp(gcum))[..., None]], -1)
    sol = lax.linalg.triangular_solve(jnp.eye(CHUNK, dtype=jnp.float32) + a_low, rhs, left_side=True, lower=True,
                                      transpose_a=False, conjugate_a=False, unit_diagonal=True)
    u, w = sol[..., :dv], sol[..., dv:]
    attn = jnp.einsum('nbhid,nbhjd->nbhij', qc, kc) * decay_mat
    qe = qc * jnp.exp(gcum)[..., None]
    kd = kc * jnp.exp(gcum[..., -1:] - gcum)[..., None]
    g_end = jnp.exp(gcum[..., -1])

    def step(s_st, chunk):
        uc, wc, ac, qec, kdc, gec = chunk
        v_new = uc - jnp.einsum('bhld,bhdv->bhlv', wc, s_st)
        o = jnp.einsum('bhld,bhdv->bhlv', qec, s_st) + jnp.einsum('bhij,bhjv->bhiv', ac, v_new)
        s_new = s_st * gec[..., None, None] + jnp.einsum('bhld,bhlv->bhdv', kdc, v_new)
        return s_new, o

    init = jnp.zeros((bsz, h, dk, dv), jnp.float32)
    _, os_ = lax.scan(step, init, (u, w, attn, qe, kd, g_end))
    return _from_chunks(os_)

def _layer(x, w_in, b_igate, b_fgate, g_mlstm_norm, conv_w, a_log, dt_bias, g_gdn_norm,
           w_branch_a, w_branch_b, w_out, ln1_g, ln1_b, w_ffn_up, w_ffn_down, ln2_g, ln2_b):
    bsz, s, _ = x.shape
    f32 = jnp.float32
    proj = jnp.einsum('bsd,dn->bsn', x, w_in)
    qa, ka, va, oa, ia, fa, qkv_b, zb, beta_b, a_b, gate_a, gate_b = jnp.split(proj, SPLIT_POINTS, axis=-1)

    ha = _mlstm_chunked(qa.reshape(bsz, s, A_HEADS, A_DK).astype(f32),
                        ka.reshape(bsz, s, A_HEADS, A_DK).astype(f32),
                        va.reshape(bsz, s, A_HEADS, A_DV).astype(f32),
                        ia.astype(f32) + b_igate.astype(f32),
                        fa.astype(f32) + b_fgate.astype(f32))
    ha = _head_rmsnorm(ha, g_mlstm_norm.reshape(A_HEADS, A_DV)).reshape(bsz, s, A_V)
    ha = (ha * jax.nn.sigmoid(oa.astype(f32))).astype(x.dtype)

    qkv = jax.nn.silu(_causal_conv(qkv_b, conv_w))
    qb, kb, vb = jnp.split(qkv, [B_WIDTH, 2 * B_WIDTH], axis=-1)
    beta = jax.nn.sigmoid(beta_b.astype(f32))
    g = -jnp.exp(a_log.astype(f32)) * jax.nn.softplus(a_b.astype(f32) + dt_bias.astype(f32))
    hb = _gated_delta_chunked(qb.reshape(bsz, s, B_HEADS, B_DK).astype(f32),
                              kb.reshape(bsz, s, B_HEADS, B_DK).astype(f32),
                              vb.reshape(bsz, s, B_HEADS, B_DV).astype(f32), beta, g)
    hb = _head_rmsnorm(hb, g_gdn_norm).reshape(bsz, s, B_WIDTH)
    hb = (hb * jax.nn.silu(zb.astype(f32))).astype(x.dtype)

    y = (jax.nn.sigmoid(gate_a) * jnp.einsum('bsc,cd->bsd', ha, w_branch_a)
         + jax.nn.sigmoid(gate_b) * jnp.einsum('bsc,cd->bsd', hb, w_branch_b))
    mix = jnp.einsum('bsd,de->bse', y, w_out)
    x = _layernorm(DEEPNORM_ALPHA * x + mix, ln1_g, ln1_b)

    gu = jnp.einsum('bsd,df->bsf', x, w_ffn_up)
    gt, up = jnp.split(gu, [D_FF], axis=-1)
    ffn = jnp.einsum('bsf,fd->bsd', jax.nn.silu(gt) * up, w_ffn_down)
    x = _layernorm(DEEPNORM_ALPHA * x + ffn, ln2_g, ln2_b)
    return x

def first_inputs(seed: int = 0) -> dict:
    key = jax.random.key(seed)
    ks = jax.random.split(key, 20)
    f32 = jnp.float32

    def nrm(k, shape, scale):
        return jax.random.normal(k, shape, f32) * scale

    x = nrm(ks[0], (BATCH, SEQ, D_MODEL), 1.0)
    w_in = nrm(ks[1], (DEPTH, D_MODEL, N_IN), D_MODEL ** -0.5)
    b_igate = -2.0 + nrm(ks[2], (DEPTH, A_HEADS), 0.3)
    b_fgate = 3.0 + jax.random.uniform(ks[3], (DEPTH, A_HEADS), f32, 0.0, 3.0)
    g_mlstm_norm = 1.0 + nrm(ks[4], (DEPTH, A_V), 0.02)
    conv_w = nrm(ks[5], (DEPTH, CONV_K, 3 * B_WIDTH), CONV_K ** -0.5)
    a_log = jnp.log(jax.random.uniform(ks[6], (DEPTH, B_HEADS), f32, 1.0, 16.0))
    dt = jnp.exp(jax.random.uniform(ks[7], (DEPTH, B_HEADS), f32, math.log(1e-3), math.log(1e-1)))
    dt_bias = dt + jnp.log(-jnp.expm1(-dt))
    g_gdn_norm = 1.0 + nrm(ks[8], (DEPTH, B_DV), 0.02)
    w_branch_a = nrm(ks[9], (DEPTH, A_V, D_MODEL), A_V ** -0.5)
    w_branch_b = nrm(ks[10], (DEPTH, B_WIDTH, D_MODEL), B_WIDTH ** -0.5)
    w_out = nrm(ks[11], (DEPTH, D_MODEL, D_MODEL), D_MODEL ** -0.5 * DEEPNORM_BETA)
    ln1_g = 1.0 + nrm(ks[12], (DEPTH, D_MODEL), 0.02)
    ln1_b = nrm(ks[13], (DEPTH, D_MODEL), 0.02)
    w_ffn_up = nrm(ks[14], (DEPTH, D_MODEL, 2 * D_FF), D_MODEL ** -0.5)
    w_ffn_down = nrm(ks[15], (DEPTH, D_FF, D_MODEL), D_FF ** -0.5 * DEEPNORM_BETA)
    ln2_g = 1.0 + nrm(ks[16], (DEPTH, D_MODEL), 0.02)
    ln2_b = nrm(ks[17], (DEPTH, D_MODEL), 0.02)
    return {'x': x, 'w_in': w_in, 'b_igate': b_igate, 'b_fgate': b_fgate, 'g_mlstm_norm': g_mlstm_norm,
            'conv_w': conv_w, 'a_log': a_log, 'dt_bias': dt_bias, 'g_gdn_norm': g_gdn_norm,
            'w_branch_a': w_branch_a, 'w_branch_b': w_branch_b, 'w_out': w_out, 'ln1_g': ln1_g, 'ln1_b': ln1_b,
            'w_ffn_up': w_ffn_up, 'w_ffn_down': w_ffn_down, 'ln2_g': ln2_g, 'ln2_b': ln2_b}

def first_block(x, w_in, b_igate, b_fgate, g_mlstm_norm, conv_w, a_log, dt_bias, g_gdn_norm,
              w_branch_a, w_branch_b, w_out, ln1_g, ln1_b, w_ffn_up, w_ffn_down, ln2_g, ln2_b):
    for l in range(DEPTH):
        x = _layer(x, w_in[l], b_igate[l], b_fgate[l], g_mlstm_norm[l], conv_w[l], a_log[l], dt_bias[l],
                   g_gdn_norm[l], w_branch_a[l], w_branch_b[l], w_out[l], ln1_g[l], ln1_b[l],
                   w_ffn_up[l], w_ffn_down[l], ln2_g[l], ln2_b[l])
    return x


HEAD_DIM = 64
D_RNN = D_MODEL // 2
H_RNN = D_RNN // HEAD_DIM
RNN_BLOCK = D_RNN // H_RNN
CONV_W = 4
RG_C = 8.0
H_FOX = (D_MODEL // 2) // HEAD_DIM
FOX_W = H_FOX * HEAD_DIM
H_SB = D_MODEL // HEAD_DIM
SB_W = H_SB * HEAD_DIM
D_FF_2 = 11 * D_MODEL // 4
Q_BLOCK = 128
N_EVEN = (DEPTH + 1) // 2
N_ODD = DEPTH // 2
HY_IN = 2 * D_RNN + 3 * FOX_W + H_FOX
HY_MIX = D_RNN + FOX_W


def _rmsnorm(x, g):
    x32 = x.astype(jnp.float32)
    y = x32 * lax.rsqrt(jnp.mean(x32 * x32, axis=-1, keepdims=True) + RMS_EPS)
    return (y * g.astype(jnp.float32)).astype(x.dtype)

def _swiglu(h, w_in, w_out):
    a, b = jnp.split(h @ w_in, 2, axis=-1)
    return (jax.nn.silu(a) * b) @ w_out

def _lin_combine(left, right):
    a1, b1 = left
    a2, b2 = right
    return a1 * a2, a2 * b1 + b2

def _rglru_branch(u, gate, conv_w, conv_b, gate_w, gate_b, lam):
    B, S, _ = u.shape
    up = jnp.pad(u, ((0, 0), (CONV_W - 1, 0), (0, 0)))
    xc = conv_b + sum(conv_w[j] * up[:, j:j + S] for j in range(CONV_W))
    xh = xc.reshape(B, S, H_RNN, RNN_BLOCK)
    g = jnp.einsum('bshi,ghij->gbshj', xh, gate_w).reshape(2, B, S, D_RNN) + gate_b[:, None, None, :]
    r = jax.nn.sigmoid(g[0].astype(jnp.float32))
    i = jax.nn.sigmoid(g[1].astype(jnp.float32))
    log_a = -RG_C * r * jax.nn.softplus(-lam.astype(jnp.float32))
    a = jnp.exp(log_a)
    b = jnp.sqrt(-jnp.expm1(2.0 * log_a)) * (i * xc.astype(jnp.float32))
    _, h = lax.associative_scan(_lin_combine, (a, b), axis=1)
    return h.astype(u.dtype) * jax.nn.gelu(gate)

def _to_query_blocks(q):
    B, H, S, d = q.shape
    return q.reshape(B, H, S // Q_BLOCK, Q_BLOCK, d).transpose(2, 0, 1, 3, 4)

def _from_query_blocks(o):
    nb, B, H, QB, d = o.shape
    return o.transpose(1, 0, 3, 2, 4).reshape(B, nb * QB, H * d)

def _fox_attention(q, k, v, logf):
    B, H, S, d = q.shape
    c = jnp.cumsum(logf, axis=-1)
    nb = S // Q_BLOCK
    qb = _to_query_blocks(q)
    cb = c.reshape(B, H, nb, Q_BLOCK).transpose(2, 0, 1, 3)
    kpos = jnp.arange(S)
    scale = d ** -0.5

    def block(args):
        qi, ci, bi = args
        qpos = bi * Q_BLOCK + jnp.arange(Q_BLOCK)
        s = jnp.einsum('bhqd,bhkd->bhqk', qi, k).astype(jnp.float32) * scale
        s = s + ci[..., None] - c[:, :, None, :]
        s = jnp.where(kpos[None, :] <= qpos[:, None], s, -jnp.inf)
        p = jax.nn.softmax(s, axis=-1)
        return jnp.einsum('bhqk,bhkd->bhqd', p.astype(v.dtype), v)

    return _from_query_blocks(lax.map(block, (qb, cb, jnp.arange(nb))))

def _stick_breaking_attention(q, k, v):
    B, H, S, d = q.shape
    nb = S // Q_BLOCK
    qb = _to_query_blocks(q)
    kpos = jnp.arange(S)
    scale = d ** -0.5

    def block(args):
        qi, bi = args
        qpos = bi * Q_BLOCK + jnp.arange(Q_BLOCK)
        mask = kpos[None, :] < qpos[:, None]
        z = jnp.einsum('bhqd,bhkd->bhqk', qi, k).astype(jnp.float32) * scale
        log_nb = jnp.where(mask, jax.nn.log_sigmoid(-z), 0.0)
        after = lax.cumsum(log_nb, axis=3, reverse=True) - log_nb
        w = jnp.where(mask, jnp.exp(jax.nn.log_sigmoid(z) + after), 0.0)
        return jnp.einsum('bhqk,bhkd->bhqd', w.astype(v.dtype), v)

    return _from_query_blocks(lax.map(block, (qb, jnp.arange(nb))))

def _heads(t, n):
    B, S, _ = t.shape
    return t.reshape(B, S, n, HEAD_DIM)

def _hybrid_mixer(h, w_in, conv_w, conv_b, gate_w, gate_b, lam, f_b, qk_g, w_out):
    proj = h @ w_in
    o = 2 * D_RNN
    u, gate, q, k, v, f = jnp.split(proj, [D_RNN, o, o + FOX_W, o + 2 * FOX_W, o + 3 * FOX_W], axis=-1)
    y_rnn = _rglru_branch(u, gate, conv_w, conv_b, gate_w, gate_b, lam)
    qh = _rmsnorm(_heads(q, H_FOX), qk_g[0]).transpose(0, 2, 1, 3)
    kh = _rmsnorm(_heads(k, H_FOX), qk_g[1]).transpose(0, 2, 1, 3)
    vh = _heads(v, H_FOX).transpose(0, 2, 1, 3)
    logf = jax.nn.log_sigmoid((f + f_b).astype(jnp.float32)).transpose(0, 2, 1)
    y_fox = _fox_attention(qh, kh, vh, logf)
    return jnp.concatenate([y_rnn, y_fox], axis=-1) @ w_out

def _sb_mixer(h, w_qkv, w_out):
    q, k, v = jnp.split(h @ w_qkv, 3, axis=-1)
    qh, kh, vh = (_heads(t, H_SB).transpose(0, 2, 1, 3) for t in (q, k, v))
    return _stick_breaking_attention(qh, kh, vh) @ w_out

def second_inputs(seed: int = 0) -> dict:
    key = jax.random.key(seed)
    ks = jax.random.split(key, 20)
    f32 = jnp.float32

    def nrm(k, shape, fan_in):
        return jax.random.normal(k, shape, f32) * (fan_in ** -0.5)

    a0 = jax.random.uniform(ks[9], (N_EVEN, D_RNN), f32, 0.9, 0.999)
    return {
        "x": jax.random.normal(ks[0], (BATCH, SEQ, D_MODEL), f32),
        "ffn_norm": 1.0 + 0.05 * jax.random.normal(ks[1], (DEPTH, 2, D_MODEL), f32),
        "ffn_w_in": nrm(ks[2], (DEPTH, 2, D_MODEL, 2 * D_FF_2), D_MODEL),
        "ffn_w_out": nrm(ks[3], (DEPTH, 2, D_FF_2, D_MODEL), D_FF_2),
        "mix_norm": 1.0 + 0.05 * jax.random.normal(ks[4], (DEPTH, D_MODEL), f32),
        "hy_w_in": nrm(ks[5], (N_EVEN, D_MODEL, HY_IN), D_MODEL),
        "rg_conv_w": nrm(ks[6], (N_EVEN, CONV_W, D_RNN), CONV_W),
        "rg_conv_b": 0.02 * jax.random.normal(ks[7], (N_EVEN, D_RNN), f32),
        "rg_gate_w": nrm(ks[8], (N_EVEN, 2, H_RNN, RNN_BLOCK, RNN_BLOCK), RNN_BLOCK),
        "rg_gate_b": 0.02 * jax.random.normal(ks[10], (N_EVEN, 2, D_RNN), f32),
        "rg_lambda": jnp.log(a0) - jnp.log1p(-a0),
        "fox_fgate_b": jax.random.uniform(ks[11], (N_EVEN, H_FOX), f32, 1.0, 4.0),
        "fox_qk_norm": 1.0 + 0.05 * jax.random.normal(ks[12], (N_EVEN, 2, HEAD_DIM), f32),
        "hy_w_out": nrm(ks[13], (N_EVEN, HY_MIX, D_MODEL), HY_MIX),
        "sb_w_qkv": nrm(ks[14], (N_ODD, D_MODEL, 3 * SB_W), D_MODEL),
        "sb_w_out": nrm(ks[15], (N_ODD, SB_W, D_MODEL), SB_W),
    }

def second_block(x, ffn_norm, ffn_w_in, ffn_w_out, mix_norm, hy_w_in, rg_conv_w, rg_conv_b,
              rg_gate_w, rg_gate_b, rg_lambda, fox_fgate_b, fox_qk_norm, hy_w_out,
              sb_w_qkv, sb_w_out):
    for layer in range(DEPTH):
        x = x + 0.5 * _swiglu(_rmsnorm(x, ffn_norm[layer, 0]), ffn_w_in[layer, 0], ffn_w_out[layer, 0])
        h = _rmsnorm(x, mix_norm[layer])
        if layer % 2 == 0:
            e = layer // 2
            y = _hybrid_mixer(h, hy_w_in[e], rg_conv_w[e], rg_conv_b[e], rg_gate_w[e], rg_gate_b[e],
                              rg_lambda[e], fox_fgate_b[e], fox_qk_norm[e], hy_w_out[e])
        else:
            o = layer // 2
            y = _sb_mixer(h, sb_w_qkv[o], sb_w_out[o])
        x = x + y
        x = x + 0.5 * _swiglu(_rmsnorm(x, ffn_norm[layer, 1]), ffn_w_in[layer, 1], ffn_w_out[layer, 1])
    return x


def setup_inputs(seed=0):
    out = dict(first_inputs(seed))
    for name, value in second_inputs(seed + 1).items():
        if name != "x":
            out[name + "_2"] = value
    return out


def reference(
    x, w_in, b_igate, b_fgate, g_mlstm_norm, conv_w, a_log, dt_bias, g_gdn_norm, w_branch_a,
    w_branch_b, w_out, ln1_g, ln1_b, w_ffn_up, w_ffn_down, ln2_g, ln2_b, ffn_norm_2, ffn_w_in_2,
    ffn_w_out_2, mix_norm_2, hy_w_in_2, rg_conv_w_2, rg_conv_b_2, rg_gate_w_2, rg_gate_b_2,
    rg_lambda_2, fox_fgate_b_2, fox_qk_norm_2, hy_w_out_2, sb_w_qkv_2, sb_w_out_2,
):
    x = first_block(
        x, w_in, b_igate, b_fgate, g_mlstm_norm, conv_w, a_log, dt_bias, g_gdn_norm, w_branch_a,
        w_branch_b, w_out, ln1_g, ln1_b, w_ffn_up, w_ffn_down, ln2_g, ln2_b,
    )
    return second_block(
        x, ffn_norm_2, ffn_w_in_2, ffn_w_out_2, mix_norm_2, hy_w_in_2, rg_conv_w_2, rg_conv_b_2,
        rg_gate_w_2, rg_gate_b_2, rg_lambda_2, fox_fgate_b_2, fox_qk_norm_2, hy_w_out_2,
        sb_w_qkv_2, sb_w_out_2,
    )


_drawn_inputs = setup_inputs


def setup_inputs(seed=0):
    import zlib

    import numpy as np

    out = dict(_drawn_inputs(seed))
    spreads = {}
    factors = {'b_igate': 8.0,
     'g_mlstm_norm': 49.804,
     'g_gdn_norm': 8.0,
     'rg_conv_b_2': 3.22,
     'rg_gate_b_2': 23.084,
     'fox_qk_norm_2': 4.15}
    for name, (base, spread) in spreads.items():
        noise = np.random.default_rng([zlib.crc32(name.encode()), seed]).standard_normal(out[name].shape)
        drawn = base * np.exp(spread * noise) if base else spread * noise
        out[name] = jnp.asarray(drawn.astype(out[name].dtype))
    for name, factor in factors.items():
        out[name] = (out[name] * factor).astype(out[name].dtype)
    return out
```

```python
import math
from contextlib import ExitStack

import numpy as np

import concourse.bass as bass
from concourse import mybir

F32 = mybir.dt.float32
F32R = mybir.dt.float32r
ALU = mybir.AluOpType
ACT = mybir.ActivationFunctionType
AX = mybir.AxisListType

P = 128
DEPTH = 2
D = 1024
S = 256
TT = S // P
KT = D // P
D_FF = 2816
FPAIRS = D_FF // (2 * P)
UNIT = 2048
RING = 3
ALPHA = (2.0 * DEPTH) ** 0.25
LN_EPS = 1e-5
RMS_EPS = 1e-6
BIG = 1e30

A_HEADS, A_DK, A_DV = 4, 128, 256
B_HEADS, B_DK = 8, 128
CAP = 15.0
QKV_UNITS = 12
QKA_UNITS = 4
VA_UNITS = 4
OA_UNITS = 4
BRANCH_UNITS = 8
ZB_UNITS = 4
OUT_UNITS = 4
MIX1_UNITS = QKV_UNITS + QKA_UNITS + VA_UNITS + OA_UNITS + BRANCH_UNITS + ZB_UNITS + BRANCH_UNITS + OUT_UNITS
FFN_UNITS = 3 * FPAIRS
N_GATES = 2 * A_HEADS + 2 * B_HEADS


def split_matmul(pe, out, lhs, rhs, start, stop):
    (lhs_hi, lhs_lo), (rhs_hi, rhs_lo) = lhs, rhs
    pe.matmul(out, lhs_hi, rhs_hi, start=start, stop=False, skip_group_check=True)
    pe.matmul(out, lhs_hi, rhs_lo, start=False, stop=False, skip_group_check=True)
    return pe.matmul(out, lhs_lo, rhs_hi, start=False, stop=stop, skip_group_check=True)


class Chain:

    def __init__(self, engine, sem):
        self.engine, self.sem, self.n = engine, sem, 0

    def step(self, ins):
        ins.then_inc(self.sem, 1)
        self.n += 1

    def settle(self):
        self.engine.wait_ge(self.sem, self.n)


class Weights:

    def __init__(self, nc, enter, raw, hi, lo):
        self.nc, self.raw, self.hi, self.lo = nc, raw, hi, lo
        self.loaded = [enter(nc.semaphore(f"unit_loaded_{i}")) for i in range(RING)]
        self.hi_done = enter(nc.semaphore("unit_hi_done"))
        self.lo_done = enter(nc.semaphore("unit_lo_done"))
        self.used = enter(nc.semaphore("unit_used"))
        self.hi_next = self.lo_next = 0

    def sems(self):
        return [*self.loaded, self.hi_done, self.lo_done, self.used]

    def load(self, sp, src, u, turn=0):
        slot = u % RING
        if u >= RING:
            sp.wait_ge(self.lo_done, u - RING + 1 + RING * turn)
        sp.dma_start(self.raw[:, slot, :], src).then_inc(self.loaded[slot], 16)

    def split_hi(self, act, u, turn=0):
        slot = u % RING
        act.wait_ge(self.loaded[slot], 16 * (u // RING + 1) + 16 * turn)
        if u >= RING:
            act.wait_ge(self.used, u - RING + 1 + RING * turn)
        act.activation(self.hi[:, slot, :], self.raw[:, slot, :], ACT.Copy).then_inc(self.hi_done, 1)

    def split_lo(self, dve, u, turn=0):
        slot = u % RING
        dve.wait_ge(self.hi_done, u + 1 + RING * turn)
        dve.tensor_tensor(self.lo[:, slot, :], self.raw[:, slot, :], self.hi[:, slot, :].bitcast(F32),
                          ALU.subtract).then_inc(self.lo_done, 1)

    def hi_through(self, act, u):
        while self.hi_next <= u:
            self.split_hi(act, self.hi_next)
            self.hi_next += 1

    def lo_through(self, dve, u):
        while self.lo_next <= u:
            self.split_lo(dve, self.lo_next)
            self.lo_next += 1

    def pair(self, u, shape, *index):
        def view(t):
            v = t[:, u % RING, :].rearrange("p (a b) -> p a b", b=shape[1])
            return v[(slice(None), *index)]
        return view(self.hi), view(self.lo)


def ffn_tensor(pe, w, u0, xT, hT, acc, up_ps, zero, sem, xT_ready, xT_by_tile):
    def up(u, turn, first=False):
        for f in range(2):
            pe.wait_ge(w.lo_done, u + f + 1 + RING * turn)
            if not first:
                pe.wait_ge(sem["h_done"], f + 1 + 2 * turn)
            for part in range(2):
                for k in range(KT):
                    if first and f == part == 0:
                        pe.wait_ge(xT_ready, max(k + 1, 2) if xT_by_tile else k // 2 + 1)
                    mm = split_matmul(pe, up_ps[:, f, part * S:(part + 1) * S],
                                      w.pair(u + f, (16, P), part * KT + k, slice(None)),
                                      (xT[0][:, k, :], xT[1][:, k, :]), k == 0, k == KT - 1)
            mm.then_inc(w.used, 1)

    def down(u, turn, pairs_before, last=False):
        pe.wait_ge(w.lo_done, u + 1 + RING * turn)
        pe.wait_ge(sem["hT_ready"], pairs_before + 1 + turn)
        for t in range(TT):
            for f in range(2):
                for half in range(2):
                    mm = split_matmul(pe, acc[:, 2 * t + half, :],
                                      (hT[0][:, f, t * P:(t + 1) * P], hT[1][:, f, t * P:(t + 1) * P]),
                                      w.pair(u, (4, 512), 2 * f + half, slice(None)), False, last and f == 1)
            if last and t < TT - 1:
                mm.then_inc(sem["acc_done"], 1)
        mm.then_inc(w.used, 1)

    up(u0, 0, first=True)
    for b in range(4):
        pe.matmul(acc[:, b, :], zero[:, :], xT[0][:, 0:2, :].rearrange("p a b -> p (a b)"), start=True, stop=False, skip_group_check=True)
    with pe.Fori(0, FPAIRS - 1) as i:
        up(u0 + 2, i)
        down(u0 + 4, i, 0)
    down(u0 + 2 + 3 * (FPAIRS - 1), 0, FPAIRS - 1, last=True)


def ffn_scalar(act, w, u0, up_ps, gate, h, hT_hi, sem, ahead):
    def hidden(u, pair, turn, ahead=0):
        for f in range(2):
            act.wait_ge(w.used, u + f + 1 + RING * turn)
            act.activation(gate[:, f, :], up_ps[:, f, 0:S], ACT.Silu).then_inc(sem["gate_done"], 1)
        if ahead:
            w.hi_through(act, u0 + FFN_UNITS)
        for f in range(2):
            act.wait_ge(sem["h_done"], 2 * pair + f + 1 + 2 * turn)
            if f == 0:
                act.wait_ge(w.used, u + 3 + RING * turn if pair else u + 2)
            act.activation(hT_hi[:, f, :], h[:, f, :], ACT.Copy).then_inc(sem["hT_hi_done"], 1)

    w.hi_through(act, u0 + 2)
    hidden(u0, 0, 0)
    with act.Fori(0, FPAIRS - 2) as i:
        for j in range(3):
            w.split_hi(act, u0 + 3 + j, i)
        hidden(u0 + 2, 1, i)
    w.hi_next = u0 + 3 * (FPAIRS - 1)
    w.hi_through(act, u0 + 3 * FPAIRS - 1)
    hidden(u0 + 2 + 3 * (FPAIRS - 2), FPAIRS - 1, 0, ahead)
    if ahead:
        w.hi_through(act, u0 + FFN_UNITS + 1)


def ffn_vector(dve, w, u0, up_ps, gate, h, hT, sem, ahead):
    def hidden(pair, turn, ahead=0):
        if pair:
            dve.wait_ge(sem["hT_ready"], pair + turn)
        for f in range(2):
            dve.wait_ge(sem["gate_done"], 2 * pair + f + 1 + 2 * turn)
            dve.tensor_tensor(h[:, f, :], gate[:, f, :], up_ps[:, f, S:2 * S], ALU.mult).then_inc(sem["h_done"], 1)
        if ahead:
            w.lo_through(dve, u0 + FFN_UNITS)
        dve.wait_ge(sem["hT_hi_done"], 2 * pair + 2 + 2 * turn)
        dve.tensor_tensor(hT[1][:, :, :], h[:, :, :], hT[0][:, :, :].bitcast(F32), ALU.subtract)\
           .then_inc(sem["hT_ready"], 1)

    w.lo_through(dve, u0 + 2)
    hidden(0, 0)
    with dve.Fori(0, FPAIRS - 2) as i:
        for j in range(3):
            w.split_lo(dve, u0 + 3 + j, i)
        hidden(1, i)
    w.lo_next = u0 + 3 * (FPAIRS - 1)
    w.lo_through(dve, u0 + 3 * FPAIRS - 1)
    hidden(FPAIRS - 1, 0, ahead)
    if ahead:
        w.lo_through(dve, u0 + FFN_UNITS + 1)


def ffn_load_first(sp, w, u0, up_w):
    for f in range(2):
        w.load(sp, up_w(0, f), u0 + f)
    w.load(sp, up_w(1, 0), u0 + 2)


def ffn_load(sp, w, u0, up_w, down_w, first=0):
    if not first:
        ffn_load_first(sp, w, u0, up_w)
    with sp.Fori(0, FPAIRS - 2) as i:
        w.load(sp, up_w(i + 1, 1), u0 + 3, i)
        w.load(sp, down_w(i), u0 + 4, i)
        w.load(sp, up_w(i + 2, 0), u0 + 5, i)
    last = u0 + 3 * (FPAIRS - 1)
    w.load(sp, up_w(FPAIRS - 1, 1), last)
    w.load(sp, down_w(FPAIRS - 2), last + 1)
    w.load(sp, down_w(FPAIRS - 1), last + 2)


def norm_transposes(pe, ps, x, ident, ready, counts, sem):
    for t in range(TT):
        pe.wait_ge(ready, counts[t])
        for j in range(4):
            for k in range(2):
                mm = pe.transpose(ps[:, 4 + j, k * S + t * P:k * S + (t + 1) * P],
                                  x[:, t, (2 * j + k) * P:(2 * j + k + 1) * P], ident[:, :])
            if t == TT - 1:
                mm.then_inc(sem["xT_mm"], 1)


def layer_norm_vector(dve, chain, x, acc, gain, shift, stats, sem):
    mean_var, std, rstd, raw_stats = stats
    for t in range(TT):
        for half in range(2):
            cols = slice(half * 512, (half + 1) * 512)
            chain.step(dve.scalar_tensor_tensor(x[:, t, cols], x[:, t, cols], ALPHA, acc[:, 2 * t + half, :],
                                                ALU.mult, ALU.add))
    chain.settle()
    for t in range(TT):
        for half in range(2):
            chain.step(dve.bn_stats(raw_stats[:, t, half, :], x[:, t, half * 512:(half + 1) * 512]))
    chain.settle()
    for t in range(TT):
        dve.bn_aggr(mean_var[:, t, :], raw_stats[:, t, :, :].rearrange("p a b -> p (a b)")).then_inc(sem["var_done"], 1)
    dve.wait_ge(sem["std_done"], 1)
    chain.step(dve.reciprocal(rstd, std))
    chain.settle()
    for t in range(TT):
        chain.step(dve.tensor_scalar(x[:, t, :], x[:, t, :], mean_var[:, t, 0:1], rstd[:, t:t + 1],
                                     ALU.subtract, ALU.mult))
    chain.settle()
    dve.wait_ge(sem["norm_rows"], 32)
    for t in range(TT):
        chain.step(dve.tensor_tensor(x[:, t, :], x[:, t, :], gain, ALU.mult))
    chain.settle()
    for t in range(TT):
        dve.tensor_tensor(x[:, t, :], x[:, t, :], shift, ALU.add).then_inc(sem["x_normed"], 1)


def layer_norm_scalar(act, stats, eps, sem):
    mean_var, std, _, _ = stats
    act.wait_ge(sem["var_done"], TT)
    act.activation(std, mean_var[:, :, 1], ACT.Sqrt, bias=eps).then_inc(sem["std_done"], 1)


def transposed_scalar(act, ps, xT_hi, sem):
    for j in range(4):
        act.wait_ge(sem["xT_mm"], j + 1)
        act.activation(xT_hi[:, 2 * j:2 * j + 2, :].rearrange("p a b -> p (a b)"), ps[:, 4 + j, :], ACT.Copy)\
           .then_inc(sem["xT_hi_done"], 1)


def transposed_vector(dve, ps, xT, sem):
    for j in range(4):
        dve.wait_ge(sem["xT_hi_done"], j + 1)
        part = slice(2 * j, 2 * j + 2)
        dve.tensor_tensor(xT[1][:, part, :].rearrange("p a b -> p (a b)"), ps[:, 4 + j, :],
                          xT[0][:, part, :].rearrange("p a b -> p (a b)").bitcast(F32),
                          ALU.subtract).then_inc(sem["xT_ready"], 1)


NORM_SEMS = ["var_done", "std_done", "norm_rows", "x_normed", "xT_mm", "xT_hi_done", "xT_ready"]
FFN_SEMS = ["h_done", "hT_ready", "gate_done", "hT_hi_done", "acc_done"]
MIX1_SEMS = [
    "x_loaded", "params", "gate_w_hi", "gate_w", "gates_mm", "cv_zero", "cv_copied", "conv_done", "silu_done", "sq_done",
    "ss_mm", "qka_done", "va_done", "g24", "tanh_done", "z_ready", "ln_done", "decays", "cum_mm", "cums",
    "norms", "exps", "a_ready", "a_rows_mm", "m_rows", "m_cols_mm", "m_ready", "emt", "v_mm", "v_done", "k_mm", "k_done",
    "gb_mm", "diff", "dec_exp", "kkqk_mm", "a_done", "xt_init", "x_mm", "x_init", "p_mm", "p_done", "y_mm", "y_done",
    "ks_mm", "rhs_done", "vn_mm", "vn_done", "o_mm", "o_done", "s_mm", "s_done", "hb_sq", "hb_std",
    "kq_mm", "w_diff", "w_exp", "s_done2", "num_mm", "num_done", "ha_sq", "ha_std", "ha_done",
    "og_done", "hT_mm", "abF", "ab_hi", "ab_done", "sg_done", "yp_done", "yT_hi", "yT_done", "masks",
]
N_SMALL = 640


def block_one(nc, a):
    with ExitStack() as ctx:
        enter = ctx.enter_context

        def sb(name, shape, dt=F32):
            return enter(nc.sbuf_tensor(name, shape, dt))

        ps = enter(nc.psum_tensor("ps", [P, 8, 512], F32))
        raw = sb("raw", [P, RING, UNIT])
        w_hi, w_lo = (sb(n, [P, RING, UNIT], F32R) for n in ("w_hi", "w_lo"))
        x = a["x_sb"]
        xT = [sb(n, [P, KT, S], F32R) for n in ("xT_hi", "xT_lo")]
        abT = [sb(n, [P, KT, S], F32R) for n in ("abT_hi", "abT_lo")]
        hT = [sb(n, [P, 2, S], F32R) for n in ("hT_hi", "hT_lo")]
        wg = [sb(n, [P, KT, N_GATES], F32R) for n in ("wg_hi", "wg_lo")]
        zero = sb("zero", [P, P], F32R)
        qkvT = sb("qkvT", [P, 24, S])
        k_tm = sb("k_tm", [P, TT, B_HEADS, P])
        hb = sb("hb", [P, TT, B_HEADS, P])
        va = sb("va", [P, TT, A_HEADS, A_DV + 1])
        scratch = sb("scratch", [P, 6144])
        cm = sb("cm", [P, a["masks"].shape[1]])
        sel = sb("sel", [A_HEADS, A_HEADS, P])
        pa = sb("pa", [P, 96 + N_GATES + 8 + P + A_HEADS * A_DV])
        rows = sb("rows", [A_HEADS, 2, S])
        sm = sb("sm", [P, N_SMALL])

        ident, tri, strict, ones = (cm[:, i * P:(i + 1) * P] for i in range(4))
        level0 = cm[:, 4 * P:5 * P]
        levels = [cm[:, (5 + i) * P:(6 + i) * P] for i in range(6)]
        conv_w = pa[:, 0:96].rearrange("p (c j) -> p c j", j=4)
        gate_bias = pa[:, 96:96 + N_GATES]
        a_log = pa[:, 120:128]
        g_gdn = pa[:, 128:256]
        g_mlstm = pa[:, 256:256 + A_HEADS * A_DV]

        at = [0]

        def small(*shape):
            n = int(np.prod(shape))
            v = sm[:, at[0]:at[0] + n]
            at[0] += n
            assert at[0] <= N_SMALL
            if len(shape) == 2:
                v = v.rearrange("p (a b) -> p a b", b=shape[1])
            if len(shape) == 3:
                v = v.rearrange("p (a b c) -> p a b c", b=shape[1], c=shape[2])
            return v

        g24, t8, li, z, zabs, sp = small(2, 24), small(2, 8), small(2, 4), small(2, 12), small(2, 12), small(2, 12)
        beta, e_alog, gs, cs, tot = small(2, 8), small(8), small(2, 12), small(2, 12), small(2, 12)
        ssq, nrm, rnrm, eg, neg_eg = small(2, 16), small(2, 16), small(2, 16), small(2, 8), small(2, 8)
        kdf, cj, brk, rq, a_col, m_col, emt = (small(2, 8), small(2, 8), small(2, 8), small(2, 8), small(2, 4),
                                               small(2, 4), small(2, 4))
        den, rs8, rs4, eps_ln, eps_rms, one = small(2, 4), small(2, 8), small(2, 4), small(1), small(1), small(1)
        stats = (small(2, 2), small(2), small(2), small(2, 2, 6))

        cv = scratch[:, 0:1036].rearrange("p (r c t) -> p r c t", r=2, t=259)
        ca = scratch[:, 1040:2064].rearrange("p (r c t) -> p r c t", r=2, t=S)
        sq = scratch[:, 2064:3088].rearrange("p (r c t) -> p r c t", r=2, t=S)
        AT, attn, X, XT, PB, ST8 = (scratch[:, i * 1024:(i + 1) * 1024].rearrange("p (h t) -> p h t", t=P)
                                    for i in range(6))
        mw = scratch[:, 0:768].rearrange("p (r t) -> p r t", r=2)
        mst = scratch[:, 768:1536].rearrange("p (r t) -> p r t", r=2)
        junk = scratch[:, 1536:1792]
        og = scratch[:, 2048:3072].rearrange("p (r t) -> p r t", r=2)
        abF = scratch[:, 3072:4096].rearrange("p (r t) -> p r t", r=2)
        sg = scratch[:, 4096:4608].rearrange("p (r t) -> p r t", r=2)
        ln_gain, ln_shift = scratch[:, 0:1024], scratch[:, 1024:2048]
        gate = scratch[:, 4608:5120].rearrange("p (f t) -> p f t", f=2)
        h = scratch[:, 5120:5632].rearrange("p (f t) -> p f t", f=2)
        wg_raw = scratch[:, 5632:5632 + KT * N_GATES]
        yF = qkvT[:, 16:24, :]
        acc = ps[:, 0:4, :]
        up_ps = ps[:, 4:6, :]
        gates_ps = ps[:, 7, 0:48].rearrange("p (t n) -> p t n", t=TT)
        ss_ps = ps[:, 7, 64:96].rearrange("p (t n) -> p t n", t=TT)
        cum_ps = ps[:, 7, 128:176].rearrange("p (a t n) -> p a t n", a=2, t=TT)
        mcol_ps = ps[:, 7, 192:200].rearrange("p (t n) -> p t n", t=TT)
        arow_ps = ps[0:A_HEADS, 7, 256:512]

        w = Weights(nc, enter, raw, w_hi, w_lo)
        sem = {n: enter(nc.semaphore(n)) for n in MIX1_SEMS}
        norm1 = {n: enter(nc.semaphore(f"{n}_1")) for n in NORM_SEMS}
        norm2 = {n: enter(nc.semaphore(f"{n}_2")) for n in NORM_SEMS + FFN_SEMS}
        steps = {n: enter(nc.semaphore(f"{n}_steps")) for n in ("scalar", "vector")}

        U_QKA = QKV_UNITS
        U_VA = U_QKA + QKA_UNITS
        U_OA = U_VA + VA_UNITS
        U_BA = U_OA + OA_UNITS
        U_ZB = U_BA + BRANCH_UNITS
        U_BB = U_ZB + ZB_UNITS
        U_OUT = U_BB + BRANCH_UNITS
        U_FFN = U_OUT + OUT_UNITS
        assert U_FFN == MIX1_UNITS and U_FFN % RING == 0

        intro = {n: enter(nc.semaphore(f"intro_{n}")) for n in ["loaded", "x_normed", "xT_mm", "xT_hi_done", "xT_ready"]}
        with nc.Block() as block:
            @block.sync
            def _(sp):
                for t in range(TT):
                    sp.dma_start(x[:, t, :], a["x"][0, t * P:(t + 1) * P, :]).then_inc(intro["x_normed"], 16)
                sp.dma_start(cm[:, :], a["masks"]).then_inc(intro["loaded"], 16)
                sp.dma_start(sel[:, :, :], a["sel"]).then_inc(intro["loaded"], 16)
                sp.wait_ge(intro["loaded"], 32)

            @block.tensor
            def _(pe):
                pe.wait_ge(intro["loaded"], 32)
                norm_transposes(pe, ps, x, ident, intro["x_normed"], (32, 32), intro)

            @block.scalar
            def _(act):
                transposed_scalar(act, ps, xT[0], intro)

            @block.vector
            def _(dve):
                transposed_vector(dve, ps, xT, intro)
        end_stage(nc, intro.values())

        with nc.Fori(0, DEPTH) as layer:
            with nc.Block() as block:

                @block.sync
                def _(sp_):
                    def at_layer(t):
                        return t[bass.ds(layer, 1)].rearrange("l p n -> (l p) n")

                    sp_.dma_start(wg_raw, at_layer(a["wg"])).then_inc(sem["params"], 16)
                    sp_.dma_start(pa[:, 0:128], at_layer(a["pa"])).then_inc(sem["params"], 16)
                    for dst, src in ((g_gdn, a["g_gdn"]), (g_mlstm, a["g_mlstm"])):
                        sp_.dma_start(dst, src[bass.ds(layer, 1)].rearrange("l n -> (l n)").partition_broadcast(P))\
                           .then_inc(sem["params"], 16)

                    def mix(u):
                        w.load(sp_, a["w1"][bass.ds(layer, 1), u].rearrange("l p n -> (l p) n"), u)

                    for u in range(U_BA):
                        mix(u)
                    for u in range(U_BA, U_FFN):
                        mix(u)
                    sp_.wait_ge(sem["ab_done"], 4)
                    for name, dst in (("ln1_g", ln_gain), ("ln1_b", ln_shift)):
                        sp_.dma_start(dst, a[name][bass.ds(layer, 1)].rearrange("l n -> (l n)").partition_broadcast(P))\
                           .then_inc(norm1["norm_rows"], 16)

                    def up_w(pair, f):
                        return a["up"][bass.ds(layer, 1), bass.ds(pair, 1) if not isinstance(pair, int) else slice(pair, pair + 1), f]\
                            .rearrange("l a p n -> (l a p) n")

                    def down_w(pair):
                        return a["dn"][bass.ds(layer, 1), bass.ds(pair, 1) if not isinstance(pair, int) else slice(pair, pair + 1)]\
                            .rearrange("l a p n -> (l a p) n")

                    ffn_load(sp_, w, U_FFN, up_w, down_w)
                    sp_.wait_ge(norm1["x_normed"], TT)
                    for name, dst in (("ln2_g", ln_gain), ("ln2_b", ln_shift)):
                        sp_.dma_start(dst, a[name][bass.ds(layer, 1)].rearrange("l n -> (l n)").partition_broadcast(P))\
                           .then_inc(norm2["norm_rows"], 16)

                @block.scalar
                def _(act):
                    chain = Chain(act, steps["scalar"])
                    act.wait_ge(sem["params"], 64)
                    act.activation(wg[0][:, :, :].rearrange("p a b -> p (a b)"), wg_raw, ACT.Copy).then_inc(sem["gate_w_hi"], 1)
                    act.wait_ge(sem["cv_zero"], 1)

                    def finish_conv(u):
                        act.wait_ge(sem["conv_done"], u + 1)
                        tiles = qkvT[:, 2 * u:2 * u + 2, :].rearrange("p a b -> p (a b)")
                        act.activation(tiles, ca[:, u % 2].rearrange("p a b -> p (a b)"), ACT.Silu).then_inc(sem["silu_done"], 1)
                        if u < 8:
                            act.wait_ge(sem["silu_done"], u + 1)
                            if u >= 2:
                                act.wait_ge(sem["ss_mm"], u - 1)
                            act.activation(sq[:, u % 2].rearrange("p a b -> p (a b)"), tiles, ACT.Square).then_inc(sem["sq_done"], 1)

                    for u in range(QKV_UNITS):
                        w.hi_through(act, u + 2)
                        act.wait_ge(w.used, u + 1)
                        if u >= 2:
                            act.wait_ge(sem["conv_done"], u - 1)
                        act.activation(cv[:, u % 2, :, 3:259], ps[:, u % 4, :].rearrange("p (a b) -> p a b", a=2),
                                       ACT.Copy).then_inc(sem["cv_copied"], 1)
                        if u >= 1:
                            finish_conv(u - 1)
                    w.hi_through(act, QKV_UNITS + 2)
                    finish_conv(QKV_UNITS - 1)
                    w.hi_through(act, U_QKA + 3)

                    act.wait_ge(sem["g24"], 1)
                    act.activation(t8, g24[:, :, 0:8], ACT.Tanh, scale=1.0 / CAP).then_inc(sem["tanh_done"], 1)
                    act.activation(beta, g24[:, :, 8:16], ACT.Sigmoid).then_inc(sem["tanh_done"], 1)
                    act.wait_ge(sem["z_ready"], 2)
                    chain.step(act.activation(zabs, z, ACT.Abs))
                    chain.settle()
                    chain.step(act.activation(zabs, zabs, ACT.Exp, scale=-1.0))
                    act.activation(e_alog, a_log, ACT.Exp).then_inc(sem["ln_done"], 1)
                    chain.settle()
                    act.activation(zabs, zabs, ACT.Ln, bias=one).then_inc(sem["ln_done"], 1)
                    act.wait_ge(sem["cums"], 3)
                    act.activation(eg, cs[:, :, 4:12], ACT.Exp).then_inc(sem["exps"], 1)
                    act.activation(kdf, kdf, ACT.Exp).then_inc(sem["exps"], 1)
                    act.activation(nrm, ssq, ACT.Sqrt, bias=eps_rms).then_inc(sem["norms"], 1)
                    act.wait_ge(sem["m_ready"], 1)
                    act.activation(emt, m_col, ACT.Exp, scale=-1.0).then_inc(sem["emt"], 1)

                    act.wait_ge(sem["v_mm"], 4)
                    for i in range(QKA_UNITS):
                        act.wait_ge(w.used, U_QKA + i + 1)
                        act.activation(qkvT[:, 16 + 2 * i:18 + 2 * i, :].rearrange("p a b -> p (a b)"),
                                       ps[:, i, :], ACT.Copy).then_inc(sem["qka_done"], 1)
                    for i in range(2):
                        w.hi_through(act, U_VA + 2 * i + 2)
                        act.wait_ge(w.used, U_VA + 2 * i + 2)
                        for t in range(TT):
                            act.activation(va[:, t, 2 * i:2 * i + 2, 0:A_DV],
                                           ps[:, 2 * i + t, :].rearrange("p (a b) -> p a b", a=2),
                                           ACT.Copy).then_inc(sem["va_done"], 1)
                    w.hi_through(act, U_OA + 1)

                    for c in range(2):
                        act.wait_ge(sem["diff"], 8 * (c + 1))
                        act.activation(PB[:, :, :], PB[:, :, :], ACT.Exp).then_inc(sem["dec_exp"], 1)
                        if c == 0:
                            for g in range(2):
                                act.wait_ge(sem["s_mm"], g + 1)
                                act.activation(ST8[:, 4 * g:4 * g + 4, :].rearrange("p a b -> p (a b)"),
                                               ps[:, 4 + g, :], ACT.Copy).then_inc(sem["s_done"], 1)
                    act.wait_ge(sem["hb_sq"], 2)
                    act.activation(rs8, rs8, ACT.Sqrt, bias=eps_rms, scale=1.0 / B_DK).then_inc(sem["hb_std"], 1)

                    for hd in range(A_HEADS):
                        act.wait_ge(sem["w_diff"], 2 * hd + 2)
                        act.activation(mw[:, hd % 2, :], mw[:, hd % 2, :], ACT.Exp, scale=-1.0).then_inc(sem["w_exp"], 1)
                    for hd in range(A_HEADS):
                        for t in range(TT):
                            act.wait_ge(sem["num_done"], 2 * hd + t + 1)
                            if hd + t:
                                act.wait_ge(sem["ha_sq"], 2 * hd + t)
                            act.activation(junk, va[:, t, hd, 0:A_DV], ACT.Square,
                                           accum_out=rs4[:, t, hd:hd + 1]).then_inc(sem["ha_sq"], 1)
                    act.wait_ge(sem["ha_sq"], 8)
                    act.activation(rs4, rs4, ACT.Sqrt, bias=eps_rms, scale=1.0 / A_DV).then_inc(sem["ha_std"], 1)

                    def gate_tiles(u0, func, before):
                        for i in range(4):
                            w.hi_through(act, u0 + i + 2)
                            act.wait_ge(w.used, u0 + i + 1)
                            n = before + i
                            if n >= 2:
                                act.wait_ge(sem["abF"], n - 1)
                            act.activation(og[:, n % 2, :], ps[:, i % 4, :], func).then_inc(sem["og_done"], 1)
                            act.wait_ge(sem["abF"], n + 1)
                            if n == 4:
                                act.wait_ge(w.used, U_ZB)
                            act.activation(abT[0][:, 2 * i:2 * i + 2, :].rearrange("p a b -> p (a b)"), abF[:, n % 2, :],
                                           ACT.Copy).then_inc(sem["ab_hi"], 1)

                    def branch_gates(u0, before):
                        for i in range(KT):
                            w.hi_through(act, u0 + i + 2)
                            act.wait_ge(w.used, u0 + i + 1)
                            n = before + i
                            if n >= 2:
                                act.wait_ge(sem["yp_done"], n - 1)
                            act.activation(sg[:, n % 2, :], ps[:, i % 4, 0:S], ACT.Sigmoid).then_inc(sem["sg_done"], 1)

                    gate_tiles(U_OA, ACT.Sigmoid, 0)
                    branch_gates(U_BA, 0)
                    gate_tiles(U_ZB, ACT.Silu, 4)
                    branch_gates(U_BB, KT)
                    for j in range(4):
                        act.wait_ge(sem["yp_done"], KT + 2 * j + 2)
                        act.wait_ge(w.used, U_OUT)
                        act.activation(abT[0][:, 2 * j:2 * j + 2, :], yF[:, 2 * j:2 * j + 2, :], ACT.Copy)\
                           .then_inc(sem["yT_hi"], 1)
                    w.hi_through(act, U_FFN + 0)
                    layer_norm_scalar(act, stats, eps_ln, norm1)
                    transposed_scalar(act, ps, xT[0], norm1)
                    ffn_scalar(act, w, U_FFN, up_ps, gate, h, hT[0], norm2, 0)
                    layer_norm_scalar(act, stats, eps_ln, norm2)
                    transposed_scalar(act, ps, xT[0], norm2)

                @block.gpsimd
                def _(pool):
                    pool.memset(eps_ln, LN_EPS).then_inc(sem["masks"], 1)
                    pool.memset(eps_rms, RMS_EPS).then_inc(sem["masks"], 1)
                    pool.memset(one, 1.0).then_inc(sem["masks"], 1)
                    pool.memset(va[:, :, :, A_DV:A_DV + 1], 1.0).then_inc(sem["masks"], 1)
                    pool.memset(zero[:, :].bitcast(F32), 0.0).then_inc(sem["masks"], 1)
                    pool.wait_ge(sem["masks"], 5)
                    pool.memset(cv[:, :, :, 0:3], 0.0).then_inc(sem["cv_zero"], 1)
                    pool.wait_ge(sem["cv_zero"], 1)

                @block.vector
                def _(dve):
                    chain = Chain(dve, steps["vector"])

                    def heads(v, g):
                        return v[:, 4 * g:4 * g + 4].unsqueeze(2).broadcast_to([P, 4, P])

                    def over_heads(m, n=4):
                        return m.unsqueeze(1).broadcast_to([P, n, P])

                    def bank(b):
                        return ps[:, b, :].rearrange("p (h t) -> p h t", t=P)

                    dve.wait_ge(sem["gate_w_hi"], 1)
                    dve.tensor_tensor(wg[1][:, :, :].rearrange("p a b -> p (a b)"), wg_raw,
                                      wg[0][:, :, :].rearrange("p a b -> p (a b)").bitcast(F32),
                                      ALU.subtract).then_inc(sem["gate_w"], 1)

                    for u in range(QKV_UNITS):
                        w.lo_through(dve, u + 2)
                        dve.wait_ge(sem["cv_copied"], u + 1)
                        if u >= 2:
                            dve.wait_ge(sem["silu_done"], u - 1)
                        for j in range(4):
                            for k in range(2):
                                tap = conv_w[:, 2 * u + k, j:j + 1]
                                src, dst = cv[:, u % 2, k, j:j + S], ca[:, u % 2, k, :]
                                if j == 0:
                                    ins = dve.tensor_scalar(dst, src, tap, None, ALU.mult)
                                else:
                                    ins = dve.scalar_tensor_tensor(dst, src, tap, dst, ALU.mult, ALU.add)
                                if j == 3 and k == 1:
                                    ins.then_inc(sem["conv_done"], 1)
                                else:
                                    chain.step(ins)
                            if j < 3:
                                chain.settle()
                    w.lo_through(dve, QKV_UNITS + 3)

                    dve.wait_ge(sem["gates_mm"], 1)
                    dve.tensor_tensor(g24, gates_ps, gate_bias.unsqueeze(1).broadcast_to([P, TT, N_GATES]), ALU.add)\
                       .then_inc(sem["g24"], 1)
                    dve.wait_ge(sem["g24"], 1)
                    dve.tensor_copy(z[:, :, 4:12], g24[:, :, 16:24]).then_inc(sem["z_ready"], 1)
                    dve.wait_ge(sem["tanh_done"], 2)
                    chain.step(dve.tensor_scalar(li, t8[:, :, 0:4], CAP, None, ALU.mult))
                    dve.tensor_scalar(z[:, :, 0:4], t8[:, :, 4:8], -CAP, None, ALU.mult).then_inc(sem["z_ready"], 1)
                    dve.wait_ge(sem["ln_done"], 2)
                    dve.wait_ge(sem["z_ready"], 2)
                    chain.step(dve.scalar_tensor_tensor(sp, z, 0.0, zabs, ALU.max, ALU.add))
                    chain.settle()
                    dve.tensor_scalar(gs[:, :, 0:4], sp[:, :, 0:4], -1.0, None, ALU.mult).then_inc(sem["decays"], 1)
                    dve.scalar_tensor_tensor(gs[:, :, 4:12], sp[:, :, 4:12], -1.0,
                                             e_alog.unsqueeze(1).broadcast_to([P, TT, B_HEADS]), ALU.mult,
                                             ALU.mult).then_inc(sem["decays"], 1)
                    dve.wait_ge(sem["cum_mm"], 1)
                    chain.step(dve.tensor_copy(cs, cum_ps[:, 0]))
                    chain.step(dve.tensor_copy(tot, cum_ps[:, 1]))
                    dve.wait_ge(sem["ss_mm"], 8)
                    dve.tensor_copy(ssq, ss_ps).then_inc(sem["cums"], 1)
                    chain.settle()
                    dve.tensor_tensor(cs[:, 1, 0:4], cs[:, 1, 0:4], tot[:, 0, 0:4], ALU.add).then_inc(sem["cums"], 1)
                    dve.tensor_tensor(kdf, tot[:, :, 4:12], cs[:, :, 4:12], ALU.subtract).then_inc(sem["cums"], 1)
                    dve.wait_ge(sem["cums"], 3)
                    dve.tensor_tensor(a_col, li, cs[:, :, 0:4], ALU.subtract).then_inc(sem["a_ready"], 1)
                    dve.wait_ge(sem["exps"], 2)
                    dve.wait_ge(sem["norms"], 1)
                    chain.step(dve.reciprocal(rnrm, nrm))
                    chain.step(dve.tensor_scalar(neg_eg, eg, -1.0, None, ALU.mult))
                    chain.settle()
                    rk = rnrm[:, :, 8:16]
                    chain.step(dve.tensor_tensor(kdf, kdf, rk, ALU.mult))
                    chain.step(dve.tensor_tensor(brk, beta, rk, ALU.mult))
                    chain.step(dve.tensor_scalar(rq, rnrm[:, :, 0:8], B_DK ** -0.5, None, ALU.mult))
                    chain.settle()
                    chain.step(dve.tensor_tensor(cj, brk, rk, ALU.mult))
                    dve.wait_ge(sem["a_rows_mm"], 1)
                    chain.step(dve.tensor_copy(rows[:, 0, :], arow_ps))
                    chain.settle()
                    dve.tensor_tensor_scan(rows[:, 1, :], rows[:, 0, :], rows[:, 0, :], 0.0, ALU.max, ALU.max)\
                       .then_inc(sem["m_rows"], 1)
                    dve.wait_ge(sem["m_cols_mm"], 1)
                    dve.tensor_tensor(m_col, mcol_ps, cs[:, :, 0:4], ALU.add).then_inc(sem["m_ready"], 1)

                    for t in range(TT):
                        for g in range(2):
                            dve.wait_ge(sem["v_mm"], 2 * t + g + 1)
                            dve.tensor_tensor(hb[:, t, 4 * g:4 * g + 4, :], bank(4 + 2 * t + g), heads(nrm[:, t, 8:16], g),
                                              ALU.mult).then_inc(sem["v_done"], 1)
                    w.lo_through(dve, U_VA + 2)
                    for t in range(TT):
                        for g in range(2):
                            dve.wait_ge(sem["k_mm"], 2 * t + g + 1)
                            dve.tensor_tensor(k_tm[:, t, 4 * g:4 * g + 4, :], bank(4 + 2 * t + g), heads(kdf[:, t, :], g),
                                              ALU.mult).then_inc(sem["k_done"], 1)
                    w.lo_through(dve, U_OA + 1)

                    for c in range(2):
                        for g in range(2):
                            dve.wait_ge(sem["gb_mm"], 2 * c + g + 1)
                            for i in range(4):
                                hd = 4 * g + i
                                dve.tensor_scalar(PB[:, hd, :], bank(4 + g)[:, i, :], cs[:, c, 4 + hd:5 + hd], 0.0,
                                                  ALU.subtract, ALU.min).then_inc(sem["diff"], 1)
                        dve.wait_ge(sem["dec_exp"], c + 1)
                        chain.step(dve.tensor_tensor(PB[:, :, :], PB[:, :, :], over_heads(tri, 8), ALU.mult))
                        chain.settle()
                        for g in range(2):
                            dve.wait_ge(sem["kkqk_mm"], 2 * c + g + 1)
                            for i in range(4):
                                hd = 4 * g + i
                                chain.step(dve.scalar_tensor_tensor(AT[:, hd, :], bank(g)[:, i, :], cj[:, c, hd:hd + 1],
                                                                    PB[:, hd, :], ALU.mult, ALU.mult))
                                chain.step(dve.scalar_tensor_tensor(attn[:, hd, :], bank(2 + g)[:, i, :],
                                                                    rk[:, c, hd:hd + 1], PB[:, hd, :], ALU.mult, ALU.mult))
                        chain.settle()
                        dve.tensor_tensor(AT[:, :, :], AT[:, :, :], over_heads(strict, 8), ALU.mult).then_inc(sem["a_done"], 1)
                        dve.wait_ge(sem["a_done"], c + 1)
                        chain.step(dve.tensor_tensor(XT[:, :, :], AT[:, :, :], over_heads(level0, 8), ALU.mult))
                        chain.settle()
                        dve.tensor_tensor(XT[:, :, :], over_heads(ident, 8), XT[:, :, :], ALU.subtract).then_inc(sem["xt_init"], 1)
                        for g in range(2):
                            dve.wait_ge(sem["x_mm"], 2 * c + g + 1)
                            dve.tensor_copy(X[:, 4 * g:4 * g + 4, :], bank(g)).then_inc(sem["x_init"], 1)
                        dve.wait_ge(sem["x_init"], 2 * c + 2)
                        for lv in range(6):
                            n = 2 * (6 * c + lv)
                            for g in range(2):
                                dve.wait_ge(sem["p_mm"], n + g + 1)
                                dve.tensor_tensor(PB[:, 4 * g:4 * g + 4, :], bank(g), over_heads(levels[lv]), ALU.mult)\
                                   .then_inc(sem["p_done"], 1)
                            for g in range(2):
                                hs = slice(4 * g, 4 * g + 4)
                                dve.wait_ge(sem["y_mm"], n + g + 1)
                                if lv < 5:
                                    dve.tensor_tensor(X[:, hs, :], X[:, hs, :], bank(2 + 2 * g), ALU.subtract)\
                                       .then_inc(sem["y_done"], 1)
                                dve.tensor_tensor(XT[:, hs, :], XT[:, hs, :], bank(3 + 2 * g), ALU.subtract)\
                                   .then_inc(sem["y_done"], 1)
                            dve.wait_ge(sem["y_done"], 22 * c + 4 * lv + (4 if lv < 5 else 2))
                        for g in range(2):
                            hs = slice(4 * g, 4 * g + 4)
                            if c == 1:
                                dve.wait_ge(sem["ks_mm"], g + 1)
                                chain.step(dve.tensor_tensor(PB[:, hs, :], bank(g), heads(neg_eg[:, 1, :], g), ALU.mult))
                                chain.step(dve.tensor_tensor(AT[:, hs, :], bank(6 + g), heads(eg[:, 1, :], g), ALU.mult))
                                chain.settle()
                                dve.tensor_tensor(PB[:, hs, :], PB[:, hs, :], hb[:, 1, hs, :], ALU.add).then_inc(sem["rhs_done"], 1)
                            dve.wait_ge(sem["vn_mm"], 2 * c + g + 1)
                            dve.tensor_tensor(X[:, hs, :], bank(2 + g), heads(brk[:, c, :], g), ALU.mult).then_inc(sem["vn_done"], 1)
                        for g in range(2):
                            hs = slice(4 * g, 4 * g + 4)
                            dve.wait_ge(sem["o_mm"], 2 * c + g + 1)
                            if c == 1:
                                chain.step(dve.tensor_tensor(AT[:, hs, :], AT[:, hs, :], bank(2 + g), ALU.add))
                                chain.settle()
                                dve.tensor_tensor(hb[:, c, hs, :], AT[:, hs, :], heads(rq[:, c, :], g), ALU.mult)\
                                   .then_inc(sem["o_done"], 1)
                            else:
                                dve.tensor_tensor(hb[:, c, hs, :], bank(2 + g), heads(rq[:, c, :], g), ALU.mult)\
                                   .then_inc(sem["o_done"], 1)
                    dve.wait_ge(sem["o_done"], 4)
                    for t in range(TT):
                        chain.step(dve.tensor_tensor(AT[:, :, :] if t else X[:, :, :], hb[:, t], hb[:, t], ALU.mult))
                    chain.settle()
                    for t in range(TT):
                        dve.tensor_reduce(rs8[:, t, :], AT[:, :, :] if t else X[:, :, :], AX.X, ALU.add).then_inc(sem["hb_sq"], 1)
                    dve.wait_ge(sem["hb_std"], 1)
                    chain.step(dve.reciprocal(rs8, rs8))
                    chain.settle()
                    for t in range(TT):
                        chain.step(dve.tensor_tensor(hb[:, t], hb[:, t], rs8[:, t, :].unsqueeze(2).broadcast_to([P, 8, P]), ALU.mult))
                    chain.settle()
                    for t in range(TT):
                        chain.step(dve.tensor_tensor(hb[:, t], hb[:, t], over_heads(g_gdn, 8), ALU.mult))
                    chain.settle()

                    def head_weights(hd):
                        dve.wait_ge(sem["kq_mm"], hd + 1)
                        if hd >= 2:
                            dve.wait_ge(sem["num_mm"], 2 * hd - 2)
                        dve.tensor_scalar(mw[:, hd % 2, 0:S], ps[:, 5, 0:S], a_col[:, 0, hd:hd + 1], 0.0,
                                          ALU.subtract, ALU.max).then_inc(sem["w_diff"], 1)
                        dve.tensor_scalar(mw[:, hd % 2, S:384], ps[:, 5, P:S], a_col[:, 1, hd:hd + 1], 0.0,
                                          ALU.subtract, ALU.max).then_inc(sem["w_diff"], 1)
                        dve.wait_ge(sem["w_exp"], hd + 1)
                        chain.step(dve.scalar_tensor_tensor(mst[:, hd % 2, :], ps[:, 4, 0:384], A_DK ** -0.5,
                                                            mw[:, hd % 2, :], ALU.mult, ALU.mult))
                        chain.settle()
                        for b in range(2):
                            blk = mst[:, hd % 2, 2 * b * P:(2 * b + 1) * P]
                            dve.tensor_tensor(blk, blk, tri, ALU.mult).then_inc(sem["s_done2"], 1)

                    def head_sums(hd):
                        dve.wait_ge(sem["num_mm"], 2 * hd + 2)
                        for t in range(TT):
                            chain.step(dve.tensor_copy(den[:, t, hd:hd + 1], ps[:, 6 + t, A_DV:A_DV + 1]))
                        chain.settle()
                        for t in range(TT):
                            chain.step(dve.scalar_tensor_tensor(rs4[:, t, hd:hd + 1], den[:, t, hd:hd + 1], -1.0,
                                                                den[:, t, hd:hd + 1], ALU.mult, ALU.max))
                        chain.settle()
                        for t in range(TT):
                            chain.step(dve.tensor_tensor(rs4[:, t, hd:hd + 1], rs4[:, t, hd:hd + 1], emt[:, t, hd:hd + 1],
                                                         ALU.max))
                        chain.settle()
                        for t in range(TT):
                            chain.step(dve.reciprocal(den[:, t, hd:hd + 1], rs4[:, t, hd:hd + 1]))
                        chain.settle()
                        for t in range(TT):
                            dve.tensor_scalar(va[:, t, hd, 0:A_DV], ps[:, 6 + t, 0:A_DV], den[:, t, hd:hd + 1], None,
                                              ALU.mult).then_inc(sem["num_done"], 1)

                    dve.wait_ge(sem["emt"], 1)
                    for hd in range(A_HEADS):
                        head_weights(hd)
                        head_sums(hd)
                    dve.wait_ge(sem["ha_std"], 1)
                    chain.step(dve.reciprocal(rs4, rs4))
                    chain.settle()
                    for t in range(TT):
                        for hd in range(A_HEADS):
                            v = va[:, t, hd, 0:A_DV]
                            dve.scalar_tensor_tensor(v, v, rs4[:, t, hd:hd + 1], g_mlstm[:, hd * A_DV:(hd + 1) * A_DV],
                                                     ALU.mult, ALU.mult).then_inc(sem["ha_done"], 1)
                    dve.wait_ge(sem["ha_done"], 8)

                    def gated_tiles(u0, before):
                        for i in range(4):
                            w.lo_through(dve, u0 + i + 2)
                            n = before + i
                            dve.wait_ge(sem["og_done"], n + 1)
                            dve.wait_ge(sem["hT_mm"], n + 1)
                            if n >= 2:
                                dve.wait_ge(sem["ab_hi"], n - 1)
                            dve.tensor_tensor(abF[:, n % 2, :], ps[:, 4 + i % 4, :], og[:, n % 2, :], ALU.mult)\
                               .then_inc(sem["abF"], 1)
                            dve.wait_ge(sem["ab_hi"], n + 1)
                            part = [v[:, 2 * i:2 * i + 2, :].rearrange("p a b -> p (a b)") for v in abT]
                            dve.tensor_tensor(part[1], abF[:, n % 2, :], part[0].bitcast(F32), ALU.subtract)\
                               .then_inc(sem["ab_done"], 1)

                    def branch(u0, before):
                        for i in range(KT):
                            w.lo_through(dve, u0 + i + 2)
                            n = before + i
                            dve.wait_ge(sem["sg_done"], n + 1)
                            if before == 0:
                                dve.tensor_tensor(yF[:, i, :], sg[:, n % 2, :], ps[:, i % 4, S:2 * S], ALU.mult)\
                                   .then_inc(sem["yp_done"], 1)
                            else:
                                chain.step(dve.tensor_tensor(sg[:, n % 2, :], sg[:, n % 2, :], ps[:, i % 4, S:2 * S], ALU.mult))
                                chain.settle()
                                dve.tensor_tensor(yF[:, i, :], yF[:, i, :], sg[:, n % 2, :], ALU.add).then_inc(sem["yp_done"], 1)

                    gated_tiles(U_OA, 0)
                    branch(U_BA, 0)
                    gated_tiles(U_ZB, 4)
                    branch(U_BB, KT)
                    for j in range(4):
                        dve.wait_ge(sem["yT_hi"], j + 1)
                        part = slice(2 * j, 2 * j + 2)
                        dve.tensor_tensor(abT[1][:, part, :], yF[:, part, :], abT[0][:, part, :].bitcast(F32), ALU.subtract)\
                           .then_inc(sem["yT_done"], 1)
                    w.lo_through(dve, U_FFN)
                    dve.wait_ge(w.used, U_FFN)
                    layer_norm_vector(dve, chain, x, acc, ln_gain, ln_shift, stats, norm1)
                    transposed_vector(dve, ps, xT, norm1)
                    ffn_vector(dve, w, U_FFN, up_ps, gate, h, hT, norm2, 0)
                    dve.wait_ge(w.used, U_FFN + FFN_UNITS)
                    layer_norm_vector(dve, chain, x, acc, ln_gain, ln_shift, stats, norm2)
                    transposed_vector(dve, ps, xT, norm2)

                @block.tensor
                def _(pe):
                    def tiles(u, bank, rhs):
                        pe.wait_ge(w.lo_done, u + 1)
                        for j in range(2):
                            for k in range(KT):
                                mm = split_matmul(pe, ps[:, bank, j * S:(j + 1) * S], w.pair(u, (16, P), j * KT + k, slice(None)),
                                                  (rhs[j][0][:, k, :], rhs[j][1][:, k, :]), k == 0, k == KT - 1)
                        mm.then_inc(w.used, 1)

                    def group(u, banks, lhs):
                        for half in range(2):
                            pe.wait_ge(w.lo_done, u + half + 1)
                            for t in range(TT):
                                for k in range(4):
                                    kk = 4 * half + k
                                    mm = split_matmul(pe, ps[:, banks[t], :],
                                                      (lhs[0][:, kk, t * P:(t + 1) * P], lhs[1][:, kk, t * P:(t + 1) * P]),
                                                      w.pair(u + half, (4, 512), k, slice(None)), kk == 0, kk == KT - 1)
                            mm.then_inc(w.used, 1)

                    pe.wait_ge(sem["gate_w"], 1)
                    for t in range(TT):
                        for k in range(KT):
                            mm = split_matmul(pe, gates_ps[:, t, :], (xT[0][:, k, t * P:(t + 1) * P], xT[1][:, k, t * P:(t + 1) * P]),
                                              (wg[0][:, k, :], wg[1][:, k, :]), k == 0, k == KT - 1)
                    mm.then_inc(sem["gates_mm"], 1)

                    def sum_squares(u):
                        pe.wait_ge(sem["sq_done"], u + 1)
                        for k in range(2):
                            for t in range(TT):
                                mm = pe.matmul(ss_ps[:, t, 2 * u + k:2 * u + k + 1], sq[:, u % 2, k, t * P:(t + 1) * P],
                                               ones[:, 0:1], start=True, stop=True)
                        mm.then_inc(sem["ss_mm"], 1)

                    for u in range(QKV_UNITS):
                        if u >= 4:
                            pe.wait_ge(sem["cv_copied"], u - 3)
                        tiles(u, u % 4, (xT, xT))
                        if 2 <= u < 10:
                            sum_squares(u - 2)
                    for i in range(QKA_UNITS):
                        pe.wait_ge(sem["cv_copied"], QKV_UNITS - 3 + i)
                        tiles(U_QKA + i, i, (xT, xT))
                    pe.wait_ge(sem["decays"], 2)
                    for t in range(TT):
                        pe.matmul(cum_ps[:, 0, t, :], tri, gs[:, t, :], start=True, stop=True)
                        mm = pe.matmul(cum_ps[:, 1, t, :], ones, gs[:, t, :], start=True, stop=True)
                    mm.then_inc(sem["cum_mm"], 1)
                    pe.wait_ge(sem["a_ready"], 1)
                    for t in range(TT):
                        mm = pe.transpose(arow_ps[:, t * P:(t + 1) * P], a_col[:, t, :], ident)
                    mm.then_inc(sem["a_rows_mm"], 1)
                    pe.wait_ge(sem["m_rows"], 1)
                    for t in range(TT):
                        mm = pe.transpose(mcol_ps[:, t, :], rows[:, 1, t * P:(t + 1) * P], ident[0:A_HEADS, 0:A_HEADS])
                    mm.then_inc(sem["m_cols_mm"], 1)
                    pe.wait_ge(sem["silu_done"], QKV_UNITS)
                    pe.wait_ge(sem["m_ready"], 1)
                    for first, mm_sem in ((16, "v_mm"), (8, "k_mm")):
                        for t in range(TT):
                            for g in range(2):
                                if first == 8:
                                    pe.wait_ge(sem["v_done"], 2 * t + g + 1)
                                for i in range(4):
                                    mm = pe.transpose(ps[:, 4 + 2 * t + g, i * P:(i + 1) * P],
                                                      qkvT[:, first + 4 * g + i, t * P:(t + 1) * P], ident)
                                mm.then_inc(sem[mm_sem], 1)
                    for i in range(2):
                        pe.wait_ge(sem["qka_done"], 2 * i + 2)
                        group(U_VA + 2 * i, (2 * i, 2 * i + 1), xT)

                    def by_heads(b, g, lhs, rhs, inc=None):
                        for i in range(4):
                            mm = pe.matmul(ps[:, b, i * P:(i + 1) * P], lhs(4 * g + i), rhs(4 * g + i), start=True, stop=True)
                        if inc:
                            mm.then_inc(sem[inc], 1)

                    pe.wait_ge(sem["va_done"], 4)
                    pe.wait_ge(sem["k_done"], 4)
                    for c in range(2):
                        tok = slice(c * P, (c + 1) * P)
                        if c == 1:
                            pe.wait_ge(sem["s_done"], 2)
                            pe.wait_ge(sem["o_done"], 2)
                        for g in range(2):
                            by_heads(4 + g, g, lambda hd: gs[:, c, 4 + hd:5 + hd].broadcast_to([P, P]), lambda hd: tri, "gb_mm")
                        for g in range(2):
                            by_heads(g, g, lambda hd: qkvT[:, 8 + hd, tok], lambda hd: qkvT[:, 8 + hd, tok])
                            by_heads(2 + g, g, lambda hd: qkvT[:, 8 + hd, tok], lambda hd: qkvT[:, hd, tok], "kkqk_mm")
                        pe.wait_ge(sem["xt_init"], c + 1)
                        for g in range(2):
                            for i in range(4):
                                mm = pe.transpose(ps[:, g, i * P:(i + 1) * P], XT[:, 4 * g + i, :], ident)
                            mm.then_inc(sem["x_mm"], 1)
                        for lv in range(6):
                            for g in range(2):
                                if lv == 0:
                                    pe.wait_ge(sem["x_init"], 2 * c + g + 1)
                                else:
                                    pe.wait_ge(sem["y_done"], 22 * c + 4 * (lv - 1) + 2 * g + 2)
                                by_heads(g, g, lambda hd: AT[:, hd, :], lambda hd: X[:, hd, :], "p_mm")
                            for g in range(2):
                                pe.wait_ge(sem["p_done"], 2 * (6 * c + lv) + g + 1)
                                if lv < 5:
                                    by_heads(2 + 2 * g, g, lambda hd: XT[:, hd, :], lambda hd: PB[:, hd, :])
                                by_heads(3 + 2 * g, g, lambda hd: PB[:, hd, :], lambda hd: XT[:, hd, :], "y_mm")
                        pe.wait_ge(sem["y_done"], 22 * (c + 1))
                        for g in range(2):
                            if c == 1:
                                by_heads(g, g, lambda hd: qkvT[:, 8 + hd, tok], lambda hd: ST8[:, hd, :])
                                by_heads(6 + g, g, lambda hd: qkvT[:, hd, tok], lambda hd: ST8[:, hd, :], "ks_mm")
                                pe.wait_ge(sem["rhs_done"], g + 1)
                            by_heads(2 + g, g, lambda hd: XT[:, hd, :],
                                     (lambda hd: PB[:, hd, :]) if c else (lambda hd: hb[:, 0, hd, :]), "vn_mm")
                        for g in range(2):
                            pe.wait_ge(sem["vn_done"], 2 * c + g + 1)
                            by_heads(2 + g, g, lambda hd: attn[:, hd, :], lambda hd: X[:, hd, :], "o_mm")
                            if c == 0:
                                by_heads(4 + g, g, lambda hd: k_tm[:, 0, hd, :], lambda hd: X[:, hd, :], "s_mm")

                    for hd in range(A_HEADS):
                        q, k = qkvT[:, 16 + hd, :], qkvT[:, 20 + hd, :]
                        if hd:
                            pe.wait_ge(sem["s_done2"], 2 * hd)
                            pe.wait_ge(sem["num_done"], 2 * hd)
                        pe.matmul(ps[:, 4, 0:S], k[:, 0:P], q, start=True, stop=True)
                        pe.matmul(ps[:, 4, S:384], k[:, P:S], q[:, P:S], start=True, stop=True)
                        pe.matmul(ps[:, 5, 0:S], sel[:, hd, :], rows[:, 1, :], start=True, stop=True).then_inc(sem["kq_mm"], 1)
                        pe.wait_ge(sem["s_done2"], 2 * hd + 2)
                        if hd == 0:
                            pe.wait_ge(sem["o_done"], 4)
                        m = mst[:, hd % 2, :]
                        pe.matmul(ps[:, 6, 0:A_DV + 1], m[:, 0:P], va[:, 0, hd, :], start=True, stop=True).then_inc(sem["num_mm"], 1)
                        pe.matmul(ps[:, 7, 0:A_DV + 1], m[:, P:S], va[:, 0, hd, :], start=True, stop=False)
                        pe.matmul(ps[:, 7, 0:A_DV + 1], m[:, S:384], va[:, 1, hd, :], start=False, stop=True).then_inc(sem["num_mm"], 1)

                    def head_tiles(i, n, src):
                        for k in range(2):
                            for t in range(TT):
                                mm = pe.transpose(ps[:, 4 + i, k * S + t * P:k * S + (t + 1) * P], src(t, 2 * i + k), ident)
                        mm.then_inc(sem["hT_mm"], 1)

                    pe.wait_ge(sem["ha_done"], 8)
                    for i in range(4):
                        tiles(U_OA + i, i, (xT, xT))
                        head_tiles(i, i, lambda t, k: va[:, t, k // 2, (k % 2) * P:(k % 2 + 1) * P])
                    for i in range(KT):
                        if i < 4:
                            pe.wait_ge(sem["og_done"], i + 1)
                            pe.wait_ge(sem["ab_done"], 4)
                        else:
                            pe.wait_ge(sem["yp_done"], i - 3)
                        tiles(U_BA + i, i % 4, (xT, abT))
                    for i in range(4):
                        pe.wait_ge(sem["yp_done"], 4 + i + 1)
                        tiles(U_ZB + i, i, (xT, xT))
                        head_tiles(i, 4 + i, lambda t, k: hb[:, t, k, :])
                    for i in range(KT):
                        if i < 4:
                            pe.wait_ge(sem["og_done"], 4 + i + 1)
                            pe.wait_ge(sem["ab_done"], 8)
                        else:
                            pe.wait_ge(sem["yp_done"], KT + i - 3)
                        tiles(U_BB + i, i % 4, (xT, abT))
                    pe.wait_ge(sem["yp_done"], 2 * KT)
                    pe.wait_ge(sem["yT_done"], 4)
                    for half in range(2):
                        group(U_OUT + 2 * half, (half, 2 + half), abT)
                    norm_transposes(pe, ps, x, ident, norm1["x_normed"], (1, 2), norm1)
                    ffn_tensor(pe, w, U_FFN, xT, hT, acc, up_ps, zero, norm2, norm1["xT_ready"], False)
                    norm_transposes(pe, ps, x, ident, norm2["x_normed"], (1, 2), norm2)

            end_stage(nc, [*w.sems(), *sem.values(), *norm1.values(), *norm2.values(), *steps.values()])


HD = 64
FOX_HEADS, SB_HEADS = 8, 16
D_RNN = 512
RG_C = 8.0
RNN_UNITS, FOX_QKV_UNITS, HY_OUT_UNITS = 4, 6, 4
SB_QK_UNITS, SB_V_UNITS, SB_OUT_UNITS = 8, 4, 4
RMS_SEMS = ["sq_done", "sq1_done", "std_done", "x_normed", "xT_mm", "xT_hi_done", "xT_ready", "gain_cols", "acc_done"]


def rms_scalar(act, x, junk, ss, std, eps, ps, gain, xT_hi, sem):
    act.preload_act_table_set("sqrt_and_others")
    act.activation(junk, x[:, 0, :], ACT.Square, accum_out=ss[:, 0:1]).then_inc(sem["sq_done"], 1)
    act.wait_ge(sem["sq_done"], 1)
    act.activation(std[:, 0:1], ss[:, 0:1], ACT.Sqrt, bias=eps, scale=1.0 / D).then_inc(sem["std_done"], 1)
    act.wait_ge(sem["sq1_done"], 1)
    act.activation(std[:, 1:2], ss[:, 1:2], ACT.Sqrt, bias=eps, scale=1.0 / D).then_inc(sem["std_done"], 1)
    act.wait_ge(sem["gain_cols"], 16)
    for k in range(KT):
        act.wait_ge(sem["xT_mm"], k // 2 + 1)
        act.activation(xT_hi[:, k, :], ps[:, 4 + k // 2, (k % 2) * S:(k % 2 + 1) * S], ACT.Copy,
                       scale=gain[:, k:k + 1]).then_inc(sem["xT_hi_done"], 1)


def rms_vector(dve, chain, x, xn, ss, std, ps, gain, xT, sem):
    dve.tensor_tensor_reduce(xn[:, 1, :], x[:, 1, :], x[:, 1, :], 1.0, 0.0, ALU.mult, ALU.add, ss[:, 1:2])\
       .then_inc(sem["sq1_done"], 1)
    for t in range(TT):
        dve.wait_ge(sem["std_done"], t + 1)
        chain.step(dve.reciprocal(std[:, t:t + 1], std[:, t:t + 1]))
        chain.settle()
        if t:
            dve.wait_ge(sem["sq1_done"], 1)
        dve.tensor_scalar(xn[:, t, :], x[:, t, :], std[:, t:t + 1], None, ALU.mult).then_inc(sem["x_normed"], 1)
    for k in range(KT):
        dve.wait_ge(sem["xT_hi_done"], 2 * (k // 2) + 2)
        dve.scalar_tensor_tensor(xT[1][:, k, :], ps[:, 4 + k // 2, (k % 2) * S:(k % 2 + 1) * S], gain[:, k:k + 1],
                                 xT[0][:, k, :].bitcast(F32), ALU.mult, ALU.subtract).then_inc(sem["xT_ready"], 1)


def add_to_x(dve, w, units, x, acc, factor, sem, by_tile=False):
    for t in range(TT):
        if by_tile and t == 0:
            dve.wait_ge(sem["acc_done"], 1)
        else:
            dve.wait_ge(w.used, units)
        for half in range(2):
            cols = slice(half * 512, (half + 1) * 512)
            dve.scalar_tensor_tensor(x[:, t, cols], acc[:, 2 * t + half, :], factor, x[:, t, cols],
                                     ALU.mult, ALU.add).then_inc(sem["x_added"], 1)


class Parts:
    pass


def split_tiles(pe, w, ps, u, bank, rhs):
    pe.wait_ge(w.lo_done, u + 1)
    for j in range(2):
        for k in range(KT):
            mm = split_matmul(pe, ps[:, bank, j * S:(j + 1) * S], w.pair(u, (16, P), j * KT + k, slice(None)),
                              (rhs[0][:, k, :], rhs[1][:, k, :]), k == 0, k == KT - 1)
    mm.then_inc(w.used, 1)


def split_group(pe, w, ps, u, banks, lhs):
    for half in range(2):
        pe.wait_ge(w.lo_done, u + half + 1)
        for t in range(TT):
            for k in range(4):
                kk = 4 * half + k
                mm = split_matmul(pe, ps[:, banks[t], :],
                                  (lhs[0][:, kk, t * P:(t + 1) * P], lhs[1][:, kk, t * P:(t + 1) * P]),
                                  w.pair(u + half, (4, 512), k, slice(None)), kk == 0, kk == KT - 1)
        mm.then_inc(w.used, 1)


def end_stage(nc, sems):
    numbers = sorted(s.num for s in sems)
    first = numbers[0]
    for n, after in zip(numbers, [*numbers[1:], None]):
        if after != n + 1:
            nc.sync.sem_clear(range(first, n + 1))
            first = after
    nc.all_engine_barrier()


def ffn_stage(nc, p, a, n, name, u0, last=False):
    with ExitStack() as ctx:
        w = p.w
        ahead = 0 if last else 1
        sem = {s: ctx.enter_context(nc.semaphore(f"{name}_{s}")) for s in
               dict.fromkeys(RMS_SEMS + FFN_SEMS + ["x_added", "scalar_steps", "vector_steps"])}
        with nc.Block() as block:
            @block.sync
            def _(sp):
                sp.dma_start(p.gain[:, :], a["ffn_norm_2"][n]).then_inc(sem["gain_cols"], 16)
                ffn_load(sp, w, u0,
                         lambda pair, f: a["up"][DEPTH + n, bass.ds(pair, 1) if not isinstance(pair, int) else slice(pair, pair + 1), f]
                         .rearrange("a p n -> (a p) n"),
                         lambda pair: a["dn"][DEPTH + n, bass.ds(pair, 1) if not isinstance(pair, int) else slice(pair, pair + 1)]
                         .rearrange("a p n -> (a p) n"), first=3 if u0 else 0)
                if not last:
                    p.load_first(sp, u0 + FFN_UNITS)

            @block.scalar
            def _(act):
                rms_scalar(act, p.x, p.junk, p.ss, p.std, p.eps, p.ps, p.gain, p.xT[0], sem)
                act.preload_act_table_set("silu_and_others")
                ffn_scalar(act, w, u0, p.up_ps, p.gate, p.h, p.hT[0], sem, ahead)

            @block.vector
            def _(dve):
                rms_vector(dve, Chain(dve, sem["vector_steps"]), p.x, p.xn, p.ss, p.std, p.ps, p.gain, p.xT, sem)
                ffn_vector(dve, w, u0, p.up_ps, p.gate, p.h, p.hT, sem, ahead)
                add_to_x(dve, w, u0 + FFN_UNITS, p.x, p.acc, 0.5, sem, by_tile=True)

            @block.tensor
            def _(pe):
                norm_transposes(pe, p.ps, p.xn, p.ident, sem["x_normed"], (1, 2), sem)
                ffn_tensor(pe, w, u0, p.xT, p.hT, p.acc, p.up_ps, p.zero, sem, sem["xT_ready"], True)
        end_stage(nc, sem.values())


def heads_out(pe, p, hd, bank, v, weights, first_wait=None):
    rows = slice(HD * (hd % 2), HD * (hd % 2) + HD)
    cols = slice(HD * hd, HD * (hd + 1))
    pe.matmul(p.ps[rows, bank, 0:S], v[:, 0, cols], weights[:, 0:S], start=True, stop=False, skip_group_check=True)
    return pe.matmul(p.ps[rows, bank, P:S], v[:, 1, cols], weights[:, S:384], start=False, stop=True,
                     skip_group_check=True)


HYBRID_SEMS = RMS_SEMS + [
    "params", "wf_hi", "wf_ready", "pads", "u_copied", "gelu_done", "xc_done", "gate_mm", "ri_done", "lam_abs", "lam_ln",
    "lam_done", "log_a", "a_done", "th_done", "one_minus", "root_done", "b_done", "y_rnn", "y_hi", "y_lo", "qkv_done",
    "f_mm", "f_ready", "f_ln", "logf", "cum_mm", "cums", "qk_ss", "qk_std", "qk_normed", "qkT_mm", "qkT_done", "s_mm", "z_done",
    "max_done", "p_exp", "p_done", "pT_mm", "pT_done", "o_mm", "o_done", "x_added", "scalar_steps", "vector_steps"]


def hybrid_stage(nc, p, a, u0):
    with ExitStack() as ctx:
        enter = ctx.enter_context

        def sb(name, shape, dt=F32):
            return enter(nc.sbuf_tensor(name, shape, dt))

        w = p.w
        sem = {s: enter(nc.semaphore(f"hybrid_{s}")) for s in HYBRID_SEMS}
        yT = [sb(n, [P, KT, S], F32R) for n in ("hy_yT_hi", "hy_yT_lo")]
        wf = [sb(n, [P, KT, FOX_HEADS], F32R) for n in ("wf_hi", "wf_lo")]
        wf_raw = sb("wf_raw", [P, KT * FOX_HEADS])
        uc = sb("uc", [P, 4, S + 3])
        xc = sb("xc", [P, 4, S])
        gl = sb("gl", [P, 4, S])
        ri = sb("ri", [P, 2, 4, S])
        la = sb("la", [P, 4, S])
        th = sb("th", [P, 4, S])
        gw = sb("gw", [P, 2, 4, P])
        pp = sb("pp", [P, 4 * 4 + 4 + 8 + 4])
        fb = sb("fb", [P, FOX_HEADS])
        qk_gain = sb("qk_gain", [P, 2, HD])
        qkv = sb("qkv", [P, TT, 3, 512])
        qk_sq = sb("qk_sq", [P, 1024])
        qkT = sb("qkT", [P, 8, S])
        yF = sb("hy_yF", [P, 4, S])
        zs = sb("zs", [P, 2, 384])
        pT = sb("pT", [P, 2, 384])
        sm = sb("hy_sm", [P, 256])
        ps, ident, tri, ones = p.ps, p.ident, p.tri, p.ones
        conv_w, conv_b, gate_b, lam = (pp[:, 0:16].rearrange("p (c j) -> p c j", j=4), pp[:, 16:20],
                                       pp[:, 20:28].rearrange("p (g c) -> p g c", g=2), pp[:, 28:32])
        lam1, lam2 = sm[:, 0:4], sm[:, 4:8]
        f1, f2, lf, nlf, cf, ctot = (sm[:, 8 + 16 * i:24 + 16 * i].rearrange("p (t h) -> p t h", t=TT) for i in range(6))
        qs = sm[:, 104:136].rearrange("p (t h) -> p t h", t=TT)
        mx, sums = sm[:, 136:152].rearrange("p (h t) -> p h t", t=TT), sm[:, 152:168].rearrange("p (h t) -> p h t", t=TT)
        one = sm[:, 168:169]
        f_ps = ps[:, 7, 0:16].rearrange("p (t h) -> p t h", t=TT)
        cum_ps = ps[:, 7, 32:64].rearrange("p (a t h) -> p a t h", a=2, t=TT)
        U_QKV = u0 + RNN_UNITS
        U_OUT = U_QKV + FOX_QKV_UNITS
        with nc.Block() as block:
            @block.sync
            def _(sp):
                sp.dma_start(p.gain[:, :], a["mix_norm_2"][0]).then_inc(sem["gain_cols"], 16)
                sp.dma_start(wf_raw[:, :], a["wf"]).then_inc(sem["params"], 16)
                sp.dma_start(pp[:, :], a["pp"]).then_inc(sem["params"], 16)
                sp.wait_ge(sem["pads"], 1)
                for g in range(2):
                    for b in range(8):
                        r = (b % 2) * HD
                        sp.dma_start(gw[r:r + HD, g, b // 2, r:r + HD], a["rg_gate_w_2"][0, g, b]).then_inc(sem["params"], 16)
                sp.dma_start(fb[:, :], a["fox_fgate_b_2"][0].partition_broadcast(P)).then_inc(sem["params"], 16)
                for i in range(2):
                    sp.dma_start(qk_gain[:, i, :], a["fox_qk_norm_2"][0, i].partition_broadcast(P)).then_inc(sem["params"], 16)
                for u in range(u0 + RING, U_OUT + HY_OUT_UNITS):
                    w.load(sp, a["w2h"][u - u0], u)
                p.load_first(sp, U_OUT + HY_OUT_UNITS)

            n_params = 16 * (2 + 16 + 3)

            @block.gpsimd
            def _(pool):
                pool.memset(gw[:, :, :, :], 0.0).then_inc(sem["pads"], 1)
                pool.memset(uc[:, :, 0:3], 0.0).then_inc(sem["pads"], 1)
                pool.memset(one, 1.0).then_inc(sem["pads"], 1)

            @block.scalar
            def _(act):
                chain = Chain(act, sem["scalar_steps"])
                rms_scalar(act, p.x, p.junk, p.ss, p.std, p.eps, ps, p.gain, p.xT[0], sem)
                act.wait_ge(sem["params"], n_params)
                act.activation(wf[0][:, :, :].rearrange("p a b -> p (a b)"), wf_raw[:, :], ACT.Copy).then_inc(sem["wf_hi"], 1)
                w.hi_through(act, u0 + 2)
                act.wait_ge(sem["pads"], 3)
                for i in range(2):
                    w.hi_through(act, u0 + i + 2)
                    act.wait_ge(w.used, u0 + i + 1)
                    act.activation(uc[:, 2 * i:2 * i + 2, 3:], ps[:, i, :].rearrange("p (a b) -> p a b", a=2), ACT.Copy)\
                       .then_inc(sem["u_copied"], 1)
                for i in range(2):
                    w.hi_through(act, u0 + i + 4)
                    act.wait_ge(w.used, u0 + i + 3)
                    act.activation(gl[:, 2 * i:2 * i + 2, :].rearrange("p a b -> p (a b)"), ps[:, 2 + i, :],
                                   ACT.Gelu_apprx_tanh).then_inc(sem["gelu_done"], 1)
                for i in range(3):
                    w.hi_through(act, U_QKV + 2 * i + 2)
                    act.wait_ge(w.used, U_QKV + 2 * i + 2)
                    for t in range(TT):
                        act.activation(qkv[:, t, i, :], ps[:, (2 * i + t) % 4, :], ACT.Copy).then_inc(sem["qkv_done"], 1)
                chain.step(act.activation(lam1, lam, ACT.Abs))
                act.wait_ge(sem["f_ready"], 1)
                chain.step(act.activation(f2, f1, ACT.Abs))
                chain.settle()
                chain.step(act.activation(lam1, lam1, ACT.Exp, scale=-1.0))
                chain.step(act.activation(f2, f2, ACT.Exp, scale=-1.0))
                chain.settle()
                act.activation(lam1, lam1, ACT.Ln, bias=one).then_inc(sem["lam_ln"], 1)
                act.activation(f2, f2, ACT.Ln, bias=one).then_inc(sem["lam_ln"], 1)
                for g in range(2):
                    for j in range(4):
                        act.wait_ge(sem["gate_mm"], 2 * g + j // 2 + 1)
                        act.activation(ri[:, g, j, :], ps[:, 2 * g + j // 2, (j % 2) * S:(j % 2 + 1) * S], ACT.Sigmoid,
                                       bias=gate_b[:, g, j:j + 1]).then_inc(sem["ri_done"], 1)
                act.wait_ge(sem["log_a"], 4)
                act.activation(th[:, :, :], la[:, :, :], ACT.Tanh).then_inc(sem["th_done"], 1)
                act.wait_ge(sem["th_done"], 1)
                act.activation(la[:, :, :], la[:, :, :], ACT.Exp).then_inc(sem["a_done"], 1)
                act.wait_ge(sem["one_minus"], 1)
                act.activation(th[:, :, :], th[:, :, :], ACT.Sqrt).then_inc(sem["root_done"], 1)
                act.wait_ge(sem["qk_ss"], 2)
                act.activation(qs, qs, ACT.Sqrt, bias=p.eps, scale=1.0 / HD).then_inc(sem["qk_std"], 1)
                for j in range(2):
                    act.wait_ge(sem["y_rnn"], 4)
                    act.activation(yT[0][:, 2 * j:2 * j + 2, :], xc[:, 2 * j:2 * j + 2, :], ACT.Copy).then_inc(sem["y_hi"], 1)
                for i in range(4):
                    act.wait_ge(sem["qkT_mm"], i + 1)
                    act.activation(qkT[:, 2 * i:2 * i + 2, :].rearrange("p a b -> p (a b)"), ps[:, i, :], ACT.Copy)\
                       .then_inc(sem["qkT_done"], 1)
                for hd in range(FOX_HEADS):
                    act.wait_ge(sem["max_done"], 2 * hd + 2)
                    for t in range(TT):
                        cols = slice(0, P) if t == 0 else slice(P, 384)
                        act.activation(zs[:, hd % 2, cols], zs[:, hd % 2, cols], ACT.Exp, bias=mx[:, hd, t:t + 1],
                                       accum_out=sums[:, hd, t:t + 1]).then_inc(sem["p_exp"], 1)
                    act.wait_ge(sem["pT_mm"], hd + 1)
                    if hd >= 2:
                        act.wait_ge(sem["o_mm"], hd - 1)
                    act.activation(pT[:, hd % 2, :], ps[:, 4 + hd % 2, 0:384], ACT.Copy).then_inc(sem["pT_done"], 1)
                for j in range(4):
                    act.wait_ge(sem["o_done"], j + 1)
                    act.activation(yT[0][:, 4 + j, :], yF[:, j, :], ACT.Copy).then_inc(sem["y_hi"], 1)
                w.hi_through(act, U_OUT + 5)

            @block.vector
            def _(dve):
                chain = Chain(dve, sem["vector_steps"])
                rms_vector(dve, chain, p.x, p.xn, p.ss, p.std, ps, p.gain, p.xT, sem)
                dve.wait_ge(sem["wf_hi"], 1)
                dve.tensor_tensor(wf[1][:, :, :].rearrange("p a b -> p (a b)"), wf_raw[:, :],
                                  wf[0][:, :, :].rearrange("p a b -> p (a b)").bitcast(F32), ALU.subtract)\
                   .then_inc(sem["wf_ready"], 1)
                w.lo_through(dve, u0 + 3)
                dve.wait_ge(sem["u_copied"], 2)
                for j in range(4):
                    for c in range(4):
                        tap, src, dst = conv_w[:, c, j:j + 1], uc[:, c, j:j + S], xc[:, c, :]
                        if j == 0:
                            ins = dve.tensor_scalar(dst, src, tap, conv_b[:, c:c + 1], ALU.mult, ALU.add)
                        else:
                            ins = dve.scalar_tensor_tensor(dst, src, tap, dst, ALU.mult, ALU.add)
                        if j == 3:
                            ins.then_inc(sem["xc_done"], 1)
                        else:
                            chain.step(ins)
                    if j < 3:
                        chain.settle()
                dve.wait_ge(sem["f_mm"], 1)
                chain.step(dve.tensor_tensor(f1, f_ps, fb[:, :].unsqueeze(1).broadcast_to([P, TT, FOX_HEADS]), ALU.add))
                chain.settle()
                dve.tensor_scalar(f1, f1, -1.0, None, ALU.mult).then_inc(sem["f_ready"], 1)
                w.lo_through(dve, U_QKV + 6)
                dve.wait_ge(sem["lam_ln"], 2)
                dve.wait_ge(sem["f_ready"], 1)
                chain.step(dve.tensor_scalar(lam2, lam, -1.0, 0.0, ALU.mult, ALU.max))
                chain.step(dve.scalar_tensor_tensor(lf, f1, 0.0, f2, ALU.max, ALU.add))
                chain.settle()
                chain.step(dve.tensor_tensor(lam2, lam2, lam1, ALU.add))
                dve.tensor_copy(nlf, lf).then_inc(sem["logf"], 1)
                dve.tensor_scalar(lf, lf, -1.0, None, ALU.mult).then_inc(sem["logf"], 1)
                chain.settle()
                chain.step(dve.tensor_scalar(lam2, lam2, -RG_C, None, ALU.mult))
                chain.settle()
                dve.wait_ge(sem["cum_mm"], 1)
                chain.step(dve.tensor_copy(cf, cum_ps[:, 0]))
                chain.step(dve.tensor_copy(ctot, cum_ps[:, 1]))
                chain.settle()
                chain.step(dve.tensor_tensor(cf[:, 1, :], cf[:, 1, :], ctot[:, 0, :], ALU.add))
                for j in range(4):
                    dve.wait_ge(sem["ri_done"], j + 1)
                    dve.tensor_scalar(la[:, j, :], ri[:, 0, j, :], lam2[:, j:j + 1], None, ALU.mult).then_inc(sem["log_a"], 1)
                dve.wait_ge(sem["a_done"], 1)
                chain.step(dve.tensor_tensor(ri[:, 0], la[:, :, :], la[:, :, :], ALU.mult))
                dve.wait_ge(sem["ri_done"], 8)
                chain.step(dve.tensor_tensor(xc[:, :, :], xc[:, :, :], ri[:, 1], ALU.mult))
                chain.settle()
                chain.step(dve.tensor_scalar(ri[:, 0], ri[:, 0], -1.0, -1.0, ALU.mult, ALU.add))
                chain.settle()
                dve.tensor_tensor(th[:, :, :], th[:, :, :], ri[:, 0], ALU.mult).then_inc(sem["one_minus"], 1)
                for t in range(TT):
                    dve.wait_ge(sem["qkv_done"], 6)
                    if t:
                        dve.wait_ge(sem["qk_ss"], t)
                    both = qkv[:, t, 0:2, :].rearrange("p a b -> p (a b)")
                    chain.step(dve.tensor_tensor(qk_sq[:, :], both, both, ALU.mult))
                    chain.settle()
                    dve.tensor_reduce(qs[:, t, :], qk_sq[:, :].rearrange("p (h d) -> p h d", d=HD), AX.X, ALU.add)\
                       .then_inc(sem["qk_ss"], 1)
                dve.wait_ge(sem["root_done"], 1)
                chain.step(dve.tensor_tensor(xc[:, :, :], xc[:, :, :], th[:, :, :], ALU.mult))
                chain.settle()
                for j in range(4):
                    chain.step(dve.tensor_tensor_scan(th[:, j, :], la[:, j, :], xc[:, j, :], 0.0, ALU.mult, ALU.add))
                chain.settle()
                dve.wait_ge(sem["gelu_done"], 2)
                for j in range(4):
                    dve.tensor_tensor(xc[:, j, :], th[:, j, :], gl[:, j, :], ALU.mult).then_inc(sem["y_rnn"], 1)
                dve.wait_ge(sem["qk_std"], 1)
                chain.step(dve.reciprocal(qs, qs))
                chain.settle()
                chain.step(dve.tensor_scalar(qs[:, :, 0:8], qs[:, :, 0:8], HD ** -0.5, None, ALU.mult))
                chain.settle()
                for t in range(TT):
                    both = qkv[:, t, 0:2, :].rearrange("p a (h d) -> p (a h) d", d=HD)
                    chain.step(dve.tensor_tensor(both, both, qs[:, t, :].unsqueeze(2).broadcast_to([P, 16, HD]), ALU.mult))
                chain.settle()
                for t in range(TT):
                    for i in range(2):
                        part = qkv[:, t, i, :].rearrange("p (h d) -> p h d", d=HD)
                        dve.tensor_tensor(part, part, qk_gain[:, i, :].unsqueeze(1).broadcast_to([P, 8, HD]), ALU.mult)\
                           .then_inc(sem["qk_normed"], 1)
                for j in range(2):
                    dve.wait_ge(sem["y_hi"], j + 1)
                    dve.tensor_tensor(yT[1][:, 2 * j:2 * j + 2, :], xc[:, 2 * j:2 * j + 2, :],
                                      yT[0][:, 2 * j:2 * j + 2, :].bitcast(F32), ALU.subtract).then_inc(sem["y_lo"], 1)
                for hd in range(FOX_HEADS):
                    z = zs[:, hd % 2, :]
                    dve.wait_ge(sem["s_mm"], hd + 1)
                    if hd >= 2:
                        dve.wait_ge(sem["pT_mm"], hd - 1)
                    chain.step(dve.scalar_tensor_tensor(z[:, 0:P], ps[:, hd % 2, 0:P], cf[:, 0, hd:hd + 1], p.causal[:, P:S],
                                                        ALU.add, ALU.add))
                    chain.step(dve.scalar_tensor_tensor(z[:, P:384], ps[:, hd % 2, P:384], cf[:, 1, hd:hd + 1], p.causal,
                                                        ALU.add, ALU.add))
                    chain.settle()
                    for t in range(TT):
                        dve.tensor_reduce(mx[:, hd, t:t + 1], z[:, 0:P] if t == 0 else z[:, P:384], AX.X, ALU.max,
                                          negate=True).then_inc(sem["max_done"], 1)
                    dve.wait_ge(sem["p_exp"], 2 * hd + 2)
                    chain.step(dve.reciprocal(sums[:, hd, :], sums[:, hd, :]))
                    chain.settle()
                    for t in range(TT):
                        part = z[:, 0:P] if t == 0 else z[:, P:384]
                        dve.tensor_scalar(part, part, sums[:, hd, t:t + 1], None, ALU.mult).then_inc(sem["p_done"], 1)
                    if hd % 2 == 1:
                        dve.wait_ge(sem["o_mm"], hd + 1)
                        dve.tensor_copy(yF[:, hd // 2, :], ps[:, 6 + (hd // 2) % 2, 0:S]).then_inc(sem["o_done"], 1)
                for j in range(4):
                    dve.wait_ge(sem["y_hi"], 2 + j + 1)
                    dve.tensor_tensor(yT[1][:, 4 + j, :], yF[:, j, :], yT[0][:, 4 + j, :].bitcast(F32), ALU.subtract)\
                       .then_inc(sem["y_lo"], 1)
                w.lo_through(dve, U_OUT + 5)
                add_to_x(dve, w, U_OUT + HY_OUT_UNITS, p.x, p.acc, 1.0, sem)

            @block.tensor
            def _(pe):
                norm_transposes(pe, ps, p.xn, ident, sem["x_normed"], (1, 2), sem)
                pe.wait_ge(sem["xT_ready"], KT)
                pe.wait_ge(sem["wf_ready"], 1)
                for t in range(TT):
                    for k in range(KT):
                        mm = split_matmul(pe, f_ps[:, t, :], (p.xT[0][:, k, t * P:(t + 1) * P], p.xT[1][:, k, t * P:(t + 1) * P]),
                                          (wf[0][:, k, :], wf[1][:, k, :]), k == 0, k == KT - 1)
                mm.then_inc(sem["f_mm"], 1)
                for u in range(RNN_UNITS):
                    split_tiles(pe, w, ps, u0 + u, u, p.xT)
                for i in range(3):
                    if i == 0:
                        pe.wait_ge(sem["u_copied"], 2)
                    elif i == 1:
                        pe.wait_ge(sem["gelu_done"], 2)
                    else:
                        pe.wait_ge(sem["qkv_done"], 2)
                    split_group(pe, w, ps, U_QKV + 2 * i, ((2 * i) % 4, (2 * i + 1) % 4), p.xT)
                pe.wait_ge(sem["logf"], 2)
                for t in range(TT):
                    pe.matmul(cum_ps[:, 0, t, :], tri, lf[:, t, :], start=True, stop=True)
                    mm = pe.matmul(cum_ps[:, 1, t, :], ones, lf[:, t, :], start=True, stop=True)
                mm.then_inc(sem["cum_mm"], 1)
                pe.wait_ge(sem["xc_done"], 4)
                pe.wait_ge(sem["qkv_done"], 6)
                pe.wait_ge(sem["params"], n_params)
                for g in range(2):
                    for j in range(4):
                        mm = pe.matmul(ps[:, 2 * g + j // 2, (j % 2) * S:(j % 2 + 1) * S], gw[:, g, j, :], xc[:, j, :],
                                       start=True, stop=True)
                        if j % 2:
                            mm.then_inc(sem["gate_mm"], 1)
                pe.wait_ge(sem["qk_normed"], 4)
                pe.wait_ge(sem["ri_done"], 8)
                for i in range(4):
                    for k in range(2):
                        for t in range(TT):
                            tile = 2 * i + k
                            mm = pe.transpose(ps[:, i, k * S + t * P:k * S + (t + 1) * P],
                                              qkv[:, t, tile // 4, (tile % 4) * P:(tile % 4 + 1) * P], ident)
                    mm.then_inc(sem["qkT_mm"], 1)
                pe.wait_ge(sem["qkT_done"], 4)

                def scores(hd):
                    rows = slice(HD * (hd % 2), HD * (hd % 2) + HD)
                    q, k = qkT[rows, hd // 2, :], qkT[rows, 4 + hd // 2, :]
                    if hd >= 2:
                        pe.wait_ge(sem["max_done"], 2 * hd - 2)
                    pe.matmul(ps[:, hd % 2, 0:P], q[:, 0:P], k[:, 0:P], start=True, stop=False, skip_group_check=True)
                    pe.matmul(ps[:, hd % 2, P:384], q[:, P:S], k, start=False, stop=False, skip_group_check=True)
                    decays = [nlf[:, t, hd:hd + 1].broadcast_to([P, P]) for t in range(TT)]
                    pe.matmul(ps[:, hd % 2, 0:P], decays[0], tri, start=False, stop=False, skip_group_check=True)
                    pe.matmul(ps[:, hd % 2, P:S], decays[0], tri, start=False, stop=False, skip_group_check=True)
                    pe.matmul(ps[:, hd % 2, S:384], decays[0], ones, start=False, stop=False, skip_group_check=True)
                    pe.matmul(ps[:, hd % 2, S:384], decays[1], tri, start=False, stop=True, skip_group_check=True)\
                      .then_inc(sem["s_mm"], 1)

                scores(0)
                for hd in range(FOX_HEADS):
                    if hd + 1 < FOX_HEADS:
                        scores(hd + 1)
                    pe.wait_ge(sem["p_done"], 2 * hd + 2)
                    if hd >= 2:
                        pe.wait_ge(sem["pT_done"], hd - 1)
                    z = zs[:, hd % 2, :]
                    for i in range(3):
                        mm = pe.transpose(ps[:, 4 + hd % 2, i * P:(i + 1) * P], z[:, i * P:(i + 1) * P], ident)
                    mm.then_inc(sem["pT_mm"], 1)
                    pe.wait_ge(sem["pT_done"], hd + 1)
                    if hd % 2 == 0 and hd >= 4:
                        pe.wait_ge(sem["o_done"], hd // 2 - 1)
                    heads_out(pe, p, hd, 6 + (hd // 2) % 2, qkv[:, :, 2, :], pT[:, hd % 2, :]).then_inc(sem["o_mm"], 1)
                pe.wait_ge(sem["y_lo"], 6)
                for half in range(2):
                    split_group(pe, w, ps, U_OUT + 2 * half, (half, 2 + half), yT)
        end_stage(nc, sem.values())


SB_SEMS = RMS_SEMS + ["qk_done", "v_done", "z_mm", "abs_done", "ln_done", "sp_done", "e_mm", "e_min", "w_exp", "w_done", "o_mm",
                      "y_hi", "y_lo", "x_added", "scalar_steps", "vector_steps"]


def stick_stage(nc, p, a, u0):
    with ExitStack() as ctx:
        enter = ctx.enter_context

        def sb(name, shape, dt=F32):
            return enter(nc.sbuf_tensor(name, shape, dt))

        w = p.w
        sem = {s: enter(nc.semaphore(f"stick_{s}")) for s in SB_SEMS}
        yT = [sb(n, [P, KT, S], F32R) for n in ("sb_yT_hi", "sb_yT_lo")]
        qkT = sb("sb_qkT", [P, 16, S])
        v = sb("sb_v", [P, TT, D])
        ln = sb("sb_ln", [P, 2, 384])
        sp_ = sb("sb_sp", [P, 2, 384])
        wt = sb("sb_w", [P, 2, 384])
        ps = p.ps
        U_V = u0 + SB_QK_UNITS
        U_OUT = U_V + SB_V_UNITS

        def diagonals(t):
            return t.rearrange("p (a b) -> p a b", b=P)[:, 0:3:2, :]

        with nc.Block() as block:
            @block.sync
            def _(sp):
                sp.dma_start(p.gain[:, :], a["mix_norm_2"][1]).then_inc(sem["gain_cols"], 16)
                for u in range(u0 + RING, U_OUT + SB_OUT_UNITS):
                    w.load(sp, a["w2s"][u - u0], u)
                p.load_first(sp, U_OUT + SB_OUT_UNITS)

            @block.scalar
            def _(act):
                chain = Chain(act, sem["scalar_steps"])
                rms_scalar(act, p.x, p.junk, p.ss, p.std, p.eps, ps, p.gain, p.xT[0], sem)
                for u in range(SB_QK_UNITS):
                    w.hi_through(act, u0 + u + 2)
                    act.wait_ge(w.used, u0 + u + 1)
                    act.activation(qkT[:, 2 * u:2 * u + 2, :].rearrange("p a b -> p (a b)"), ps[:, u % 4, :], ACT.Copy,
                                   scale=HD ** -0.5 if u < 4 else 1.0).then_inc(sem["qk_done"], 1)
                for i in range(2):
                    w.hi_through(act, U_V + 2 * i + 2)
                    act.wait_ge(w.used, U_V + 2 * i + 2)
                    for t in range(TT):
                        act.activation(v[:, t, i * 512:(i + 1) * 512], ps[:, 2 * i + t, :], ACT.Copy).then_inc(sem["v_done"], 1)
                w.hi_through(act, U_OUT + 2)
                act.preload_act_table_set("natural_log_exp_and_others")

                def softplus(hd):
                    act.wait_ge(sem["z_mm"], hd + 1)
                    if hd >= 2:
                        act.wait_ge(sem["sp_done"], hd - 1)
                    l = ln[:, hd % 2, :]
                    chain.step(act.activation(l, ps[:, hd % 4, 0:384], ACT.Abs))
                    chain.settle()
                    chain.step(act.activation(l, l, ACT.Exp, scale=-1.0))
                    chain.settle()
                    act.activation(l, l, ACT.Ln, bias=p.one).then_inc(sem["ln_done"], 1)

                def exponentials(hd):
                    act.wait_ge(sem["e_min"], hd + 1)
                    act.activation(wt[:, hd % 2, :], wt[:, hd % 2, :], ACT.Exp).then_inc(sem["w_exp"], 1)

                def output(tile):
                    act.wait_ge(sem["o_mm"], 2 * tile + 2)
                    act.activation(yT[0][:, tile, :], ps[:, 4 + tile % 2, 0:S], ACT.Copy).then_inc(sem["y_hi"], 1)

                softplus(0)
                for hd in range(SB_HEADS):
                    if hd + 1 < SB_HEADS:
                        softplus(hd + 1)
                    exponentials(hd)
                    if hd >= 2 and hd % 2 == 0:
                        output(hd // 2 - 1)
                output(SB_HEADS // 2 - 1)
                w.hi_through(act, U_OUT + 5)

            @block.vector
            def _(dve):
                chain = Chain(dve, sem["vector_steps"])
                rms_vector(dve, chain, p.x, p.xn, p.ss, p.std, ps, p.gain, p.xT, sem)
                w.lo_through(dve, U_OUT + 2)
                strict2 = p.strict.unsqueeze(1).broadcast_to([P, 2, P])

                def softplus(hd):
                    dve.wait_ge(sem["ln_done"], hd + 1)
                    s_ = sp_[:, hd % 2, :]
                    if hd >= 2:
                        dve.wait_ge(sem["e_mm"], hd - 1)
                    chain.step(dve.scalar_tensor_tensor(s_, ps[:, hd % 4, 0:384], 0.0, ln[:, hd % 2, :], ALU.max, ALU.add))
                    chain.settle()
                    dve.tensor_tensor(diagonals(s_), diagonals(s_), strict2, ALU.mult).then_inc(sem["sp_done"], 1)

                def weights(hd):
                    dve.wait_ge(sem["e_mm"], hd + 1)
                    if hd >= 2:
                        dve.wait_ge(sem["o_mm"], hd - 1)
                    w_ = wt[:, hd % 2, :]
                    dve.tensor_scalar(w_, ps[:, hd % 4, 0:384], 0.0, None, ALU.min).then_inc(sem["e_min"], 1)
                    dve.wait_ge(sem["w_exp"], hd + 1)
                    dve.tensor_tensor(diagonals(w_), diagonals(w_), strict2, ALU.mult).then_inc(sem["w_done"], 1)

                def output(tile):
                    dve.wait_ge(sem["y_hi"], tile + 1)
                    dve.tensor_tensor(yT[1][:, tile, :], ps[:, 4 + tile % 2, 0:S], yT[0][:, tile, :].bitcast(F32),
                                      ALU.subtract).then_inc(sem["y_lo"], 1)

                softplus(0)
                for hd in range(SB_HEADS):
                    if hd + 1 < SB_HEADS:
                        softplus(hd + 1)
                    weights(hd)
                    if hd >= 2 and hd % 2 == 0:
                        output(hd // 2 - 1)
                output(SB_HEADS // 2 - 1)
                w.lo_through(dve, U_OUT + 5)
                add_to_x(dve, w, U_OUT + SB_OUT_UNITS, p.x, p.acc, 1.0, sem)

            @block.tensor
            def _(pe):
                norm_transposes(pe, ps, p.xn, p.ident, sem["x_normed"], (1, 2), sem)
                pe.wait_ge(sem["xT_ready"], KT)
                for u in range(SB_QK_UNITS):
                    if u >= 4:
                        pe.wait_ge(sem["qk_done"], u - 3)
                    split_tiles(pe, w, ps, u0 + u, u % 4, p.xT)
                for i in range(2):
                    pe.wait_ge(sem["qk_done"], 6 + 2 * i)
                    split_group(pe, w, ps, U_V + 2 * i, (2 * i, 2 * i + 1), p.xT)

                def scores(hd):
                    rows = slice(HD * (hd % 2), HD * (hd % 2) + HD)
                    q, k = qkT[rows, hd // 2, :], qkT[rows, 8 + hd // 2, :]
                    if hd >= 4:
                        pe.wait_ge(sem["e_min"], hd - 3)
                    pe.matmul(ps[:, hd % 4, 0:S], k[:, 0:P], q, start=True, stop=False, skip_group_check=True)
                    pe.matmul(ps[:, hd % 4, S:384], k[:, P:S], q[:, P:S], start=False, stop=False, skip_group_check=True)\
                      .then_inc(sem["z_mm"], 1)

                def exponents(hd):
                    s_ = sp_[:, hd % 2, :]
                    pe.wait_ge(sem["sp_done"], hd + 1)
                    pe.matmul(ps[:, hd % 4, 0:S], p.neg_from, s_[:, 0:S], start=False, stop=False, skip_group_check=True)
                    pe.matmul(ps[:, hd % 4, P:S], p.neg_ones, s_[:, S:384], start=False, stop=False, skip_group_check=True)
                    pe.matmul(ps[:, hd % 4, S:384], p.neg_from, s_[:, S:384], start=False, stop=True, skip_group_check=True)\
                      .then_inc(sem["e_mm"], 1)

                pe.wait_ge(sem["v_done"], 4)
                scores(0)
                scores(1)
                exponents(0)
                for hd in range(SB_HEADS):
                    if hd + 2 < SB_HEADS:
                        scores(hd + 2)
                    if hd + 1 < SB_HEADS:
                        exponents(hd + 1)
                    pe.wait_ge(sem["w_done"], hd + 1)
                    if hd % 2 == 0 and hd >= 4:
                        pe.wait_ge(sem["y_lo"], hd // 2 - 1)
                    heads_out(pe, p, hd, 4 + (hd // 2) % 2, v, wt[:, hd % 2, :]).then_inc(sem["o_mm"], 1)
                pe.wait_ge(sem["y_lo"], 8)
                for half in range(2):
                    split_group(pe, w, ps, U_OUT + 2 * half, (half, 2 + half), yT)
        end_stage(nc, sem.values())


def block_two(nc, a):
    with ExitStack() as ctx:
        enter = ctx.enter_context

        def sb(name, shape, dt=F32):
            return enter(nc.sbuf_tensor(name, shape, dt))

        p = Parts()
        p.x = a["x_sb"]
        p.ps = enter(nc.psum_tensor("ps2", [P, 8, 512], F32))
        p.ring = (sb("raw2", [P, RING, UNIT]), sb("w2_hi", [P, RING, UNIT], F32R), sb("w2_lo", [P, RING, UNIT], F32R))
        p.xT = [sb(n, [P, KT, S], F32R) for n in ("x2T_hi", "x2T_lo")]
        p.hT = [sb(n, [P, 2, S], F32R) for n in ("h2T_hi", "h2T_lo")]
        p.zero = sb("zero2", [P, P], F32R)
        p.xn = sb("xn", [P, TT, D])
        p.junk = sb("junk2", [P, D])[:, :]
        p.gate, p.h = sb("gate2", [P, 2, S]), sb("h2", [P, 2, S])
        cm = sb("cm2", [P, a["masks2"].shape[1]])
        p.gain = sb("gain2", [P, KT])
        sm = sb("sm2", [P, 8])
        p.ss, p.std, p.eps, p.one = sm[:, 0:2], sm[:, 2:4], sm[:, 4:5], sm[:, 5:6]
        p.ident, p.tri, p.strict, p.ones, p.neg_from, p.neg_ones = (cm[:, i * P:(i + 1) * P] for i in range(6))
        p.causal = cm[:, 6 * P:8 * P]
        p.acc, p.up_ps = p.ps[:, 0:4, :], p.ps[:, 4:6, :]
        with ExitStack() as c2:
            loaded = c2.enter_context(nc.semaphore("constants2"))
            with nc.Block() as block:
                @block.sync
                def _(sp):
                    sp.dma_start(cm[:, :], a["masks2"]).then_inc(loaded, 16)
                    sp.wait_ge(loaded, 16)

                @block.gpsimd
                def _(pool):
                    pool.memset(p.zero[:, :].bitcast(F32), 0.0)
                    pool.memset(p.eps, RMS_EPS)
                    pool.memset(p.one, 1.0)
            end_stage(nc, [loaded])
        p.w = Weights(nc, enter, *p.ring)
        stages = [("ffn", 0), ("hybrid", 0), ("ffn", 1), ("ffn", 2), ("stick", 0), ("ffn", 3)]
        units = {"ffn": FFN_UNITS, "hybrid": RNN_UNITS + FOX_QKV_UNITS + HY_OUT_UNITS,
                 "stick": SB_QK_UNITS + SB_V_UNITS + SB_OUT_UNITS}
        u0 = 0
        for (kind, n), after in zip(stages, [*stages[1:], None]):
            def load_first(sp, u, after=after):
                if after[0] == "ffn":
                    ffn_load_first(sp, p.w, u, lambda pair, f: a["up"][DEPTH + after[1], pair, f])
                else:
                    for j in range(RING):
                        p.w.load(sp, a["w2h" if after[0] == "hybrid" else "w2s"][j], u + j)

            p.load_first = load_first
            if kind == "ffn":
                ffn_stage(nc, p, a, n, f"ffn{n}", u0, last=after is None)
            elif kind == "hybrid":
                hybrid_stage(nc, p, a, u0)
            else:
                stick_stage(nc, p, a, u0)
            u0 += units[kind]


def program(nc, a, out):
    with ExitStack() as ctx:
        x = ctx.enter_context(nc.sbuf_tensor("x", [P, TT, D], F32))
        a["x_sb"] = x
        block_one(nc, a)
        block_two(nc, a)
        with ExitStack() as c:
            stored = c.enter_context(nc.semaphore("stored"))
            with nc.Block() as block:
                @block.sync
                def _(sp):
                    sp.dma_start(out[0].rearrange("(t p) n -> p t n", p=P), x[:, :, :]).then_inc(stored, 16)
                    sp.wait_ge(stored, 16)


def _units_by_tiles(m):
    n = m.shape[1]
    return m.reshape(KT, P, n // 256, 2, P).transpose(2, 1, 3, 0, 4).reshape(n // 256, P, UNIT)


def _units_by_groups(m):
    n = m.shape[1]
    return m.reshape(2, 4, P, n // 512, 512).transpose(3, 0, 2, 1, 4).reshape(2 * (n // 512), P, UNIT)


def _units_of_ffn(up, down):
    u = up.reshape(KT, P, 2, FPAIRS, 2, P).transpose(3, 4, 1, 2, 0, 5).reshape(FPAIRS, 2, P, UNIT)
    d = down.reshape(FPAIRS, 2, P, D).transpose(0, 2, 1, 3).reshape(FPAIRS, P, UNIT)
    return u, d


def _columns(m):
    return np.ascontiguousarray(np.swapaxes(m.reshape(*m.shape[:-1], -1, P), -1, -2))


def _masks():
    i = np.arange(P)
    j = i[:, None]
    tri, strict = (j <= i), (j < i)
    levels = []
    for lv in range(7):
        s = 1 << lv
        row, col = i[:, None], i[None, :]
        levels.append((row // (2 * s) == col // (2 * s)) & (row // s % 2 == 1) & (col // s % 2 == 0))
    ident, ones = np.eye(P), np.ones((P, P))
    m1 = np.concatenate([ident, tri, strict, ones, levels[0].T, *levels[1:]], 1).astype(np.float32)
    causal = np.where(i[None, :] <= i[:, None], 0.0, -BIG)
    m2 = np.concatenate([ident, tri, strict, ones, -(j >= i).astype(np.float32), -ones, np.zeros((P, P)), causal], 1)
    return m1, m2.astype(np.float32)


def _lay_out(i):
    i = {k: np.asarray(v) for k, v in i.items()}
    w1, wg = [], []
    cuts = np.cumsum([512, 512, 1024, 1024, 4, 4, 3072, 1024, 8, 8, 1024, 1024])[:-1]
    for l in range(DEPTH):
        qa, ka, va, oa, ia, fa, qkv, zb, be, ab, ga, gb = np.split(i["w_in"][l], cuts, axis=1)

        def pairs(gate, branch):
            both = np.stack([gate.reshape(D, KT, P), branch.reshape(D, KT, P)], 2).reshape(D, 2 * D)
            return _units_by_tiles(both)

        w1.append(np.concatenate([
            _units_by_tiles(qkv), _units_by_tiles(qa), _units_by_tiles(ka), _units_by_groups(va), _units_by_tiles(oa),
            pairs(ga, i["w_branch_a"][l]), _units_by_tiles(zb), pairs(gb, i["w_branch_b"][l]),
            _units_by_groups(i["w_out"][l])]))
        wg.append(np.concatenate([ia, fa, be, ab], 1).reshape(KT, P, N_GATES).transpose(1, 0, 2).reshape(P, -1))
    assert w1[0].shape[0] == MIX1_UNITS
    pa = np.zeros((DEPTH, P, 128), np.float32)
    for l in range(DEPTH):
        pa[l, :, 0:96] = i["conv_w"][l].reshape(4, 24, P).transpose(2, 1, 0).reshape(P, 96)
        pa[l, :, 96:100] = i["b_igate"][l]
        pa[l, :, 100:104] = i["b_fgate"][l]
        pa[l, :, 112:120] = i["dt_bias"][l]
        pa[l, :, 120:128] = i["a_log"][l]
    ffn = [_units_of_ffn(i["w_ffn_up"][l], i["w_ffn_down"][l]) for l in range(DEPTH)]
    ffn += [_units_of_ffn(i["ffn_w_in_2"][l, j], i["ffn_w_out_2"][l, j]) for l in range(DEPTH) for j in range(2)]
    hy = i["hy_w_in_2"][0]
    w2h = np.concatenate([_units_by_tiles(hy[:, 0:1024]), _units_by_groups(hy[:, 1024:2560]), _units_by_groups(i["hy_w_out_2"][0])])
    sbw = i["sb_w_qkv_2"][0]
    w2s = np.concatenate([_units_by_tiles(sbw[:, 0:2048]), _units_by_groups(sbw[:, 2048:]), _units_by_groups(i["sb_w_out_2"][0])])
    pp = np.concatenate([i["rg_conv_w_2"][0].reshape(4, 4, P).transpose(2, 1, 0).reshape(P, 16), _columns(i["rg_conv_b_2"][0]),
                         i["rg_gate_b_2"][0].reshape(8, P).T, _columns(i["rg_lambda_2"][0])], 1)
    m1, m2 = _masks()
    sel = np.zeros((A_HEADS, A_HEADS, P), np.float32)
    for hd in range(A_HEADS):
        sel[hd, hd] = 1.0
    return {
        "x": i["x"], "w1": np.stack(w1), "wg": np.stack(wg), "pa": pa, "g_gdn": i["g_gdn_norm"], "g_mlstm": i["g_mlstm_norm"],
        "ln1_g": i["ln1_g"], "ln1_b": i["ln1_b"], "ln2_g": i["ln2_g"], "ln2_b": i["ln2_b"],
        "up": np.stack([f[0] for f in ffn]), "dn": np.stack([f[1] for f in ffn]), "w2h": w2h, "w2s": w2s,
        "wf": hy[:, 2560:].reshape(KT, P, FOX_HEADS).transpose(1, 0, 2).reshape(P, -1), "pp": pp,
        "rg_gate_w_2": i["rg_gate_w_2"], "fox_fgate_b_2": i["fox_fgate_b_2"], "fox_qk_norm_2": i["fox_qk_norm_2"],
        "ffn_norm_2": _columns(i["ffn_norm_2"].reshape(4, D)), "mix_norm_2": _columns(i["mix_norm_2"]),
        "masks": m1, "masks2": m2, "sel": sel,
    }


def kernel(**inputs):
    import concourse.bacc as bacc
    from concourse.bass_utils import run_bass_kernel_spmd

    nc = bacc.Bacc("TRN2", target_bir_lowering=False, num_devices=1)
    arrays, aps = {}, {}
    for name, array in _lay_out(inputs).items():
        array = np.ascontiguousarray(array)
        arrays[f"in_{name}"] = array
        aps[name] = nc.dram_tensor(f"in_{name}", array.shape, mybir.dt.from_np(array.dtype), kind="ExternalInput").ap()
    out = nc.dram_tensor("out", (1, S, D), F32, kind="ExternalOutput").ap()
    program(nc, aps, out)
    r = run_bass_kernel_spmd(nc, [arrays], core_ids=[0])
    return r.results[0]["out"]
```

```python
import math
from contextlib import ExitStack

import numpy as np

import concourse.bass as bass
from concourse import mybir

F32 = mybir.dt.float32
F32R = mybir.dt.float32r
ALU = mybir.AluOpType
ACT = mybir.ActivationFunctionType
AX = mybir.AxisListType

P = 128
DEPTH = 2
D = 1024
S = 256
TT = S // P
KT = D // P
D_FF = 2816
FPAIRS = D_FF // (2 * P)
UNIT = 2048
RING = 3
EARLY = 2
ALPHA = (2.0 * DEPTH) ** 0.25
LN_EPS = 1e-5
RMS_EPS = 1e-6
BIG = 1e30

A_HEADS, A_DK, A_DV = 4, 128, 256
B_HEADS, B_DK = 8, 128
CAP = 15.0
QKV_UNITS = 12
QKA_UNITS = 4
VA_UNITS = 4
OA_UNITS = 4
BRANCH_UNITS = 8
ZB_UNITS = 4
OUT_UNITS = 4
MIX1_UNITS = QKV_UNITS + QKA_UNITS + VA_UNITS + OA_UNITS + ZB_UNITS + 2 * BRANCH_UNITS + OUT_UNITS
FFN_UNITS = 3 * FPAIRS
N_GATES = 2 * A_HEADS + 2 * B_HEADS


def split_matmul(pe, out, lhs, rhs, start, stop):
    (lhs_hi, lhs_lo), (rhs_hi, rhs_lo) = lhs, rhs
    pe.matmul(out, lhs_hi, rhs_hi, start=start, stop=False, skip_group_check=True)
    pe.matmul(out, lhs_hi, rhs_lo, start=False, stop=False, skip_group_check=True)
    return pe.matmul(out, lhs_lo, rhs_hi, start=False, stop=stop, skip_group_check=True)


class Chain:

    def __init__(self, engine, sem):
        self.engine, self.sem, self.n = engine, sem, 0

    def step(self, ins):
        ins.then_inc(self.sem, 1)
        self.n += 1

    def settle(self):
        self.engine.wait_ge(self.sem, self.n)


class Weights:

    def __init__(self, nc, enter, raw, hi, lo):
        self.nc, self.raw, self.hi, self.lo = nc, raw, hi, lo
        self.loaded = [enter(nc.semaphore(f"unit_loaded_{i}")) for i in range(RING)]
        self.hi_done = enter(nc.semaphore("unit_hi_done"))
        self.lo_done = enter(nc.semaphore("unit_lo_done"))
        self.used = enter(nc.semaphore("unit_used"))
        self.begin(False)

    def begin(self, handed_on):
        self.handed_on = handed_on
        self.hi_next = self.lo_next = EARLY if handed_on else 0

    def sems(self):
        return [*self.loaded, self.hi_done, self.lo_done, self.used]

    def wait_parts(self, engine, sem, u, turn=0):
        count = u + 1 - (EARLY if self.handed_on else 0)
        if count > 0:
            engine.wait_ge(sem, count + RING * turn)

    def load(self, sp, src, u, turn=0):
        slot = u % RING
        if u >= RING:
            self.wait_parts(sp, self.lo_done, u - RING, turn)
        sp.dma_start(self.raw[:, slot, :], src).then_inc(self.loaded[slot], 16)

    def split_hi(self, act, u, turn=0):
        slot = u % RING
        count = u // RING + (0 if self.handed_on else 1)
        if count > 0:
            act.wait_ge(self.loaded[slot], 16 * count + 16 * turn)
        if u >= RING:
            act.wait_ge(self.used, u - RING + 1 + RING * turn)
        act.activation(self.hi[:, slot, :], self.raw[:, slot, :], ACT.Copy).then_inc(self.hi_done, 1)

    def split_lo(self, dve, u, turn=0):
        slot = u % RING
        self.wait_parts(dve, self.hi_done, u, turn)
        dve.tensor_tensor(self.lo[:, slot, :], self.raw[:, slot, :], self.hi[:, slot, :].bitcast(F32),
                          ALU.subtract).then_inc(self.lo_done, 1)

    def hi_through(self, act, u):
        while self.hi_next <= u:
            self.split_hi(act, self.hi_next)
            self.hi_next += 1

    def lo_through(self, dve, u):
        while self.lo_next <= u:
            self.split_lo(dve, self.lo_next)
            self.lo_next += 1

    def arrived(self, sp, units):
        for slot in range(RING):
            sp.wait_ge(self.loaded[slot], 16 * (units // RING + (0 if self.handed_on else 1)))

    def lo_half(self, dve, half):
        slot, cols = self.lo_next % RING, slice(half * UNIT // 2, (half + 1) * UNIT // 2)
        self.wait_parts(dve, self.hi_done, self.lo_next)
        ins = dve.tensor_tensor(self.lo[:, slot, cols], self.raw[:, slot, cols], self.hi[:, slot, cols].bitcast(F32),
                                ALU.subtract)
        if half:
            ins.then_inc(self.lo_done, 1)
            self.lo_next += 1

    def pair(self, u, shape, *index):
        def view(t):
            v = t[:, u % RING, :].rearrange("p (a b) -> p a b", b=shape[1])
            return v[(slice(None), *index)]
        return view(self.hi), view(self.lo)


def ffn_tensor(pe, w, u0, xT, hT, acc, up_ps, zero, sem, xT_ready, xT_by_tile):
    def up(u, turn, first=False):
        for f in range(2):
            w.wait_parts(pe, w.lo_done, u + f, turn)
            if not first:
                pe.wait_ge(sem["h_done"], f + 1 + 2 * turn)
            for part in range(2):
                for k in range(KT):
                    if first and f == part == 0:
                        pe.wait_ge(xT_ready, max(k + 1, 2) if xT_by_tile else k // 2 + 1)
                    mm = split_matmul(pe, up_ps[:, f, part * S:(part + 1) * S],
                                      w.pair(u + f, (16, P), part * KT + k, slice(None)),
                                      (xT[0][:, k, :], xT[1][:, k, :]), k == 0, k == KT - 1)
            mm.then_inc(w.used, 1)

    def down(u, turn, pairs_before, last=False):
        w.wait_parts(pe, w.lo_done, u, turn)
        pe.wait_ge(sem["hT_ready"], pairs_before + 1 + turn)
        for t in range(TT):
            for f in range(2):
                for half in range(2):
                    mm = split_matmul(pe, acc[:, 2 * t + half, :],
                                      (hT[0][:, f, t * P:(t + 1) * P], hT[1][:, f, t * P:(t + 1) * P]),
                                      w.pair(u, (4, 512), 2 * f + half, slice(None)), False, last and f == 1)
            if last and t < TT - 1:
                mm.then_inc(sem["acc_done"], 1)
        mm.then_inc(w.used, 1)

    up(u0, 0, first=True)
    for b in range(4):
        pe.matmul(acc[:, b, :], zero[:, :], xT[0][:, 0:2, :].rearrange("p a b -> p (a b)"), start=True, stop=False, skip_group_check=True)
    with pe.Fori(0, FPAIRS - 1) as i:
        up(u0 + 2, i)
        down(u0 + 4, i, 0)
    down(u0 + 2 + 3 * (FPAIRS - 1), 0, FPAIRS - 1, last=True)


def ffn_scalar(act, w, u0, up_ps, gate, h, hT_hi, sem, ahead):
    def hidden(u, pair, turn, ahead=0):
        for f in range(2):
            act.wait_ge(w.used, u + f + 1 + RING * turn)
            act.activation(gate[:, f, :], up_ps[:, f, 0:S], ACT.Silu).then_inc(sem["gate_done"], 1)
        if ahead:
            w.hi_through(act, u0 + FFN_UNITS)
        for f in range(2):
            act.wait_ge(sem["h_done"], 2 * pair + f + 1 + 2 * turn)
            if f == 0:
                act.wait_ge(w.used, u + 3 + RING * turn if pair else u + 2)
            act.activation(hT_hi[:, f, :], h[:, f, :], ACT.Copy).then_inc(sem["hT_hi_done"], 1)

    w.hi_through(act, u0 + 2)
    hidden(u0, 0, 0)
    with act.Fori(0, FPAIRS - 2) as i:
        for j in range(3):
            w.split_hi(act, u0 + 3 + j, i)
        hidden(u0 + 2, 1, i)
    w.hi_next = u0 + 3 * (FPAIRS - 1)
    w.hi_through(act, u0 + 3 * FPAIRS - 1)
    hidden(u0 + 2 + 3 * (FPAIRS - 2), FPAIRS - 1, 0, ahead)
    if ahead:
        w.hi_through(act, u0 + FFN_UNITS + 1)


def ffn_vector(dve, w, u0, up_ps, gate, h, hT, sem, ahead):
    def hidden(pair, turn, ahead=0):
        if pair:
            dve.wait_ge(sem["hT_ready"], pair + turn)
        for f in range(2):
            dve.wait_ge(sem["gate_done"], 2 * pair + f + 1 + 2 * turn)
            dve.tensor_tensor(h[:, f, :], gate[:, f, :], up_ps[:, f, S:2 * S], ALU.mult).then_inc(sem["h_done"], 1)
        if ahead:
            w.lo_through(dve, u0 + FFN_UNITS)
        dve.wait_ge(sem["hT_hi_done"], 2 * pair + 2 + 2 * turn)
        dve.tensor_tensor(hT[1][:, :, :], h[:, :, :], hT[0][:, :, :].bitcast(F32), ALU.subtract)\
           .then_inc(sem["hT_ready"], 1)

    w.lo_through(dve, u0 + 2)
    hidden(0, 0)
    with dve.Fori(0, FPAIRS - 2) as i:
        for j in range(3):
            w.split_lo(dve, u0 + 3 + j, i)
        hidden(1, i)
    w.lo_next = u0 + 3 * (FPAIRS - 1)
    w.lo_through(dve, u0 + 3 * FPAIRS - 1)
    hidden(FPAIRS - 1, 0, ahead)
    if ahead:
        w.lo_through(dve, u0 + FFN_UNITS + 1)


def ffn_load_first(sp, w, u0, up_w):
    for f in range(2):
        w.load(sp, up_w(0, f), u0 + f)
    w.load(sp, up_w(1, 0), u0 + 2)


def ffn_load(sp, w, u0, up_w, down_w, first=0):
    if not first:
        ffn_load_first(sp, w, u0, up_w)
    peeled = 0
    if w.handed_on and u0 == 0:
        peeled = 1
        w.load(sp, up_w(1, 1), u0 + 3)
        w.load(sp, down_w(0), u0 + 4)
        w.load(sp, up_w(2, 0), u0 + 5)
    with sp.Fori(0, FPAIRS - 2 - peeled) as i:
        w.load(sp, up_w(i + 1 + peeled, 1), u0 + 3 + 3 * peeled, i)
        w.load(sp, down_w(i + peeled), u0 + 4 + 3 * peeled, i)
        w.load(sp, up_w(i + 2 + peeled, 0), u0 + 5 + 3 * peeled, i)
    last = u0 + 3 * (FPAIRS - 1)
    w.load(sp, up_w(FPAIRS - 1, 1), last)
    w.load(sp, down_w(FPAIRS - 2), last + 1)
    w.load(sp, down_w(FPAIRS - 1), last + 2)


def norm_transposes(pe, ps, x, ident, ready, counts, sem):
    for t in range(TT):
        pe.wait_ge(ready, counts[t])
        for j in range(4):
            for k in range(2):
                mm = pe.transpose(ps[:, 4 + j, k * S + t * P:k * S + (t + 1) * P],
                                  x[:, t, (2 * j + k) * P:(2 * j + k + 1) * P], ident[:, :])
            if t == TT - 1:
                mm.then_inc(sem["xT_mm"], 1)


def layer_norm_vector(dve, chain, w, units, x, acc, gain, shift, stats, sem):
    mean_var, std, rstd, raw_stats = stats
    for t in range(TT):
        if t == 0:
            dve.wait_ge(sem["acc_done"], 1)
        else:
            dve.wait_ge(w.used, units)
        for half in range(2):
            cols = slice(half * 512, (half + 1) * 512)
            chain.step(dve.scalar_tensor_tensor(x[:, t, cols], x[:, t, cols], ALPHA, acc[:, 2 * t + half, :],
                                                ALU.mult, ALU.add))
        chain.settle()
        for half in range(2):
            chain.step(dve.bn_stats(raw_stats[:, t, half, :], x[:, t, half * 512:(half + 1) * 512]))
        chain.settle()
        dve.bn_aggr(mean_var[:, t, :], raw_stats[:, t, :, :].rearrange("p a b -> p (a b)")).then_inc(sem["var_done"], 1)
        dve.wait_ge(sem["var_done"], t + 1)
        dve.wait_ge(sem["norm_rows"], 32)
        chain.step(dve.scalar_tensor_tensor(x[:, t, :], x[:, t, :], mean_var[:, t, 0:1], gain, ALU.subtract, ALU.mult))
        dve.wait_ge(sem["std_done"], t + 1)
        chain.step(dve.reciprocal(rstd[:, t:t + 1], std[:, t:t + 1]))
        chain.settle()
        dve.scalar_tensor_tensor(x[:, t, :], x[:, t, :], rstd[:, t:t + 1], shift, ALU.mult, ALU.add)\
           .then_inc(sem["x_normed"], 1)


def layer_norm_scalar(act, stats, eps, sem):
    mean_var, std, _, _ = stats
    act.preload_act_table_set("sqrt_and_others")
    for t in range(TT):
        act.wait_ge(sem["var_done"], t + 1)
        act.activation(std[:, t:t + 1], mean_var[:, t, 1:2], ACT.Sqrt, bias=eps).then_inc(sem["std_done"], 1)


def transposed_scalar(act, ps, xT_hi, sem):
    for j in range(4):
        act.wait_ge(sem["xT_mm"], j + 1)
        act.activation(xT_hi[:, 2 * j:2 * j + 2, :].rearrange("p a b -> p (a b)"), ps[:, 4 + j, :], ACT.Copy)\
           .then_inc(sem["xT_hi_done"], 1)


def transposed_vector(dve, ps, xT, sem):
    for j in range(4):
        dve.wait_ge(sem["xT_hi_done"], j + 1)
        part = slice(2 * j, 2 * j + 2)
        dve.tensor_tensor(xT[1][:, part, :].rearrange("p a b -> p (a b)"), ps[:, 4 + j, :],
                          xT[0][:, part, :].rearrange("p a b -> p (a b)").bitcast(F32),
                          ALU.subtract).then_inc(sem["xT_ready"], 1)


NORM_SEMS = ["acc_done", "var_done", "std_done", "norm_rows", "x_normed", "xT_mm", "xT_hi_done", "xT_ready"]
FFN_SEMS = ["h_done", "hT_ready", "gate_done", "hT_hi_done", "acc_done"]
MIX1_SEMS = [
    "gate_w_loaded", "gate_rows_mm", "gate_rows", "gain_loaded", "tap0_done", "hb_sums", "hb_done",
    "x_loaded", "params", "gate_w_hi", "gate_w", "gates_mm", "cv_zero", "cv_copied", "conv_done", "silu_done", "sq_done",
    "ss_mm", "qka_done", "va_done", "g24", "tanh_done", "z_ready", "ln_done", "decays", "cum_mm", "cums",
    "norms", "exps", "a_ready", "a_rows_mm", "m_rows", "m_cols_mm", "m_ready", "emt", "v_mm", "v_done", "k_mm", "k_done",
    "gb_mm", "diff", "dec_exp", "kkqk_mm", "a_done", "xt_init", "x_mm", "x_init", "p_mm", "p_done", "y_mm", "y_done",
    "ks_mm", "rhs_done", "vn_mm", "vn_done", "o_mm", "o_done", "s_mm", "s_done", "hb_sq", "hb_std",
    "kq_mm", "w_diff", "w_exp", "s_done2", "num_mm", "num_done", "ha_sq", "ha_std", "ha_done",
    "og_done", "hT_mm", "abF", "ab_hi", "ab_done", "sg_done", "yp_done", "yT_hi", "yT_done", "masks",
]
N_SMALL = 640


def block_one(nc, a):
    with ExitStack() as ctx:
        enter = ctx.enter_context

        def sb(name, shape, dt=F32):
            return enter(nc.sbuf_tensor(name, shape, dt))

        ps = enter(nc.psum_tensor("ps", [P, 8, 512], F32))
        x = a["x_sb"]
        xT = [sb(n, [P, KT, S], F32R) for n in ("xT_hi", "xT_lo")]
        abT = [sb(n, [P, KT, S], F32R) for n in ("abT_hi", "abT_lo")]
        hT = [sb(n, [P, 2, S], F32R) for n in ("hT_hi", "hT_lo")]
        wg = [sb(n, [P, KT, N_GATES], F32R) for n in ("wg_hi", "wg_lo")]
        zero = sb("zero", [P, P], F32R)
        qkvT = sb("qkvT", [P, 24, S])
        k_or_gates = sb("k_or_gates", [P, 4, 512])
        hb = sb("hb", [P, TT, B_HEADS, P])
        va = sb("va", [P, TT, A_HEADS, A_DV + 1])
        scratch = sb("scratch", [P, 6144])
        cm = sb("cm", [P, a["masks"].shape[1]])
        sel = sb("sel", [A_HEADS, A_HEADS, P])
        pa = sb("pa", [P, 96 + N_GATES + 8 + 1 + A_HEADS * A_DV])
        rows = sb("rows", [A_HEADS, 2, S])
        sm = sb("sm", [P, N_SMALL])

        ident, tri, strict, ones = (cm[:, i * P:(i + 1) * P] for i in range(4))
        level0 = cm[:, 4 * P:5 * P]
        levels = [cm[:, (5 + i) * P:(6 + i) * P] for i in range(6)]
        conv_w = pa[:, 0:96].rearrange("p (c j) -> p c j", j=4)
        gate_bias = pa[:, 96:96 + N_GATES]
        a_log = pa[:, 120:128]
        g_gdn = pa[:, 128:129]
        g_mlstm = pa[:, 129:129 + A_HEADS * A_DV]

        at = [0]

        def small(*shape):
            n = int(np.prod(shape))
            v = sm[:, at[0]:at[0] + n]
            at[0] += n
            assert at[0] <= N_SMALL
            if len(shape) == 2:
                v = v.rearrange("p (a b) -> p a b", b=shape[1])
            if len(shape) == 3:
                v = v.rearrange("p (a b c) -> p a b c", b=shape[1], c=shape[2])
            return v

        g24, t8, li, z, zabs, sp = small(2, 24), small(2, 8), small(2, 4), small(2, 12), small(2, 12), small(2, 12)
        beta, e_alog, gs, cs, tot = small(2, 8), small(8), small(2, 12), small(2, 12), small(2, 12)
        ssq, nrm, rnrm, eg, neg_eg = small(2, 16), small(2, 16), small(2, 16), small(2, 8), small(2, 8)
        kdf, cj, brk, rq, a_col, m_col, emt = (small(2, 8), small(2, 8), small(2, 8), small(2, 8), small(2, 4),
                                               small(2, 4), small(2, 4))
        den, rs8, rs4, eps_ln, eps_rms, one = small(2, 4), small(2, 8), small(2, 4), small(1), small(1), small(1)
        stats = (small(2, 2), small(2), small(2), small(2, 2, 6))

        cv = scratch[:, 0:1036].rearrange("p (r c t) -> p r c t", r=2, t=259)
        ca = scratch[:, 1040:2064].rearrange("p (r c t) -> p r c t", r=2, t=S)
        sq = scratch[:, 2064:3088].rearrange("p (r c t) -> p r c t", r=2, t=S)
        AT, attn, X, XT, PB, ST8 = (scratch[:, i * 1024:(i + 1) * 1024].rearrange("p (h t) -> p h t", t=P)
                                    for i in range(6))
        mw = scratch[:, 0:768].rearrange("p (r t) -> p r t", r=2)
        mst = scratch[:, 768:1536].rearrange("p (r t) -> p r t", r=2)
        junk = scratch[:, 1536:1792]
        abF = scratch[:, 0:2048].rearrange("p (r t) -> p r t", r=4)
        gates_a = k_or_gates
        gates_b = scratch[:, 2048:4096].rearrange("p (r t) -> p r t", r=4)
        k_tm = k_or_gates[:, 0:2, :].rearrange("p a (h d) -> p (a h) d", d=P)
        sg = scratch[:, 4096:4608].rearrange("p (r t) -> p r t", r=2)
        ln_gain, ln_shift = scratch[:, 0:1024], scratch[:, 1024:2048]
        gate = scratch[:, 4608:5120].rearrange("p (f t) -> p f t", f=2)
        h = scratch[:, 5120:5632].rearrange("p (f t) -> p f t", f=2)
        wg_raw = scratch[:, 5632:5632 + KT * N_GATES]
        yF = qkvT[:, 16:24, :]
        token_banks = ((6, 7), (4, 5))
        acc = ps[:, 0:4, :]
        up_ps = ps[:, 4:6, :]
        gate_rows = scratch[0:N_GATES, 5824:5824 + S]
        gate_rows_ps = ps[0:N_GATES, 6, 0:S]
        gates_ps = ps[:, 7, 0:48].rearrange("p (t n) -> p t n", t=TT)
        ss_ps = ps[:, 7, 64:96].rearrange("p (t n) -> p t n", t=TT)
        cum_ps = ps[:, 7, 128:176].rearrange("p (a t n) -> p a t n", a=2, t=TT)
        mcol_ps = ps[:, 7, 192:200].rearrange("p (t n) -> p t n", t=TT)
        arow_ps = ps[0:A_HEADS, 7, 256:512]

        w = a["ring"]
        sem = {n: enter(nc.semaphore(n)) for n in MIX1_SEMS}
        norm1 = {n: enter(nc.semaphore(f"{n}_1")) for n in NORM_SEMS}
        norm2 = {n: enter(nc.semaphore(f"{n}_2")) for n in dict.fromkeys(NORM_SEMS + FFN_SEMS)}
        steps = {n: enter(nc.semaphore(f"{n}_steps")) for n in ("scalar", "vector")}

        U_QKA = QKV_UNITS
        U_VA = U_QKA + QKA_UNITS
        U_OA = U_VA + VA_UNITS
        U_ZB = U_OA + OA_UNITS
        U_BA = U_ZB + ZB_UNITS
        U_BB = U_BA + BRANCH_UNITS
        U_OUT = U_BB + BRANCH_UNITS
        U_FFN = U_OUT + OUT_UNITS
        assert U_FFN == MIX1_UNITS and U_FFN % RING == 0

        intro = {n: enter(nc.semaphore(f"intro_{n}")) for n in ["loaded", "x_normed", "xT_mm", "xT_hi_done", "xT_ready"]}
        with nc.Block() as block:
            @block.sync
            def _(sp):
                w.load(sp, a["first"][0, 0], 0)
                for t in range(TT):
                    sp.dma_start(x[:, t, :], a["x"][0, t * P:(t + 1) * P, :]).then_inc(intro["x_normed"], 16)
                sp.dma_start(cm[:, :], a["masks"]).then_inc(intro["loaded"], 16)
                sp.dma_start(sel[:, :, :], a["sel"]).then_inc(intro["loaded"], 16)
                for u in range(1, RING):
                    w.load(sp, a["first"][0, u], u)
                w.arrived(sp, 0)
                sp.wait_ge(intro["loaded"], 32)

            @block.tensor
            def _(pe):
                pe.wait_ge(intro["loaded"], 32)
                norm_transposes(pe, ps, x, ident, intro["x_normed"], (32, 32), intro)

            @block.scalar
            def _(act):
                w.hi_through(act, 0)
                transposed_scalar(act, ps, xT[0], intro)
                w.hi_through(act, EARLY - 1)

            @block.vector
            def _(dve):
                w.lo_through(dve, 0)
                transposed_vector(dve, ps, xT, intro)
                w.lo_through(dve, EARLY - 1)
        end_stage(nc, [*w.sems(), *intro.values()])
        w.begin(True)

        with nc.Fori(0, DEPTH) as layer:
            with nc.Block() as block:

                @block.sync
                def _(sp_):
                    def at_layer(t):
                        return t[bass.ds(layer, 1)].rearrange("l p n -> (l p) n")


                    def mix(u):
                        w.load(sp_, a["w1"][bass.ds(layer, 1), u - RING].rearrange("l p n -> (l p) n"), u)

                    sp_.dma_start(pa[:, 0:129], at_layer(a["pa"])).then_inc(sem["params"], 16)
                    sp_.dma_start(wg_raw, at_layer(a["wg"])).then_inc(sem["gate_w_loaded"], 16)
                    sp_.dma_start(g_mlstm, a["g_mlstm"][bass.ds(layer, 1)].rearrange("l n -> (l n)").partition_broadcast(P))\
                       .then_inc(sem["gain_loaded"], 16)
                    for u in range(RING, U_FFN):
                        mix(u)
                    sp_.wait_ge(sem["ab_done"], 8)
                    for name, dst in (("ln1_g", ln_gain), ("ln1_b", ln_shift)):
                        sp_.dma_start(dst, a[name][bass.ds(layer, 1)].rearrange("l n -> (l n)").partition_broadcast(P))\
                           .then_inc(norm1["norm_rows"], 16)

                    def up_w(pair, f):
                        return a["up"][bass.ds(layer, 1), bass.ds(pair, 1) if not isinstance(pair, int) else slice(pair, pair + 1), f]\
                            .rearrange("l a p n -> (l a p) n")

                    def down_w(pair):
                        return a["dn"][bass.ds(layer, 1), bass.ds(pair, 1) if not isinstance(pair, int) else slice(pair, pair + 1)]\
                            .rearrange("l a p n -> (l a p) n")

                    ffn_load(sp_, w, U_FFN, up_w, down_w)
                    sp_.wait_ge(norm1["x_normed"], TT)
                    for name, dst in (("ln2_g", ln_gain), ("ln2_b", ln_shift)):
                        sp_.dma_start(dst, a[name][bass.ds(layer, 1)].rearrange("l n -> (l n)").partition_broadcast(P))\
                           .then_inc(norm2["norm_rows"], 16)
                    for u in range(RING):
                        w.load(sp_, a["first"][bass.ds(layer + 1, 1), u].rearrange("l p n -> (l p) n"), U_FFN + FFN_UNITS + u)
                    w.arrived(sp_, U_FFN + FFN_UNITS)

                @block.scalar
                def _(act):
                    chain = Chain(act, steps["scalar"])
                    act.wait_ge(sem["cv_zero"], 1)
                    act.wait_ge(sem["params"], 16)

                    def finish_conv(u):
                        act.wait_ge(sem["conv_done"], u + 1)
                        tiles = qkvT[:, 2 * u:2 * u + 2, :].rearrange("p a b -> p (a b)")
                        act.activation(tiles, ca[:, u % 2].rearrange("p a b -> p (a b)"), ACT.Silu).then_inc(sem["silu_done"], 1)
                        if u < 8:
                            act.wait_ge(sem["silu_done"], u + 1)
                            if u >= 2:
                                act.wait_ge(sem["ss_mm"], u - 1)
                            act.activation(sq[:, u % 2].rearrange("p a b -> p (a b)"), tiles, ACT.Square).then_inc(sem["sq_done"], 1)

                    for u in range(QKV_UNITS):
                        w.hi_through(act, u + 2)
                        act.wait_ge(w.used, u + 1)
                        if u >= 2:
                            act.wait_ge(sem["conv_done"], u - 1)
                        act.activation(cv[:, u % 2, :, 3:259], ps[:, u % 4, :].rearrange("p (a b) -> p a b", a=2),
                                       ACT.Copy).then_inc(sem["cv_copied"], 1)
                        act.wait_ge(sem["cv_copied"], u + 1)
                        if u >= 2:
                            act.wait_ge(sem["silu_done"], u - 1)
                        for k in range(2):
                            act.activation(ca[:, u % 2, k, :], cv[:, u % 2, k, 0:S], ACT.Copy,
                                           scale=conv_w[:, 2 * u + k, 0:1]).then_inc(sem["tap0_done"], 1)
                        if u == 0:
                            act.wait_ge(sem["gate_w_loaded"], 16)
                            act.activation(wg[0][:, :, :].rearrange("p a b -> p (a b)"), wg_raw, ACT.Copy)\
                               .then_inc(sem["gate_w_hi"], 1)
                        if u == 4:
                            act.wait_ge(sem["gate_rows_mm"], 1)
                            act.activation(gate_rows, gate_rows_ps, ACT.Copy).then_inc(sem["gate_rows"], 1)
                        if u >= 1:
                            finish_conv(u - 1)
                    w.hi_through(act, QKV_UNITS + 2)
                    finish_conv(QKV_UNITS - 1)
                    w.hi_through(act, U_QKA + 3)

                    act.wait_ge(sem["g24"], 1)
                    act.activation(t8, g24[:, :, 0:8], ACT.Tanh, scale=1.0 / CAP).then_inc(sem["tanh_done"], 1)
                    act.activation(beta, g24[:, :, 8:16], ACT.Sigmoid).then_inc(sem["tanh_done"], 1)
                    act.wait_ge(sem["z_ready"], 2)
                    chain.step(act.activation(zabs, z, ACT.Abs))
                    chain.settle()
                    chain.step(act.activation(zabs, zabs, ACT.Exp, scale=-1.0))
                    act.activation(e_alog, a_log, ACT.Exp).then_inc(sem["ln_done"], 1)
                    chain.settle()
                    act.activation(zabs, zabs, ACT.Ln, bias=one).then_inc(sem["ln_done"], 1)
                    w.hi_through(act, U_VA + 1)
                    act.wait_ge(sem["cums"], 3)
                    act.activation(eg, cs[:, :, 4:12], ACT.Exp).then_inc(sem["exps"], 1)
                    act.activation(kdf, kdf, ACT.Exp).then_inc(sem["exps"], 1)
                    act.activation(nrm, ssq, ACT.Sqrt, bias=eps_rms).then_inc(sem["norms"], 1)

                    def value_columns(i, banks):
                        act.wait_ge(w.used, U_VA + 2 * i + 2)
                        for t in range(TT):
                            act.activation(va[:, t, 2 * i:2 * i + 2, 0:A_DV],
                                           ps[:, banks[t], :].rearrange("p (a b) -> p a b", a=2),
                                           ACT.Copy).then_inc(sem["va_done"], 1)

                    w.hi_through(act, U_VA + 3)
                    value_columns(0, (4, 5))
                    act.wait_ge(sem["m_ready"], 1)
                    act.activation(emt, m_col, ACT.Exp, scale=-1.0).then_inc(sem["emt"], 1)
                    w.hi_through(act, U_OA)

                    act.wait_ge(sem["v_mm"], 4)
                    for i in range(QKA_UNITS):
                        act.wait_ge(w.used, U_QKA + i + 1)
                        act.activation(qkvT[:, 16 + 2 * i:18 + 2 * i, :].rearrange("p a b -> p (a b)"),
                                       ps[:, i, :], ACT.Copy).then_inc(sem["qka_done"], 1)

                    for c in range(2):
                        act.wait_ge(sem["diff"], 8 * (c + 1))
                        act.activation(PB[:, :, :], PB[:, :, :], ACT.Exp).then_inc(sem["dec_exp"], 1)
                        if c == 0:
                            value_columns(1, (6, 7))
                            w.hi_through(act, U_OA + 2)
                            for g in range(2):
                                act.wait_ge(sem["s_mm"], g + 1)
                                act.activation(ST8[:, 4 * g:4 * g + 4, :].rearrange("p a b -> p (a b)"),
                                               ps[:, 4 + g, :], ACT.Copy).then_inc(sem["s_done"], 1)
                        else:
                            act.wait_ge(sem["s_done"], 2)
                            for i in range(2):
                                act.wait_ge(w.used, U_OA + i + 1)
                                act.activation(gates_a[:, i, :], ps[:, 6 + i, :], ACT.Sigmoid).then_inc(sem["og_done"], 1)
                            w.hi_through(act, U_OA + 4)
                    act.wait_ge(sem["o_done"], 4)
                    for t in range(TT):
                        act.activation((ST8 if t else PB)[:, :, :], hb[:, t], ACT.Square).then_inc(sem["hb_sq"], 1)

                    def squares(hd):
                        for t in range(TT):
                            act.wait_ge(sem["num_done"], 2 * hd + t + 1)
                            if hd + t:
                                act.wait_ge(sem["ha_sq"], 2 * hd + t)
                            act.activation(junk, va[:, t, hd, 0:A_DV], ACT.Square,
                                           accum_out=rs4[:, t, hd:hd + 1]).then_inc(sem["ha_sq"], 1)

                    act.wait_ge(w.used, U_OA + 3)
                    act.activation(gates_a[:, 2, :], ps[:, 0, :], ACT.Sigmoid).then_inc(sem["og_done"], 1)
                    act.preload_act_table_set("natural_log_exp_and_others")
                    for hd in range(A_HEADS):
                        act.wait_ge(sem["w_diff"], 2 * hd + 2)
                        act.activation(mw[:, hd % 2, :], mw[:, hd % 2, :], ACT.Exp, scale=-1.0).then_inc(sem["w_exp"], 1)
                        if hd == A_HEADS - 1:
                            act.wait_ge(w.used, U_OA + 4)
                            act.activation(gates_a[:, 3, :], ps[:, 1, :], ACT.Sigmoid).then_inc(sem["og_done"], 1)
                        if hd:
                            squares(hd - 1)
                            w.hi_through(act, U_ZB + hd)
                    w.hi_through(act, U_ZB + A_HEADS)
                    act.preload_act_table_set("sqrt_and_others")
                    squares(A_HEADS - 1)
                    act.wait_ge(sem["ha_sq"], 8)
                    act.activation(rs4, rs4, ACT.Sqrt, bias=eps_rms, scale=1.0 / A_DV).then_inc(sem["ha_std"], 1)
                    act.wait_ge(sem["hb_sums"], 2)
                    act.activation(rs8, rs8, ACT.Sqrt, bias=eps_rms, scale=1.0 / B_DK).then_inc(sem["hb_std"], 1)
                    for i in range(4):
                        act.wait_ge(w.used, U_ZB + i + 1)
                        if i == 0:
                            act.wait_ge(sem["o_done"], 4)
                        act.activation(gates_b[:, i, :], ps[:, (2 + i) % 4, :], ACT.Silu).then_inc(sem["og_done"], 1)
                        w.hi_through(act, U_BA + i - 1)

                    def gated_heads(before):
                        if before:
                            act.wait_ge(w.used, U_BB)
                        for i in range(4):
                            act.wait_ge(sem["abF"], before + i + 1)
                            act.activation(abT[0][:, 2 * i:2 * i + 2, :].rearrange("p a b -> p (a b)"), abF[:, i, :],
                                           ACT.Copy).then_inc(sem["ab_hi"], 1)

                    def branch_gates(u0, before):
                        for i in range(KT):
                            w.hi_through(act, u0 + i + 2)
                            act.wait_ge(w.used, u0 + i + 1)
                            n = before + i
                            if n >= 2:
                                act.wait_ge(sem["yp_done"], n - 1)
                            act.activation(sg[:, n % 2, :], ps[:, i % 4, 0:S], ACT.Sigmoid).then_inc(sem["sg_done"], 1)

                    gated_heads(0)
                    branch_gates(U_BA, 0)
                    gated_heads(4)
                    branch_gates(U_BB, KT)
                    for j in range(4):
                        act.wait_ge(sem["yp_done"], KT + 2 * j + 2)
                        act.wait_ge(w.used, U_OUT)
                        act.activation(abT[0][:, 2 * j:2 * j + 2, :], yF[:, 2 * j:2 * j + 2, :], ACT.Copy)\
                           .then_inc(sem["yT_hi"], 1)
                    w.hi_through(act, U_FFN + 0)
                    layer_norm_scalar(act, stats, eps_ln, norm1)
                    act.preload_act_table_set("silu_and_others")
                    transposed_scalar(act, ps, xT[0], norm1)
                    ffn_scalar(act, w, U_FFN, up_ps, gate, h, hT[0], norm2, 1)
                    layer_norm_scalar(act, stats, eps_ln, norm2)
                    transposed_scalar(act, ps, xT[0], norm2)

                @block.gpsimd
                def _(pool):
                    pool.memset(eps_ln, LN_EPS).then_inc(sem["masks"], 1)
                    pool.memset(eps_rms, RMS_EPS).then_inc(sem["masks"], 1)
                    pool.memset(one, 1.0).then_inc(sem["masks"], 1)
                    pool.memset(va[:, :, :, A_DV:A_DV + 1], 1.0).then_inc(sem["masks"], 1)
                    pool.memset(zero[:, :].bitcast(F32), 0.0).then_inc(sem["masks"], 1)
                    pool.wait_ge(sem["masks"], 5)
                    pool.memset(cv[:, :, :, 0:3], 0.0).then_inc(sem["cv_zero"], 1)
                    pool.wait_ge(sem["cv_zero"], 1)

                @block.vector
                def _(dve):
                    chain = Chain(dve, steps["vector"])

                    def heads(v, g):
                        return v[:, 4 * g:4 * g + 4].unsqueeze(2).broadcast_to([P, 4, P])

                    def over_heads(m, n=4):
                        return m.unsqueeze(1).broadcast_to([P, n, P])

                    def bank(b):
                        return ps[:, b, :].rearrange("p (h t) -> p h t", t=P)

                    for u in range(QKV_UNITS):
                        w.lo_through(dve, u + 2)
                        dve.wait_ge(sem["tap0_done"], 2 * u + 2)
                        for j in range(1, 4):
                            for k in range(2):
                                ins = dve.scalar_tensor_tensor(ca[:, u % 2, k, :], cv[:, u % 2, k, j:j + S],
                                                               conv_w[:, 2 * u + k, j:j + 1], ca[:, u % 2, k, :],
                                                               ALU.mult, ALU.add)
                                if j == 3 and k == 1:
                                    ins.then_inc(sem["conv_done"], 1)
                                else:
                                    chain.step(ins)
                            if j < 3:
                                chain.settle()
                        if u == 1:
                            dve.wait_ge(sem["gate_w_hi"], 1)
                            dve.tensor_tensor(wg[1][:, :, :].rearrange("p a b -> p (a b)"), wg_raw,
                                              wg[0][:, :, :].rearrange("p a b -> p (a b)").bitcast(F32),
                                              ALU.subtract).then_inc(sem["gate_w"], 1)
                    w.lo_through(dve, QKV_UNITS + 3)

                    dve.wait_ge(sem["gates_mm"], 1)
                    dve.tensor_tensor(g24, gates_ps, gate_bias.unsqueeze(1).broadcast_to([P, TT, N_GATES]), ALU.add)\
                       .then_inc(sem["g24"], 1)
                    dve.wait_ge(sem["g24"], 1)
                    dve.tensor_copy(z[:, :, 4:12], g24[:, :, 16:24]).then_inc(sem["z_ready"], 1)
                    dve.wait_ge(sem["tanh_done"], 2)
                    chain.step(dve.tensor_scalar(li, t8[:, :, 0:4], CAP, None, ALU.mult))
                    dve.tensor_scalar(z[:, :, 0:4], t8[:, :, 4:8], -CAP, None, ALU.mult).then_inc(sem["z_ready"], 1)
                    dve.wait_ge(sem["ln_done"], 2)
                    dve.wait_ge(sem["z_ready"], 2)
                    chain.step(dve.scalar_tensor_tensor(sp, z, 0.0, zabs, ALU.max, ALU.add))
                    chain.settle()
                    dve.tensor_scalar(gs[:, :, 0:4], sp[:, :, 0:4], -1.0, None, ALU.mult).then_inc(sem["decays"], 1)
                    dve.scalar_tensor_tensor(gs[:, :, 4:12], sp[:, :, 4:12], -1.0,
                                             e_alog.unsqueeze(1).broadcast_to([P, TT, B_HEADS]), ALU.mult,
                                             ALU.mult).then_inc(sem["decays"], 1)
                    w.lo_through(dve, U_VA + 1)
                    dve.wait_ge(sem["cum_mm"], 1)
                    chain.step(dve.tensor_copy(cs, cum_ps[:, 0]))
                    chain.step(dve.tensor_copy(tot, cum_ps[:, 1]))
                    dve.wait_ge(sem["ss_mm"], 8)
                    dve.tensor_copy(ssq, ss_ps).then_inc(sem["cums"], 1)
                    chain.settle()
                    dve.tensor_tensor(cs[:, 1, 0:4], cs[:, 1, 0:4], tot[:, 0, 0:4], ALU.add).then_inc(sem["cums"], 1)
                    dve.tensor_tensor(kdf, tot[:, :, 4:12], cs[:, :, 4:12], ALU.subtract).then_inc(sem["cums"], 1)
                    dve.wait_ge(sem["cums"], 3)
                    dve.tensor_tensor(a_col, li, cs[:, :, 0:4], ALU.subtract).then_inc(sem["a_ready"], 1)
                    dve.wait_ge(sem["exps"], 2)
                    dve.wait_ge(sem["norms"], 1)
                    chain.step(dve.reciprocal(rnrm, nrm))
                    chain.step(dve.tensor_scalar(neg_eg, eg, -1.0, None, ALU.mult))
                    chain.settle()
                    rk = rnrm[:, :, 8:16]
                    chain.step(dve.tensor_tensor(kdf, kdf, rk, ALU.mult))
                    chain.step(dve.tensor_tensor(brk, beta, rk, ALU.mult))
                    chain.step(dve.tensor_scalar(rq, rnrm[:, :, 0:8], B_DK ** -0.5, None, ALU.mult))
                    chain.settle()
                    chain.step(dve.tensor_tensor(cj, brk, rk, ALU.mult))
                    w.lo_through(dve, U_VA + 2)
                    dve.wait_ge(sem["a_rows_mm"], 1)
                    chain.step(dve.tensor_copy(rows[:, 0, :], arow_ps))
                    chain.settle()
                    dve.tensor_tensor_scan(rows[:, 1, :], rows[:, 0, :], rows[:, 0, :], 0.0, ALU.max, ALU.max)\
                       .then_inc(sem["m_rows"], 1)
                    w.lo_through(dve, U_VA + 3)
                    dve.wait_ge(sem["m_cols_mm"], 1)
                    dve.tensor_tensor(m_col, mcol_ps, cs[:, :, 0:4], ALU.add).then_inc(sem["m_ready"], 1)

                    for t in range(TT):
                        for g in range(2):
                            dve.wait_ge(sem["v_mm"], 2 * t + g + 1)
                            dve.tensor_tensor(hb[:, t, 4 * g:4 * g + 4, :], bank(token_banks[t][g]), heads(nrm[:, t, 8:16], g),
                                              ALU.mult).then_inc(sem["v_done"], 1)
                    for g in range(2):
                        dve.wait_ge(sem["k_mm"], g + 1)
                        dve.tensor_tensor(k_tm[:, 4 * g:4 * g + 4, :], bank(6 + g), heads(kdf[:, 0, :], g),
                                          ALU.mult).then_inc(sem["k_done"], 1)

                    for c in range(2):
                        for g in range(2):
                            dve.wait_ge(sem["gb_mm"], 2 * c + g + 1)
                            for i in range(4):
                                hd = 4 * g + i
                                dve.tensor_scalar(PB[:, hd, :], bank(4 + g)[:, i, :], cs[:, c, 4 + hd:5 + hd], 0.0,
                                                  ALU.subtract, ALU.min).then_inc(sem["diff"], 1)
                        dve.wait_ge(sem["dec_exp"], c + 1)
                        chain.step(dve.tensor_tensor(PB[:, :, :], PB[:, :, :], over_heads(tri, 8), ALU.mult))
                        chain.settle()
                        for g in range(2):
                            dve.wait_ge(sem["kkqk_mm"], 2 * c + g + 1)
                            for i in range(4):
                                hd = 4 * g + i
                                chain.step(dve.scalar_tensor_tensor(AT[:, hd, :], bank(g)[:, i, :], cj[:, c, hd:hd + 1],
                                                                    PB[:, hd, :], ALU.mult, ALU.mult))
                                chain.step(dve.scalar_tensor_tensor(attn[:, hd, :], bank(2 + g)[:, i, :],
                                                                    rk[:, c, hd:hd + 1], PB[:, hd, :], ALU.mult, ALU.mult))
                        chain.settle()
                        dve.tensor_tensor(AT[:, :, :], AT[:, :, :], over_heads(strict, 8), ALU.mult).then_inc(sem["a_done"], 1)
                        dve.wait_ge(sem["a_done"], c + 1)
                        chain.step(dve.tensor_tensor(XT[:, :, :], AT[:, :, :], over_heads(level0, 8), ALU.mult))
                        chain.settle()
                        dve.tensor_tensor(XT[:, :, :], over_heads(ident, 8), XT[:, :, :], ALU.subtract).then_inc(sem["xt_init"], 1)
                        for g in range(2):
                            dve.wait_ge(sem["x_mm"], 2 * c + g + 1)
                            dve.tensor_copy(X[:, 4 * g:4 * g + 4, :], bank(g)).then_inc(sem["x_init"], 1)
                        dve.wait_ge(sem["x_init"], 2 * c + 2)
                        for lv in range(6):
                            n = 2 * (6 * c + lv)
                            for g in range(2):
                                dve.wait_ge(sem["p_mm"], n + g + 1)
                                dve.tensor_tensor(PB[:, 4 * g:4 * g + 4, :], bank(g), over_heads(levels[lv]), ALU.mult)\
                                   .then_inc(sem["p_done"], 1)
                            if 6 * c + lv < 10:
                                w.lo_half(dve, lv % 2)
                            for g in range(2):
                                hs = slice(4 * g, 4 * g + 4)
                                if lv < 5:
                                    dve.wait_ge(sem["y_mm"], 22 * c + 4 * lv + 2 * g + 1)
                                    dve.tensor_tensor(X[:, hs, :], X[:, hs, :], bank(2 + 2 * g), ALU.subtract)\
                                       .then_inc(sem["y_done"], 1)
                                dve.wait_ge(sem["y_mm"], 22 * c + 4 * lv + (2 * g + 2 if lv < 5 else g + 1))
                                dve.tensor_tensor(XT[:, hs, :], XT[:, hs, :], bank(3 + 2 * g), ALU.subtract)\
                                   .then_inc(sem["y_done"], 1)
                            dve.wait_ge(sem["y_done"], 22 * c + 4 * lv + (4 if lv < 5 else 2))
                        for g in range(2):
                            hs = slice(4 * g, 4 * g + 4)
                            if c == 1:
                                dve.wait_ge(sem["ks_mm"], g + 1)
                                chain.step(dve.tensor_tensor(PB[:, hs, :], bank(g), heads(neg_eg[:, 1, :], g), ALU.mult))
                                chain.step(dve.tensor_tensor(AT[:, hs, :], bank(6 + g), heads(eg[:, 1, :], g), ALU.mult))
                                chain.settle()
                                dve.tensor_tensor(PB[:, hs, :], PB[:, hs, :], hb[:, 1, hs, :], ALU.add).then_inc(sem["rhs_done"], 1)
                            dve.wait_ge(sem["vn_mm"], 2 * c + g + 1)
                            dve.tensor_tensor(X[:, hs, :], bank(2 + g), heads(brk[:, c, :], g), ALU.mult).then_inc(sem["vn_done"], 1)
                        for g in range(2):
                            hs = slice(4 * g, 4 * g + 4)
                            dve.wait_ge(sem["o_mm"], 2 * c + g + 1)
                            if c == 1:
                                chain.step(dve.tensor_tensor(AT[:, hs, :], AT[:, hs, :], bank(2 + g), ALU.add))
                                chain.settle()
                                dve.tensor_tensor(hb[:, c, hs, :], AT[:, hs, :], heads(rq[:, c, :], g), ALU.mult)\
                                   .then_inc(sem["o_done"], 1)
                            else:
                                dve.tensor_tensor(hb[:, c, hs, :], bank(2 + g), heads(rq[:, c, :], g), ALU.mult)\
                                   .then_inc(sem["o_done"], 1)
                    def head_weights(hd):
                        dve.wait_ge(sem["kq_mm"], hd + 1)
                        if hd >= 2:
                            dve.wait_ge(sem["num_mm"], 2 * hd - 2)
                        dve.tensor_scalar(mw[:, hd % 2, 0:S], ps[:, 5, 0:S], a_col[:, 0, hd:hd + 1], 0.0,
                                          ALU.subtract, ALU.max).then_inc(sem["w_diff"], 1)
                        dve.tensor_scalar(mw[:, hd % 2, S:384], ps[:, 5, P:S], a_col[:, 1, hd:hd + 1], 0.0,
                                          ALU.subtract, ALU.max).then_inc(sem["w_diff"], 1)
                        dve.wait_ge(sem["w_exp"], hd + 1)
                        chain.step(dve.scalar_tensor_tensor(mst[:, hd % 2, :], ps[:, 4, 0:384], A_DK ** -0.5,
                                                            mw[:, hd % 2, :], ALU.mult, ALU.mult))
                        chain.settle()
                        for b in range(2):
                            blk = mst[:, hd % 2, 2 * b * P:(2 * b + 1) * P]
                            dve.tensor_tensor(blk, blk, tri, ALU.mult).then_inc(sem["s_done2"], 1)

                    def head_sums(hd):
                        dve.wait_ge(sem["num_mm"], 2 * hd + 2)
                        chain.step(dve.tensor_copy(den[:, :, hd:hd + 1], ps[:, 6:8, A_DV:A_DV + 1]))
                        chain.settle()
                        chain.step(dve.scalar_tensor_tensor(rs4[:, :, hd:hd + 1], den[:, :, hd:hd + 1], -1.0,
                                                            den[:, :, hd:hd + 1], ALU.mult, ALU.max))
                        chain.settle()
                        chain.step(dve.tensor_tensor(rs4[:, :, hd:hd + 1], rs4[:, :, hd:hd + 1], emt[:, :, hd:hd + 1],
                                                     ALU.max))
                        chain.settle()
                        chain.step(dve.reciprocal(den[:, :, hd:hd + 1], rs4[:, :, hd:hd + 1]))
                        chain.settle()
                        for t in range(TT):
                            dve.tensor_scalar(va[:, t, hd, 0:A_DV], ps[:, 6 + t, 0:A_DV], den[:, t, hd:hd + 1], None,
                                              ALU.mult).then_inc(sem["num_done"], 1)

                    dve.wait_ge(sem["emt"], 1)
                    head_weights(0)
                    for hd in range(A_HEADS):
                        if hd < A_HEADS - 1:
                            head_weights(hd + 1)
                        head_sums(hd)
                        if hd < TT:
                            dve.wait_ge(sem["hb_sq"], hd + 1)
                            dve.tensor_reduce(rs8[:, hd, :], (ST8 if hd else PB)[:, :, :], AX.X, ALU.add)\
                               .then_inc(sem["hb_sums"], 1)
                        w.lo_through(dve, U_ZB + 1 + hd)
                    dve.wait_ge(sem["gain_loaded"], 16)
                    dve.wait_ge(sem["ha_std"], 1)
                    chain.step(dve.reciprocal(rs4, rs4))
                    chain.settle()
                    for hd in range(A_HEADS):
                        for t in range(TT):
                            v = va[:, t, hd, 0:A_DV]
                            dve.scalar_tensor_tensor(v, v, rs4[:, t, hd:hd + 1], g_mlstm[:, hd * A_DV:(hd + 1) * A_DV],
                                                     ALU.mult, ALU.mult).then_inc(sem["ha_done"], 1)
                    w.lo_through(dve, U_BA + 1)

                    def gated_rows(i, before):
                        dve.wait_ge(sem["hT_mm"], before + i + 1)
                        dve.wait_ge(sem["og_done"], before + i + 1)
                        if before:
                            dve.scalar_tensor_tensor(abF[:, i, :], ps[:, 4 + i, :], g_gdn, gates_b[:, i, :], ALU.mult,
                                                     ALU.mult).then_inc(sem["abF"], 1)
                        else:
                            dve.tensor_tensor(abF[:, i, :], ps[:, 4 + i, :], gates_a[:, i, :], ALU.mult)\
                               .then_inc(sem["abF"], 1)

                    def gated_low(i, before):
                        dve.wait_ge(sem["ab_hi"], before + i + 1)
                        part = [v[:, 2 * i:2 * i + 2, :].rearrange("p a b -> p (a b)") for v in abT]
                        dve.tensor_tensor(part[1], abF[:, i, :], part[0].bitcast(F32), ALU.subtract)\
                           .then_inc(sem["ab_done"], 1)

                    def branch(u0, before):
                        for i in range(KT):
                            w.lo_through(dve, u0 + i + 2)
                            n = before + i
                            if before == 0 and i in (1, 2):
                                t = i - 1
                                dve.tensor_tensor(hb[:, t], hb[:, t], rs8[:, t, :].unsqueeze(2).broadcast_to([P, 8, P]),
                                                  ALU.mult).then_inc(sem["hb_done"], 1)
                            dve.wait_ge(sem["sg_done"], n + 1)
                            if before == 0:
                                dve.tensor_tensor(yF[:, i, :], sg[:, n % 2, :], ps[:, i % 4, S:2 * S], ALU.mult)\
                                   .then_inc(sem["yp_done"], 1)
                                if i == KT - 2:
                                    for j in range(4):
                                        gated_rows(j, 4)
                            else:
                                chain.step(dve.tensor_tensor(sg[:, n % 2, :], sg[:, n % 2, :], ps[:, i % 4, S:2 * S], ALU.mult))
                                chain.settle()
                                dve.tensor_tensor(yF[:, i, :], yF[:, i, :], sg[:, n % 2, :], ALU.add).then_inc(sem["yp_done"], 1)

                    gated_rows(0, 0)
                    for i in range(4):
                        if i < 3:
                            gated_rows(i + 1, 0)
                        gated_low(i, 0)
                    w.lo_through(dve, U_BA + 2)
                    dve.wait_ge(sem["hb_std"], 1)
                    chain.step(dve.reciprocal(rs8, rs8))
                    chain.settle()
                    branch(U_BA, 0)
                    for i in range(4):
                        gated_low(i, 4)
                    branch(U_BB, KT)
                    for j in range(4):
                        dve.wait_ge(sem["yT_hi"], j + 1)
                        part = slice(2 * j, 2 * j + 2)
                        dve.tensor_tensor(abT[1][:, part, :], yF[:, part, :], abT[0][:, part, :].bitcast(F32), ALU.subtract)\
                           .then_inc(sem["yT_done"], 1)
                    w.lo_through(dve, U_FFN)
                    layer_norm_vector(dve, chain, w, U_FFN, x, acc, ln_gain, ln_shift, stats, norm1)
                    transposed_vector(dve, ps, xT, norm1)
                    ffn_vector(dve, w, U_FFN, up_ps, gate, h, hT, norm2, 1)
                    layer_norm_vector(dve, chain, w, U_FFN + FFN_UNITS, x, acc, ln_gain, ln_shift, stats, norm2)
                    transposed_vector(dve, ps, xT, norm2)

                @block.tensor
                def _(pe):
                    def tiles(u, bank, rhs, ab_before=None):
                        w.wait_parts(pe, w.lo_done, u)
                        for j in range(2):
                            for k in range(KT):
                                if j == 1 and ab_before is not None:
                                    pe.wait_ge(sem["ab_done"], ab_before + k // 2 + 1)
                                mm = split_matmul(pe, ps[:, bank, j * S:(j + 1) * S], w.pair(u, (16, P), j * KT + k, slice(None)),
                                                  (rhs[j][0][:, k, :], rhs[j][1][:, k, :]), k == 0, k == KT - 1)
                        mm.then_inc(w.used, 1)

                    def half_group(u, half, t, bank, lhs):
                        w.wait_parts(pe, w.lo_done, u + half)
                        for k in range(4):
                            kk = 4 * half + k
                            mm = split_matmul(pe, ps[:, bank, :],
                                              (lhs[0][:, kk, t * P:(t + 1) * P], lhs[1][:, kk, t * P:(t + 1) * P]),
                                              w.pair(u + half, (4, 512), k, slice(None)), kk == 0, kk == KT - 1)
                        return mm

                    def group(u, banks, lhs, between=None):
                        for half in range(2):
                            if half and between:
                                between()
                            for t in range(TT):
                                mm = half_group(u, half, t, banks[t], lhs)
                            mm.then_inc(w.used, 1)

                    def group_by_tile(u, banks, lhs, tile_done):
                        for t in range(TT):
                            for half in range(2):
                                mm = half_group(u, half, t, banks[t], lhs)
                                if t == TT - 1:
                                    mm.then_inc(w.used, 1)
                            if t == 0:
                                mm.then_inc(tile_done, 1)

                    def sum_squares(u):
                        pe.wait_ge(sem["sq_done"], u + 1)
                        for k in range(2):
                            for t in range(TT):
                                mm = pe.matmul(ss_ps[:, t, 2 * u + k:2 * u + k + 1], sq[:, u % 2, k, t * P:(t + 1) * P],
                                               ones[:, 0:1], start=True, stop=True)
                        mm.then_inc(sem["ss_mm"], 1)

                    for u in range(QKV_UNITS):
                        if u >= 4:
                            pe.wait_ge(sem["cv_copied"], u - 3)
                        tiles(u, u % 4, (xT, xT))
                        if u == 3:
                            pe.wait_ge(sem["gate_w"], 1)
                            for k in range(KT):
                                mm = split_matmul(pe, gate_rows_ps, (wg[0][:, k, :], wg[1][:, k, :]),
                                                  (xT[0][:, k, :], xT[1][:, k, :]), k == 0, k == KT - 1)
                            mm.then_inc(sem["gate_rows_mm"], 1)
                        if u == 5:
                            pe.wait_ge(sem["gate_rows"], 1)
                            for t in range(TT):
                                mm = pe.transpose(gates_ps[:, t, :], gate_rows[:, t * P:(t + 1) * P],
                                                  ident[0:N_GATES, 0:N_GATES])
                            mm.then_inc(sem["gates_mm"], 1)
                        if 2 <= u < 10:
                            sum_squares(u - 2)
                    for i in range(QKA_UNITS):
                        pe.wait_ge(sem["cv_copied"], QKV_UNITS - 3 + i)
                        tiles(U_QKA + i, i, (xT, xT))

                    pe.wait_ge(sem["decays"], 2)
                    for t in range(TT):
                        pe.matmul(cum_ps[:, 0, t, :], tri, gs[:, t, :], start=True, stop=True)
                        mm = pe.matmul(cum_ps[:, 1, t, :], ones, gs[:, t, :], start=True, stop=True)
                    mm.then_inc(sem["cum_mm"], 1)

                    def input_gate_rows():
                        pe.wait_ge(sem["a_ready"], 1)
                        for t in range(TT):
                            mm = pe.transpose(arow_ps[:, t * P:(t + 1) * P], a_col[:, t, :], ident)
                        mm.then_inc(sem["a_rows_mm"], 1)

                    def by_tokens(first, t, g, mm_sem):
                        for i in range(4):
                            mm = pe.transpose(ps[:, token_banks[t][g], i * P:(i + 1) * P],
                                              qkvT[:, first + 4 * g + i, t * P:(t + 1) * P], ident)
                        mm.then_inc(sem[mm_sem], 1)

                    group(U_VA, (4, 5), xT, between=input_gate_rows)
                    pe.wait_ge(sem["silu_done"], QKV_UNITS)
                    by_tokens(16, 0, 0, "v_mm")
                    pe.wait_ge(sem["m_rows"], 1)
                    for t in range(TT):
                        mm = pe.transpose(mcol_ps[:, t, :], rows[:, 1, t * P:(t + 1) * P], ident[0:A_HEADS, 0:A_HEADS])
                    mm.then_inc(sem["m_cols_mm"], 1)
                    pe.wait_ge(sem["m_ready"], 1)
                    by_tokens(16, 0, 1, "v_mm")
                    for g in range(2):
                        pe.wait_ge(sem["va_done"], g + 1)
                        by_tokens(16, 1, g, "v_mm")
                    for g in range(2):
                        pe.wait_ge(sem["v_done"], g + 1)
                        by_tokens(8, 0, g, "k_mm")

                    def by_heads(b, g, lhs, rhs, inc=None):
                        for i in range(4):
                            mm = pe.matmul(ps[:, b, i * P:(i + 1) * P], lhs(4 * g + i), rhs(4 * g + i), start=True, stop=True)
                        if inc:
                            mm.then_inc(sem[inc], 1)

                    def scores(hd):
                        q, k = qkvT[:, 16 + hd, :], qkvT[:, 20 + hd, :]
                        if hd:
                            pe.wait_ge(sem["s_done2"], 2 * hd)
                        pe.matmul(ps[:, 4, 0:S], k[:, 0:P], q, start=True, stop=True)
                        pe.matmul(ps[:, 4, S:384], k[:, P:S], q[:, P:S], start=True, stop=True)
                        pe.matmul(ps[:, 5, 0:S], sel[:, hd, :], rows[:, 1, :], start=True, stop=True).then_inc(sem["kq_mm"], 1)

                    def sums(hd):
                        pe.wait_ge(sem["s_done2"], 2 * hd + 2)
                        if hd == 0:
                            pe.wait_ge(sem["o_done"], 4)
                        else:
                            pe.wait_ge(sem["num_done"], 2 * hd)
                        m = mst[:, hd % 2, :]
                        pe.matmul(ps[:, 6, 0:A_DV + 1], m[:, 0:P], va[:, 0, hd, :], start=True, stop=True).then_inc(sem["num_mm"], 1)
                        pe.matmul(ps[:, 7, 0:A_DV + 1], m[:, P:S], va[:, 0, hd, :], start=True, stop=False)
                        pe.matmul(ps[:, 7, 0:A_DV + 1], m[:, S:384], va[:, 1, hd, :], start=False, stop=True).then_inc(sem["num_mm"], 1)

                    pe.wait_ge(sem["v_done"], 4)
                    for c in range(2):
                        tok = slice(c * P, (c + 1) * P)
                        if c == 1:
                            pe.wait_ge(sem["s_done"], 2)
                        for g in range(2):
                            by_heads(4 + g, g, lambda hd: gs[:, c, 4 + hd:5 + hd].broadcast_to([P, P]), lambda hd: tri, "gb_mm")
                        if c == 0:
                            pe.wait_ge(sem["qka_done"], 4)
                        for g in range(2):
                            by_heads(g, g, lambda hd: qkvT[:, 8 + hd, tok], lambda hd: qkvT[:, 8 + hd, tok])
                            if c == 1:
                                pe.wait_ge(sem["o_done"], g + 1)
                            by_heads(2 + g, g, lambda hd: qkvT[:, 8 + hd, tok], lambda hd: qkvT[:, hd, tok], "kkqk_mm")
                        if c == 0:
                            pe.wait_ge(sem["k_done"], 2)
                            group(U_VA + 2, (6, 7), xT)
                        else:
                            pe.wait_ge(sem["va_done"], 4)
                            for i in range(2):
                                tiles(U_OA + i, 6 + i, (xT, xT))
                        pe.wait_ge(sem["xt_init"], c + 1)
                        for g in range(2):
                            for i in range(4):
                                mm = pe.transpose(ps[:, g, i * P:(i + 1) * P], XT[:, 4 * g + i, :], ident)
                            mm.then_inc(sem["x_mm"], 1)
                        for lv in range(6):
                            for g in range(2):
                                if lv == 0:
                                    pe.wait_ge(sem["x_init"], 2 * c + g + 1)
                                else:
                                    pe.wait_ge(sem["y_done"], 22 * c + 4 * (lv - 1) + 2 * g + 1)
                                by_heads(g, g, lambda hd: AT[:, hd, :], lambda hd: X[:, hd, :], "p_mm")
                            for g in range(2):
                                pe.wait_ge(sem["p_done"], 2 * (6 * c + lv) + g + 1)
                                if lv:
                                    pe.wait_ge(sem["y_done"], 22 * c + 4 * (lv - 1) + 2 * g + 2)
                                if lv < 5:
                                    by_heads(2 + 2 * g, g, lambda hd: XT[:, hd, :], lambda hd: PB[:, hd, :], "y_mm")
                                by_heads(3 + 2 * g, g, lambda hd: PB[:, hd, :], lambda hd: XT[:, hd, :], "y_mm")
                        pe.wait_ge(sem["y_done"], 22 * (c + 1))
                        if c == 1:
                            for g in range(2):
                                pe.wait_ge(sem["og_done"], g + 1)
                                by_heads(g, g, lambda hd: qkvT[:, 8 + hd, tok], lambda hd: ST8[:, hd, :])
                                by_heads(6 + g, g, lambda hd: qkvT[:, hd, tok], lambda hd: ST8[:, hd, :], "ks_mm")
                            scores(0)
                        for g in range(2):
                            if c == 1:
                                pe.wait_ge(sem["rhs_done"], g + 1)
                            by_heads(2 + g, g, lambda hd: XT[:, hd, :],
                                     (lambda hd: PB[:, hd, :]) if c else (lambda hd: hb[:, 0, hd, :]), "vn_mm")
                        if c == 1:
                            tiles(U_OA + 2, 0, (xT, xT))
                        for g in range(2):
                            pe.wait_ge(sem["vn_done"], 2 * c + g + 1)
                            by_heads(2 + g, g, lambda hd: attn[:, hd, :], lambda hd: X[:, hd, :], "o_mm")
                            if c == 0:
                                by_heads(4 + g, g, lambda hd: k_tm[:, hd, :], lambda hd: X[:, hd, :], "s_mm")

                    def head_tiles(i, src):
                        for k in range(2):
                            for t in range(TT):
                                mm = pe.transpose(ps[:, 4 + i, k * S + t * P:k * S + (t + 1) * P], src(t, 2 * i + k), ident)
                        mm.then_inc(sem["hT_mm"], 1)

                    for hd in range(A_HEADS):
                        if hd == 1:
                            pe.wait_ge(sem["o_done"], 4)
                        if hd == 3:
                            pe.wait_ge(sem["og_done"], 3)
                        tiles(U_OA + 3 + hd, (hd + 1) % 4, (xT, xT))
                        if hd < A_HEADS - 1:
                            scores(hd + 1)
                        sums(hd)
                    pe.wait_ge(sem["og_done"], 4)
                    tiles(U_ZB + 3, 1, (xT, xT))
                    for i in range(4):
                        pe.wait_ge(sem["ha_done"], 2 * i + 2)
                        head_tiles(i, lambda t, k: va[:, t, k // 2, (k % 2) * P:(k % 2 + 1) * P])
                    for i in range(KT):
                        pe.wait_ge(*((sem["og_done"], (7, 8, 7, 8)[i]) if i < 4 else (sem["yp_done"], i - 3)))
                        tiles(U_BA + i, i % 4, (xT, abT), 0 if i == 0 else None)
                        if i == 5:
                            pe.wait_ge(sem["hb_done"], 2)
                            pe.wait_ge(sem["abF"], 4)
                            for j in range(4):
                                head_tiles(j, lambda t, k: hb[:, t, k, :])
                    for i in range(KT):
                        pe.wait_ge(sem["yp_done"], KT + i - 3)
                        tiles(U_BB + i, i % 4, (xT, abT), 4 if i == 0 else None)
                    pe.wait_ge(sem["yp_done"], 2 * KT)
                    pe.wait_ge(sem["yT_done"], 4)
                    group(U_OUT, (0, 2), abT)
                    group_by_tile(U_OUT + 2, (1, 3), abT, norm1["acc_done"])
                    norm_transposes(pe, ps, x, ident, norm1["x_normed"], (1, 2), norm1)
                    ffn_tensor(pe, w, U_FFN, xT, hT, acc, up_ps, zero, norm2, norm1["xT_ready"], False)
                    norm_transposes(pe, ps, x, ident, norm2["x_normed"], (1, 2), norm2)

            end_stage(nc, [*w.sems(), *sem.values(), *norm1.values(), *norm2.values(), *steps.values()])


HD = 64
FOX_HEADS, SB_HEADS = 8, 16
D_RNN = 512
RG_C = 8.0
RNN_UNITS, FOX_QKV_UNITS, HY_OUT_UNITS = 4, 6, 4
SB_QK_UNITS, SB_V_UNITS, SB_OUT_UNITS = 8, 4, 4
RMS_SEMS = ["sq_done", "sq1_done", "std_done", "x_normed", "xT_mm", "xT_hi_done", "xT_ready", "gain_cols", "acc_done"]


def rms_scalar(act, x, junk, ss, std, eps, ps, gain, xT_hi, sem):
    act.preload_act_table_set("sqrt_and_others")
    act.activation(junk, x[:, 0, :], ACT.Square, accum_out=ss[:, 0:1]).then_inc(sem["sq_done"], 1)
    act.wait_ge(sem["sq_done"], 1)
    act.activation(std[:, 0:1], ss[:, 0:1], ACT.Sqrt, bias=eps, scale=1.0 / D).then_inc(sem["std_done"], 1)
    act.wait_ge(sem["sq1_done"], 1)
    act.activation(std[:, 1:2], ss[:, 1:2], ACT.Sqrt, bias=eps, scale=1.0 / D).then_inc(sem["std_done"], 1)
    act.wait_ge(sem["gain_cols"], 16)
    for k in range(KT):
        act.wait_ge(sem["xT_mm"], k // 2 + 1)
        act.activation(xT_hi[:, k, :], ps[:, 4 + k // 2, (k % 2) * S:(k % 2 + 1) * S], ACT.Copy,
                       scale=gain[:, k:k + 1]).then_inc(sem["xT_hi_done"], 1)


def rms_vector(dve, chain, x, xn, ss, std, ps, gain, xT, sem):
    dve.tensor_tensor_reduce(xn[:, 1, :], x[:, 1, :], x[:, 1, :], 1.0, 0.0, ALU.mult, ALU.add, ss[:, 1:2])\
       .then_inc(sem["sq1_done"], 1)
    for t in range(TT):
        dve.wait_ge(sem["std_done"], t + 1)
        chain.step(dve.reciprocal(std[:, t:t + 1], std[:, t:t + 1]))
        chain.settle()
        if t:
            dve.wait_ge(sem["sq1_done"], 1)
        dve.tensor_scalar(xn[:, t, :], x[:, t, :], std[:, t:t + 1], None, ALU.mult).then_inc(sem["x_normed"], 1)
    for k in range(KT):
        dve.wait_ge(sem["xT_hi_done"], 2 * (k // 2) + 2)
        dve.scalar_tensor_tensor(xT[1][:, k, :], ps[:, 4 + k // 2, (k % 2) * S:(k % 2 + 1) * S], gain[:, k:k + 1],
                                 xT[0][:, k, :].bitcast(F32), ALU.mult, ALU.subtract).then_inc(sem["xT_ready"], 1)


def add_to_x(dve, w, units, x, acc, factor, sem, by_tile=False):
    for t in range(TT):
        if by_tile and t == 0:
            dve.wait_ge(sem["acc_done"], 1)
        else:
            dve.wait_ge(w.used, units)
        for half in range(2):
            cols = slice(half * 512, (half + 1) * 512)
            dve.scalar_tensor_tensor(x[:, t, cols], acc[:, 2 * t + half, :], factor, x[:, t, cols],
                                     ALU.mult, ALU.add).then_inc(sem["x_added"], 1)


class Parts:
    pass


def split_tiles(pe, w, ps, u, bank, rhs, ready=None):
    w.wait_parts(pe, w.lo_done, u)
    for j in range(2):
        for k in range(KT):
            if ready and j == 0:
                pe.wait_ge(ready, k + 1)
            mm = split_matmul(pe, ps[:, bank, j * S:(j + 1) * S], w.pair(u, (16, P), j * KT + k, slice(None)),
                              (rhs[0][:, k, :], rhs[1][:, k, :]), k == 0, k == KT - 1)
    mm.then_inc(w.used, 1)


def split_group(pe, w, ps, u, banks, lhs):
    for half in range(2):
        w.wait_parts(pe, w.lo_done, u + half)
        for t in range(TT):
            for k in range(4):
                kk = 4 * half + k
                mm = split_matmul(pe, ps[:, banks[t], :],
                                  (lhs[0][:, kk, t * P:(t + 1) * P], lhs[1][:, kk, t * P:(t + 1) * P]),
                                  w.pair(u + half, (4, 512), k, slice(None)), kk == 0, kk == KT - 1)
        mm.then_inc(w.used, 1)


def end_stage(nc, sems):
    numbers = sorted(s.num for s in sems)
    first = numbers[0]
    for n, after in zip(numbers, [*numbers[1:], None]):
        if after != n + 1:
            nc.sync.sem_clear(range(first, n + 1))
            first = after
    nc.all_engine_barrier()


def ffn_stage(nc, p, a, n, name, u0, last=False):
    with ExitStack() as ctx:
        w = p.w
        ahead = 0 if last else 1
        sem = {s: ctx.enter_context(nc.semaphore(f"{name}_{s}")) for s in
               dict.fromkeys(RMS_SEMS + FFN_SEMS + ["x_added", "scalar_steps", "vector_steps"])}
        with nc.Block() as block:
            @block.sync
            def _(sp):
                sp.dma_start(p.gain[:, :], a["ffn_norm_2"][n]).then_inc(sem["gain_cols"], 16)
                ffn_load(sp, w, u0,
                         lambda pair, f: a["up"][DEPTH + n, bass.ds(pair, 1) if not isinstance(pair, int) else slice(pair, pair + 1), f]
                         .rearrange("a p n -> (a p) n"),
                         lambda pair: a["dn"][DEPTH + n, bass.ds(pair, 1) if not isinstance(pair, int) else slice(pair, pair + 1)]
                         .rearrange("a p n -> (a p) n"), first=RING)
                if not last:
                    p.load_first(sp, u0 + FFN_UNITS)

            @block.scalar
            def _(act):
                rms_scalar(act, p.x, p.junk, p.ss, p.std, p.eps, p.ps, p.gain, p.xT[0], sem)
                act.preload_act_table_set("silu_and_others")
                ffn_scalar(act, w, u0, p.up_ps, p.gate, p.h, p.hT[0], sem, ahead)

            @block.vector
            def _(dve):
                rms_vector(dve, Chain(dve, sem["vector_steps"]), p.x, p.xn, p.ss, p.std, p.ps, p.gain, p.xT, sem)
                ffn_vector(dve, w, u0, p.up_ps, p.gate, p.h, p.hT, sem, ahead)
                add_to_x(dve, w, u0 + FFN_UNITS, p.x, p.acc, 0.5, sem, by_tile=True)

            @block.tensor
            def _(pe):
                norm_transposes(pe, p.ps, p.xn, p.ident, sem["x_normed"], (1, 2), sem)
                ffn_tensor(pe, w, u0, p.xT, p.hT, p.acc, p.up_ps, p.zero, sem, sem["xT_ready"], True)
        end_stage(nc, sem.values())


def heads_out(pe, p, hd, bank, v, weights, first_wait=None):
    rows = slice(HD * (hd % 2), HD * (hd % 2) + HD)
    cols = slice(HD * hd, HD * (hd + 1))
    pe.matmul(p.ps[rows, bank, 0:S], v[:, 0, cols], weights[:, 0:S], start=True, stop=False, skip_group_check=True)
    return pe.matmul(p.ps[rows, bank, P:S], v[:, 1, cols], weights[:, S:384], start=False, stop=True,
                     skip_group_check=True)


HYBRID_SEMS = RMS_SEMS + [
    "params", "wf_loaded", "f_rows_mm", "f_rows", "wf_hi", "wf_ready", "pads", "u_copied", "gelu_done", "xc_done", "gate_mm", "ri_done", "lam_abs", "lam_ln",
    "lam_done", "log_a", "a_done", "th_done", "one_minus", "root_done", "b_done", "y_rnn", "y_hi", "y_lo", "qkv_done",
    "f_mm", "f_ready", "f_ln", "logf", "cum_mm", "cums", "qk_ss", "qk_std", "qk_normed", "qkT_mm", "qkT_done", "s_mm", "z_done",
    "max_done", "p_exp", "p_done", "pT_mm", "pT_done", "o_mm", "o_done", "x_added", "scalar_steps", "vector_steps"]


def hybrid_stage(nc, p, a, u0):
    with ExitStack() as ctx:
        enter = ctx.enter_context

        def sb(name, shape, dt=F32):
            return enter(nc.sbuf_tensor(name, shape, dt))

        w = p.w
        sem = {s: enter(nc.semaphore(f"hybrid_{s}")) for s in HYBRID_SEMS}
        yT = [sb(n, [P, KT, S], F32R) for n in ("hy_yT_hi", "hy_yT_lo")]
        wf = [sb(n, [P, KT, FOX_HEADS], F32R) for n in ("wf_hi", "wf_lo")]
        wf_raw = sb("wf_raw", [P, KT * FOX_HEADS])
        uc = sb("uc", [P, 4, S + 3])
        xc = sb("xc", [P, 4, S])
        gl = sb("gl", [P, 4, S])
        ri = sb("ri", [P, 2, 4, S])
        la = sb("la", [P, 4, S])
        th = sb("th", [P, 4, S])
        gw = sb("gw", [P, 2, 4, P])
        pp = sb("pp", [P, 4 * 4 + 4 + 8 + 4])
        fb = sb("fb", [P, FOX_HEADS])
        qk_gain = sb("qk_gain", [P, 2, HD])
        qkv = sb("qkv", [P, TT, 3, 512])
        qk_sq = sb("qk_sq", [P, 1024])
        qkT = sb("qkT", [P, 8, S])
        yF = sb("hy_yF", [P, 4, S])
        f_rows = sb("f_rows", [FOX_HEADS, S])
        zs = sb("zs", [P, 2, 384])
        pT = sb("pT", [P, 2, 384])
        sm = sb("hy_sm", [P, 256])
        ps, ident, tri, ones = p.ps, p.ident, p.tri, p.ones
        conv_w, conv_b, gate_b, lam = (pp[:, 0:16].rearrange("p (c j) -> p c j", j=4), pp[:, 16:20],
                                       pp[:, 20:28].rearrange("p (g c) -> p g c", g=2), pp[:, 28:32])
        lam1, lam2 = sm[:, 0:4], sm[:, 4:8]
        f1, f2, lf, nlf, cf, ctot = (sm[:, 8 + 16 * i:24 + 16 * i].rearrange("p (t h) -> p t h", t=TT) for i in range(6))
        qs = sm[:, 104:136].rearrange("p (t h) -> p t h", t=TT)
        mx, sums = sm[:, 136:152].rearrange("p (h t) -> p h t", t=TT), sm[:, 152:168].rearrange("p (h t) -> p h t", t=TT)
        one = sm[:, 168:169]
        f_rows_ps = ps[0:FOX_HEADS, 6, 0:S]
        gate_banks = (4, 2)
        qkv_banks = ((0, 1), (0, 1), (2, 3))
        f_ps = ps[:, 7, 0:16].rearrange("p (t h) -> p t h", t=TT)
        cum_ps = ps[:, 7, 32:64].rearrange("p (a t h) -> p a t h", a=2, t=TT)
        U_QKV = u0 + RNN_UNITS
        U_OUT = U_QKV + FOX_QKV_UNITS
        with nc.Block() as block:
            @block.sync
            def _(sp):
                sp.dma_start(p.gain[:, :], a["mix_norm_2"][0]).then_inc(sem["gain_cols"], 16)
                sp.dma_start(wf_raw[:, :], a["wf"]).then_inc(sem["wf_loaded"], 16)
                sp.dma_start(pp[:, :], a["pp"]).then_inc(sem["params"], 16)
                sp.dma_start(gw[:, :, :, :], a["gate_blocks"]).then_inc(sem["params"], 16)
                sp.dma_start(fb[:, :], a["fox_fgate_b_2"][0].partition_broadcast(P)).then_inc(sem["params"], 16)
                for i in range(2):
                    sp.dma_start(qk_gain[:, i, :], a["fox_qk_norm_2"][0, i].partition_broadcast(P)).then_inc(sem["params"], 16)
                for u in range(u0 + RING, U_OUT + HY_OUT_UNITS):
                    w.load(sp, a["w2h"][u - u0], u)
                p.load_first(sp, U_OUT + HY_OUT_UNITS)

            n_params = 16 * (2 + 3)

            @block.gpsimd
            def _(pool):
                pool.memset(uc[:, :, 0:3], 0.0).then_inc(sem["pads"], 1)
                pool.memset(one, 1.0).then_inc(sem["pads"], 1)

            @block.scalar
            def _(act):
                chain = Chain(act, sem["scalar_steps"])
                rms_scalar(act, p.x, p.junk, p.ss, p.std, p.eps, ps, p.gain, p.xT[0], sem)
                act.wait_ge(sem["wf_loaded"], 16)
                act.activation(wf[0][:, :, :].rearrange("p a b -> p (a b)"), wf_raw[:, :], ACT.Copy).then_inc(sem["wf_hi"], 1)
                w.hi_through(act, u0 + 3)
                act.wait_ge(sem["pads"], 2)
                for i in range(2):
                    act.wait_ge(w.used, u0 + i + 1)
                    act.activation(uc[:, 2 * i:2 * i + 2, 3:], ps[:, i, :].rearrange("p (a b) -> p a b", a=2), ACT.Copy)\
                       .then_inc(sem["u_copied"], 1)
                    w.hi_through(act, u0 + i + 4)
                act.wait_ge(sem["f_rows_mm"], 1)
                act.activation(f_rows[:, :], f_rows_ps, ACT.Copy).then_inc(sem["f_rows"], 1)
                for i in range(2):
                    act.wait_ge(w.used, u0 + i + 3)
                    act.activation(gl[:, 2 * i:2 * i + 2, :].rearrange("p a b -> p (a b)"), ps[:, 2 + i, :],
                                   ACT.Gelu_apprx_tanh).then_inc(sem["gelu_done"], 1)
                    if i == 0:
                        w.hi_through(act, u0 + 6)

                def qkv_columns(i):
                    act.wait_ge(w.used, U_QKV + 2 * i + 2)
                    for t in range(TT):
                        act.activation(qkv[:, t, i, :], ps[:, qkv_banks[i][t], :], ACT.Copy).then_inc(sem["qkv_done"], 1)

                act.wait_ge(sem["params"], n_params)
                act.preload_act_table_set("natural_log_exp_and_others")
                chain.step(act.activation(lam1, lam, ACT.Abs))
                act.wait_ge(sem["f_ready"], 1)
                chain.step(act.activation(f2, f1, ACT.Abs))
                chain.settle()
                chain.step(act.activation(lam1, lam1, ACT.Exp, scale=-1.0))
                chain.step(act.activation(f2, f2, ACT.Exp, scale=-1.0))
                chain.settle()
                act.activation(lam1, lam1, ACT.Ln, bias=one).then_inc(sem["lam_ln"], 1)
                act.activation(f2, f2, ACT.Ln, bias=one).then_inc(sem["lam_ln"], 1)
                w.hi_through(act, u0 + 7)
                qkv_columns(0)
                for g in range(2):
                    for j in range(4):
                        act.wait_ge(sem["gate_mm"], 2 * g + j // 2 + 1)
                        act.activation(ri[:, g, j, :], ps[:, gate_banks[g] + j // 2, (j % 2) * S:(j % 2 + 1) * S], ACT.Sigmoid,
                                       bias=gate_b[:, g, j:j + 1]).then_inc(sem["ri_done"], 1)
                w.hi_through(act, U_QKV + 4)
                act.wait_ge(sem["log_a"], 4)
                act.activation(th[:, :, :], la[:, :, :], ACT.Tanh).then_inc(sem["th_done"], 1)
                act.wait_ge(sem["th_done"], 1)
                act.activation(la[:, :, :], la[:, :, :], ACT.Exp).then_inc(sem["a_done"], 1)
                act.preload_act_table_set("sqrt_and_others")
                w.hi_through(act, U_QKV + 5)
                act.wait_ge(sem["one_minus"], 1)
                act.activation(th[:, :, :], th[:, :, :], ACT.Sqrt).then_inc(sem["root_done"], 1)
                qkv_columns(1)
                act.wait_ge(sem["qk_ss"], 2)
                act.activation(qs, qs, ACT.Sqrt, bias=p.eps, scale=1.0 / HD).then_inc(sem["qk_std"], 1)
                w.hi_through(act, U_QKV + 6)
                act.preload_act_table_set("natural_log_exp_and_others")
                qkv_columns(2)
                for i in range(4):
                    act.wait_ge(sem["qkT_mm"], i + 1)
                    act.activation(qkT[:, 2 * i:2 * i + 2, :].rearrange("p a b -> p (a b)"), ps[:, i, :], ACT.Copy)\
                       .then_inc(sem["qkT_done"], 1)

                def exponentials(hd):
                    act.wait_ge(sem["max_done"], 2 * hd + 2)
                    for t in range(TT):
                        cols = slice(0, P) if t == 0 else slice(P, 384)
                        act.activation(zs[:, hd % 2, cols], zs[:, hd % 2, cols], ACT.Exp, bias=mx[:, hd, t:t + 1],
                                       accum_out=sums[:, hd, t:t + 1]).then_inc(sem["p_exp"], 1)

                w.hi_through(act, U_QKV + 7)
                exponentials(0)
                for hd in range(FOX_HEADS):
                    if hd + 1 < FOX_HEADS:
                        exponentials(hd + 1)
                    if hd == 2:
                        w.hi_through(act, U_QKV + 8)
                    act.wait_ge(sem["pT_mm"], hd + 1)
                    if hd >= 2:
                        act.wait_ge(sem["o_mm"], hd - 1)
                    act.activation(pT[:, hd % 2, :], ps[:, 4 + hd % 2, 0:384], ACT.Copy).then_inc(sem["pT_done"], 1)
                    if hd == 1:
                        act.wait_ge(sem["y_rnn"], 4)
                        for j in range(2):
                            act.activation(yT[0][:, 2 * j:2 * j + 2, :], xc[:, 2 * j:2 * j + 2, :], ACT.Copy)\
                               .then_inc(sem["y_hi"], 1)
                for j in range(4):
                    act.wait_ge(sem["o_done"], j + 1)
                    act.activation(yT[0][:, 4 + j, :], yF[:, j, :], ACT.Copy).then_inc(sem["y_hi"], 1)
                w.hi_through(act, U_OUT + 5)

            @block.vector
            def _(dve):
                chain = Chain(dve, sem["vector_steps"])
                rms_vector(dve, chain, p.x, p.xn, p.ss, p.std, ps, p.gain, p.xT, sem)
                dve.wait_ge(sem["wf_hi"], 1)
                dve.tensor_tensor(wf[1][:, :, :].rearrange("p a b -> p (a b)"), wf_raw[:, :],
                                  wf[0][:, :, :].rearrange("p a b -> p (a b)").bitcast(F32), ALU.subtract)\
                   .then_inc(sem["wf_ready"], 1)
                w.lo_through(dve, u0 + 4)
                dve.wait_ge(sem["params"], n_params)
                dve.wait_ge(sem["u_copied"], 2)
                for j in range(4):
                    for c in range(4):
                        tap, src, dst = conv_w[:, c, j:j + 1], uc[:, c, j:j + S], xc[:, c, :]
                        if j == 0:
                            ins = dve.tensor_scalar(dst, src, tap, conv_b[:, c:c + 1], ALU.mult, ALU.add)
                        else:
                            ins = dve.scalar_tensor_tensor(dst, src, tap, dst, ALU.mult, ALU.add)
                        if j == 3:
                            ins.then_inc(sem["xc_done"], 1)
                        else:
                            chain.step(ins)
                    if j < 3:
                        chain.settle()
                w.lo_through(dve, u0 + 5)
                dve.wait_ge(sem["f_mm"], 1)
                chain.step(dve.tensor_tensor(f1, f_ps, fb[:, :].unsqueeze(1).broadcast_to([P, TT, FOX_HEADS]), ALU.add))
                chain.settle()
                dve.tensor_scalar(f1, f1, -1.0, None, ALU.mult).then_inc(sem["f_ready"], 1)
                w.lo_through(dve, U_QKV + 3)

                def squares(i):
                    dve.wait_ge(sem["qkv_done"], 2 * i + 2)
                    if i:
                        dve.wait_ge(sem["qk_ss"], i)
                    part = qkv[:, :, i, :]
                    chain.step(dve.tensor_tensor(qk_sq[:, :].rearrange("p (t n) -> p t n", t=TT), part, part, ALU.mult))
                    chain.settle()
                    dve.tensor_reduce(qs[:, :, 8 * i:8 * i + 8], qk_sq[:, :].rearrange("p (t h d) -> p t h d", t=TT, d=HD),
                                      AX.X, ALU.add).then_inc(sem["qk_ss"], 1)

                squares(0)
                dve.wait_ge(sem["lam_ln"], 2)
                dve.wait_ge(sem["f_ready"], 1)
                chain.step(dve.tensor_scalar(lam2, lam, -1.0, 0.0, ALU.mult, ALU.max))
                chain.step(dve.scalar_tensor_tensor(lf, f1, 0.0, f2, ALU.max, ALU.add))
                chain.settle()
                chain.step(dve.tensor_tensor(lam2, lam2, lam1, ALU.add))
                dve.tensor_copy(nlf, lf).then_inc(sem["logf"], 1)
                dve.tensor_scalar(lf, lf, -1.0, None, ALU.mult).then_inc(sem["logf"], 1)
                chain.settle()
                chain.step(dve.tensor_scalar(lam2, lam2, -RG_C, None, ALU.mult))
                chain.settle()
                for j in range(4):
                    dve.wait_ge(sem["ri_done"], j + 1)
                    dve.tensor_scalar(la[:, j, :], ri[:, 0, j, :], lam2[:, j:j + 1], None, ALU.mult).then_inc(sem["log_a"], 1)
                w.lo_through(dve, U_QKV + 4)
                dve.wait_ge(sem["ri_done"], 8)
                chain.step(dve.tensor_tensor(xc[:, :, :], xc[:, :, :], ri[:, 1], ALU.mult))
                dve.wait_ge(sem["a_done"], 1)
                chain.step(dve.tensor_tensor(ri[:, 0], la[:, :, :], la[:, :, :], ALU.mult))
                chain.settle()
                chain.step(dve.tensor_scalar(ri[:, 0], ri[:, 0], -1.0, -1.0, ALU.mult, ALU.add))
                chain.settle()
                dve.tensor_tensor(th[:, :, :], th[:, :, :], ri[:, 0], ALU.mult).then_inc(sem["one_minus"], 1)
                w.lo_through(dve, U_QKV + 5)
                squares(1)
                dve.wait_ge(sem["qk_std"], 1)
                chain.step(dve.reciprocal(qs, qs))
                chain.settle()
                chain.step(dve.tensor_scalar(qs[:, :, 0:8], qs[:, :, 0:8], HD ** -0.5, None, ALU.mult))
                chain.settle()
                for t in range(TT):
                    both = qkv[:, t, 0:2, :].rearrange("p a (h d) -> p (a h) d", d=HD)
                    chain.step(dve.tensor_tensor(both, both, qs[:, t, :].unsqueeze(2).broadcast_to([P, 16, HD]), ALU.mult))
                chain.settle()
                for t in range(TT):
                    for i in range(2):
                        part = qkv[:, t, i, :].rearrange("p (h d) -> p h d", d=HD)
                        dve.tensor_tensor(part, part, qk_gain[:, i, :].unsqueeze(1).broadcast_to([P, 8, HD]), ALU.mult)\
                           .then_inc(sem["qk_normed"], 1)
                dve.wait_ge(sem["cum_mm"], 1)
                chain.step(dve.tensor_copy(cf, cum_ps[:, 0]))
                chain.step(dve.tensor_copy(ctot, cum_ps[:, 1]))
                chain.settle()
                chain.step(dve.tensor_tensor(cf[:, 1, :], cf[:, 1, :], ctot[:, 0, :], ALU.add))
                chain.settle()
                w.lo_through(dve, U_QKV + 7)

                def recurrence(step):
                    if step == 0:
                        dve.wait_ge(sem["root_done"], 1)
                        chain.step(dve.tensor_tensor(xc[:, :, :], xc[:, :, :], th[:, :, :], ALU.mult))
                        chain.settle()
                        for j in range(4):
                            chain.step(dve.tensor_tensor_scan(th[:, j, :], la[:, j, :], xc[:, j, :], 0.0, ALU.mult, ALU.add))
                    elif step == 1:
                        dve.wait_ge(sem["gelu_done"], 2)
                        for j in range(4):
                            dve.tensor_tensor(xc[:, j, :], th[:, j, :], gl[:, j, :], ALU.mult).then_inc(sem["y_rnn"], 1)
                    elif step == 4:
                        w.lo_through(dve, U_QKV + 8)
                    elif step == 3:
                        for j in range(2):
                            dve.wait_ge(sem["y_hi"], j + 1)
                            dve.tensor_tensor(yT[1][:, 2 * j:2 * j + 2, :], xc[:, 2 * j:2 * j + 2, :],
                                              yT[0][:, 2 * j:2 * j + 2, :].bitcast(F32), ALU.subtract).then_inc(sem["y_lo"], 1)

                def maxima(hd):
                    z = zs[:, hd % 2, :]
                    dve.wait_ge(sem["s_mm"], hd + 1)
                    if hd >= 2:
                        dve.wait_ge(sem["pT_mm"], hd - 1)
                    chain.step(dve.scalar_tensor_tensor(z[:, 0:P], ps[:, hd % 2, 0:P], cf[:, 0, hd:hd + 1], p.causal[:, P:S],
                                                        ALU.add, ALU.add))
                    chain.step(dve.scalar_tensor_tensor(z[:, P:384], ps[:, hd % 2, P:384], cf[:, 1, hd:hd + 1], p.causal,
                                                        ALU.add, ALU.add))
                    chain.settle()
                    for t in range(TT):
                        dve.tensor_reduce(mx[:, hd, t:t + 1], z[:, 0:P] if t == 0 else z[:, P:384], AX.X, ALU.max,
                                          negate=True).then_inc(sem["max_done"], 1)

                def output(pair):
                    dve.wait_ge(sem["o_mm"], 2 * pair + 2)
                    dve.tensor_copy(yF[:, pair, :], ps[:, 6 + pair % 2, 0:S]).then_inc(sem["o_done"], 1)

                maxima(0)
                for hd in range(FOX_HEADS):
                    if hd + 1 < FOX_HEADS:
                        maxima(hd + 1)
                    z = zs[:, hd % 2, :]
                    dve.wait_ge(sem["p_exp"], 2 * hd + 2)
                    chain.step(dve.reciprocal(sums[:, hd, :], sums[:, hd, :]))
                    chain.settle()
                    for t in range(TT):
                        part = z[:, 0:P] if t == 0 else z[:, P:384]
                        dve.tensor_scalar(part, part, sums[:, hd, t:t + 1], None, ALU.mult).then_inc(sem["p_done"], 1)
                    recurrence(hd)
                    if hd % 2 == 0 and hd >= 2:
                        output(hd // 2 - 1)
                output(FOX_HEADS // 2 - 1)
                for j in range(4):
                    dve.wait_ge(sem["y_hi"], 2 + j + 1)
                    dve.tensor_tensor(yT[1][:, 4 + j, :], yF[:, j, :], yT[0][:, 4 + j, :].bitcast(F32), ALU.subtract)\
                       .then_inc(sem["y_lo"], 1)
                w.lo_through(dve, U_OUT + 5)
                add_to_x(dve, w, U_OUT + HY_OUT_UNITS, p.x, p.acc, 1.0, sem)

            @block.tensor
            def _(pe):
                norm_transposes(pe, ps, p.xn, ident, sem["x_normed"], (1, 2), sem)
                for u in range(2):
                    split_tiles(pe, w, ps, u0 + u, u, p.xT, sem["xT_ready"] if u == 0 else None)
                pe.wait_ge(sem["wf_ready"], 1)
                for k in range(KT):
                    mm = split_matmul(pe, f_rows_ps, (wf[0][:, k, :], wf[1][:, k, :]), (p.xT[0][:, k, :], p.xT[1][:, k, :]),
                                      k == 0, k == KT - 1)
                mm.then_inc(sem["f_rows_mm"], 1)
                split_tiles(pe, w, ps, u0 + 2, 2, p.xT)
                pe.wait_ge(sem["f_rows"], 1)
                for t in range(TT):
                    mm = pe.transpose(f_ps[:, t, :], f_rows[:, t * P:(t + 1) * P], ident[0:FOX_HEADS, 0:FOX_HEADS])
                mm.then_inc(sem["f_mm"], 1)
                split_tiles(pe, w, ps, u0 + 3, 3, p.xT)
                pe.wait_ge(sem["u_copied"], 2)
                split_group(pe, w, ps, U_QKV, qkv_banks[0], p.xT)
                pe.wait_ge(sem["xc_done"], 4)
                pe.wait_ge(sem["params"], n_params)
                for g in range(2):
                    if g == 1:
                        pe.wait_ge(sem["gelu_done"], 2)
                    for j in range(4):
                        mm = pe.matmul(ps[:, gate_banks[g] + j // 2, (j % 2) * S:(j % 2 + 1) * S], gw[:, g, j, :], xc[:, j, :],
                                       start=True, stop=True)
                        if j % 2:
                            mm.then_inc(sem["gate_mm"], 1)
                pe.wait_ge(sem["qkv_done"], 2)
                split_group(pe, w, ps, U_QKV + 2, qkv_banks[1], p.xT)
                pe.wait_ge(sem["logf"], 2)
                for t in range(TT):
                    pe.matmul(cum_ps[:, 0, t, :], tri, lf[:, t, :], start=True, stop=True)
                    mm = pe.matmul(cum_ps[:, 1, t, :], ones, lf[:, t, :], start=True, stop=True)
                mm.then_inc(sem["cum_mm"], 1)
                pe.wait_ge(sem["ri_done"], 8)
                split_group(pe, w, ps, U_QKV + 4, qkv_banks[2], p.xT)
                pe.wait_ge(sem["qk_normed"], 4)
                for i in range(4):
                    if i == 2:
                        pe.wait_ge(sem["qkv_done"], 6)
                    for k in range(2):
                        for t in range(TT):
                            tile = 2 * i + k
                            mm = pe.transpose(ps[:, i, k * S + t * P:k * S + (t + 1) * P],
                                              qkv[:, t, tile // 4, (tile % 4) * P:(tile % 4 + 1) * P], ident)
                    mm.then_inc(sem["qkT_mm"], 1)
                pe.wait_ge(sem["qkT_done"], 4)

                def scores(hd):
                    rows = slice(HD * (hd % 2), HD * (hd % 2) + HD)
                    q, k = qkT[rows, hd // 2, :], qkT[rows, 4 + hd // 2, :]
                    if hd >= 2:
                        pe.wait_ge(sem["max_done"], 2 * hd - 2)
                    pe.matmul(ps[:, hd % 2, 0:P], q[:, 0:P], k[:, 0:P], start=True, stop=False, skip_group_check=True)
                    pe.matmul(ps[:, hd % 2, P:384], q[:, P:S], k, start=False, stop=False, skip_group_check=True)
                    decays = [nlf[:, t, hd:hd + 1].broadcast_to([P, P]) for t in range(TT)]
                    pe.matmul(ps[:, hd % 2, 0:P], decays[0], tri, start=False, stop=False, skip_group_check=True)
                    pe.matmul(ps[:, hd % 2, P:S], decays[0], tri, start=False, stop=False, skip_group_check=True)
                    pe.matmul(ps[:, hd % 2, S:384], decays[0], ones, start=False, stop=False, skip_group_check=True)
                    pe.matmul(ps[:, hd % 2, S:384], decays[1], tri, start=False, stop=True, skip_group_check=True)\
                      .then_inc(sem["s_mm"], 1)

                def weighted_sum(hd):
                    pe.wait_ge(sem["pT_done"], hd + 1)
                    if hd % 2 == 0 and hd >= 4:
                        pe.wait_ge(sem["o_done"], hd // 2 - 1)
                    heads_out(pe, p, hd, 6 + (hd // 2) % 2, qkv[:, :, 2, :], pT[:, hd % 2, :]).then_inc(sem["o_mm"], 1)

                scores(0)
                scores(1)
                for hd in range(FOX_HEADS):
                    if hd + 2 < FOX_HEADS:
                        scores(hd + 2)
                    pe.wait_ge(sem["p_done"], 2 * hd + 2)
                    if hd >= 2:
                        pe.wait_ge(sem["pT_done"], hd - 1)
                    z = zs[:, hd % 2, :]
                    for i in range(3):
                        mm = pe.transpose(ps[:, 4 + hd % 2, i * P:(i + 1) * P], z[:, i * P:(i + 1) * P], ident)
                    mm.then_inc(sem["pT_mm"], 1)
                    if hd:
                        weighted_sum(hd - 1)
                weighted_sum(FOX_HEADS - 1)
                pe.wait_ge(sem["y_lo"], 6)
                for half in range(2):
                    split_group(pe, w, ps, U_OUT + 2 * half, (half, 2 + half), yT)
        end_stage(nc, sem.values())


SB_SEMS = RMS_SEMS + ["qk_done", "v_done", "z_mm", "abs_done", "ln_done", "sp_done", "e_mm", "e_min", "w_exp", "w_done", "o_mm",
                      "y_hi", "y_lo", "x_added", "scalar_steps", "vector_steps"]


def stick_stage(nc, p, a, u0):
    with ExitStack() as ctx:
        enter = ctx.enter_context

        def sb(name, shape, dt=F32):
            return enter(nc.sbuf_tensor(name, shape, dt))

        w = p.w
        sem = {s: enter(nc.semaphore(f"stick_{s}")) for s in SB_SEMS}
        yT = [sb(n, [P, KT, S], F32R) for n in ("sb_yT_hi", "sb_yT_lo")]
        qkT = sb("sb_qkT", [P, 16, S])
        v = sb("sb_v", [P, TT, D])
        ln = sb("sb_ln", [P, 2, 384])
        sp_ = sb("sb_sp", [P, 2, 384])
        wt = sb("sb_w", [P, 2, 384])
        ps = p.ps
        U_V = u0 + SB_QK_UNITS
        U_OUT = U_V + SB_V_UNITS

        def diagonals(t):
            return t.rearrange("p (a b) -> p a b", b=P)[:, 0:3:2, :]

        with nc.Block() as block:
            @block.sync
            def _(sp):
                sp.dma_start(p.gain[:, :], a["mix_norm_2"][1]).then_inc(sem["gain_cols"], 16)
                for u in range(u0 + RING, U_OUT + SB_OUT_UNITS):
                    w.load(sp, a["w2s"][u - u0], u)
                p.load_first(sp, U_OUT + SB_OUT_UNITS)

            @block.scalar
            def _(act):
                chain = Chain(act, sem["scalar_steps"])
                rms_scalar(act, p.x, p.junk, p.ss, p.std, p.eps, ps, p.gain, p.xT[0], sem)
                for u in range(SB_QK_UNITS):
                    w.hi_through(act, u0 + u + 2)
                    act.wait_ge(w.used, u0 + u + 1)
                    act.activation(qkT[:, 2 * u:2 * u + 2, :].rearrange("p a b -> p (a b)"), ps[:, u % 4, :], ACT.Copy,
                                   scale=HD ** -0.5 if u < 4 else 1.0).then_inc(sem["qk_done"], 1)
                for i in range(2):
                    w.hi_through(act, U_V + 2 * i + 2)
                    act.wait_ge(w.used, U_V + 2 * i + 2)
                    for t in range(TT):
                        act.activation(v[:, t, i * 512:(i + 1) * 512], ps[:, 2 * i + t, :], ACT.Copy).then_inc(sem["v_done"], 1)
                w.hi_through(act, U_OUT + 2)
                act.preload_act_table_set("natural_log_exp_and_others")

                def softplus(hd, between=()):
                    act.wait_ge(sem["z_mm"], hd + 1)
                    if hd >= 2:
                        act.wait_ge(sem["sp_done"], hd - 1)
                    l = ln[:, hd % 2, :]
                    chain.step(act.activation(l, ps[:, hd % 4, 0:384], ACT.Abs))
                    if between:
                        exponentials(between[0])
                    chain.settle()
                    chain.step(act.activation(l, l, ACT.Exp, scale=-1.0))
                    if len(between) > 1:
                        output(between[1])
                    chain.settle()
                    act.activation(l, l, ACT.Ln, bias=p.one).then_inc(sem["ln_done"], 1)

                def exponentials(hd):
                    act.wait_ge(sem["e_min"], hd + 1)
                    act.activation(wt[:, hd % 2, :], wt[:, hd % 2, :], ACT.Exp).then_inc(sem["w_exp"], 1)

                def output(tile):
                    act.wait_ge(sem["o_mm"], 2 * tile + 2)
                    act.activation(yT[0][:, tile, :], ps[:, 4 + tile % 2, 0:S], ACT.Copy).then_inc(sem["y_hi"], 1)

                softplus(0)
                softplus(1)
                for hd in range(SB_HEADS):
                    tiles = (hd // 2 - 1,) if hd >= 2 and hd % 2 == 0 else ()
                    if hd + 2 < SB_HEADS:
                        softplus(hd + 2, (hd, *tiles))
                    else:
                        exponentials(hd)
                        for tile in tiles:
                            output(tile)
                output(SB_HEADS // 2 - 1)
                w.hi_through(act, U_OUT + 5)

            @block.vector
            def _(dve):
                chain = Chain(dve, sem["vector_steps"])
                rms_vector(dve, chain, p.x, p.xn, p.ss, p.std, ps, p.gain, p.xT, sem)
                w.lo_through(dve, U_OUT + 2)
                strict2 = p.strict.unsqueeze(1).broadcast_to([P, 2, P])

                def softplus(hd):
                    dve.wait_ge(sem["ln_done"], hd + 1)
                    s_ = sp_[:, hd % 2, :]
                    if hd >= 2:
                        dve.wait_ge(sem["e_mm"], hd - 1)
                    chain.step(dve.scalar_tensor_tensor(s_, ps[:, hd % 4, 0:384], 0.0, ln[:, hd % 2, :], ALU.max, ALU.add))
                    chain.settle()
                    dve.tensor_tensor(diagonals(s_), diagonals(s_), strict2, ALU.mult).then_inc(sem["sp_done"], 1)

                def exponents(hd):
                    dve.wait_ge(sem["e_mm"], hd + 1)
                    if hd >= 2:
                        dve.wait_ge(sem["o_mm"], hd - 1)
                    w_ = wt[:, hd % 2, :]
                    dve.tensor_scalar(w_, ps[:, hd % 4, 0:384], 0.0, None, ALU.min).then_inc(sem["e_min"], 1)

                def weights(hd):
                    w_ = wt[:, hd % 2, :]
                    dve.wait_ge(sem["w_exp"], hd + 1)
                    dve.tensor_tensor(diagonals(w_), diagonals(w_), strict2, ALU.mult).then_inc(sem["w_done"], 1)

                def output(tile):
                    dve.wait_ge(sem["y_hi"], tile + 1)
                    dve.tensor_tensor(yT[1][:, tile, :], ps[:, 4 + tile % 2, 0:S], yT[0][:, tile, :].bitcast(F32),
                                      ALU.subtract).then_inc(sem["y_lo"], 1)

                softplus(0)
                softplus(1)
                exponents(0)
                for hd in range(SB_HEADS):
                    weights(hd)
                    if hd + 1 < SB_HEADS:
                        exponents(hd + 1)
                    if hd + 2 < SB_HEADS:
                        softplus(hd + 2)
                    if hd >= 2 and hd % 2 == 0:
                        output(hd // 2 - 1)
                output(SB_HEADS // 2 - 1)
                w.lo_through(dve, U_OUT + 5)
                add_to_x(dve, w, U_OUT + SB_OUT_UNITS, p.x, p.acc, 1.0, sem)

            @block.tensor
            def _(pe):
                norm_transposes(pe, ps, p.xn, p.ident, sem["x_normed"], (1, 2), sem)
                for u in range(SB_QK_UNITS):
                    if u >= 4:
                        pe.wait_ge(sem["qk_done"], u - 3)
                    split_tiles(pe, w, ps, u0 + u, u % 4, p.xT, sem["xT_ready"] if u == 0 else None)
                for i in range(2):
                    pe.wait_ge(sem["qk_done"], 6 + 2 * i)
                    split_group(pe, w, ps, U_V + 2 * i, (2 * i, 2 * i + 1), p.xT)

                def scores(hd):
                    rows = slice(HD * (hd % 2), HD * (hd % 2) + HD)
                    q, k = qkT[rows, hd // 2, :], qkT[rows, 8 + hd // 2, :]
                    if hd >= 4:
                        pe.wait_ge(sem["e_min"], hd - 3)
                    pe.matmul(ps[:, hd % 4, 0:S], k[:, 0:P], q, start=True, stop=False, skip_group_check=True)
                    pe.matmul(ps[:, hd % 4, S:384], k[:, P:S], q[:, P:S], start=False, stop=False, skip_group_check=True)\
                      .then_inc(sem["z_mm"], 1)

                def exponents(hd):
                    s_ = sp_[:, hd % 2, :]
                    pe.wait_ge(sem["sp_done"], hd + 1)
                    pe.matmul(ps[:, hd % 4, 0:S], p.neg_from, s_[:, 0:S], start=False, stop=False, skip_group_check=True)
                    pe.matmul(ps[:, hd % 4, P:S], p.neg_ones, s_[:, S:384], start=False, stop=False, skip_group_check=True)
                    pe.matmul(ps[:, hd % 4, S:384], p.neg_from, s_[:, S:384], start=False, stop=True, skip_group_check=True)\
                      .then_inc(sem["e_mm"], 1)

                pe.wait_ge(sem["v_done"], 4)
                for hd in range(3):
                    scores(hd)
                exponents(0)
                for hd in range(SB_HEADS):
                    if hd + 3 < SB_HEADS:
                        scores(hd + 3)
                    if hd + 1 < SB_HEADS:
                        exponents(hd + 1)
                    pe.wait_ge(sem["w_done"], hd + 1)
                    if hd % 2 == 0 and hd >= 4:
                        pe.wait_ge(sem["y_lo"], hd // 2 - 1)
                    heads_out(pe, p, hd, 4 + (hd // 2) % 2, v, wt[:, hd % 2, :]).then_inc(sem["o_mm"], 1)
                pe.wait_ge(sem["y_lo"], 8)
                for half in range(2):
                    split_group(pe, w, ps, U_OUT + 2 * half, (half, 2 + half), yT)
        end_stage(nc, sem.values())


def block_two(nc, a):
    with ExitStack() as ctx:
        enter = ctx.enter_context

        def sb(name, shape, dt=F32):
            return enter(nc.sbuf_tensor(name, shape, dt))

        p = Parts()
        p.x = a["x_sb"]
        p.ps = enter(nc.psum_tensor("ps2", [P, 8, 512], F32))
        p.xT = [sb(n, [P, KT, S], F32R) for n in ("x2T_hi", "x2T_lo")]
        p.hT = [sb(n, [P, 2, S], F32R) for n in ("h2T_hi", "h2T_lo")]
        p.zero = sb("zero2", [P, P], F32R)
        p.xn = sb("xn", [P, TT, D])
        p.junk = sb("junk2", [P, D])[:, :]
        p.gate, p.h = sb("gate2", [P, 2, S]), sb("h2", [P, 2, S])
        cm = sb("cm2", [P, a["masks2"].shape[1]])
        p.gain = sb("gain2", [P, KT])
        sm = sb("sm2", [P, 8])
        p.ss, p.std, p.eps, p.one = sm[:, 0:2], sm[:, 2:4], sm[:, 4:5], sm[:, 5:6]
        p.ident, p.tri, p.strict, p.ones, p.neg_from, p.neg_ones = (cm[:, i * P:(i + 1) * P] for i in range(6))
        p.causal = cm[:, 6 * P:8 * P]
        p.acc, p.up_ps = p.ps[:, 0:4, :], p.ps[:, 4:6, :]
        with ExitStack() as c2:
            loaded = c2.enter_context(nc.semaphore("constants2"))
            with nc.Block() as block:
                @block.sync
                def _(sp):
                    sp.dma_start(cm[:, :], a["masks2"]).then_inc(loaded, 16)
                    sp.wait_ge(loaded, 16)

                @block.gpsimd
                def _(pool):
                    pool.memset(p.zero[:, :].bitcast(F32), 0.0)
                    pool.memset(p.eps, RMS_EPS)
                    pool.memset(p.one, 1.0)
            end_stage(nc, [loaded])
        p.w = a["ring"]
        p.w.begin(True)
        stages = [("ffn", 0), ("hybrid", 0), ("ffn", 1), ("ffn", 2), ("stick", 0), ("ffn", 3)]
        units = {"ffn": FFN_UNITS, "hybrid": RNN_UNITS + FOX_QKV_UNITS + HY_OUT_UNITS,
                 "stick": SB_QK_UNITS + SB_V_UNITS + SB_OUT_UNITS}
        u0 = 0
        for (kind, n), after in zip(stages, [*stages[1:], None]):
            def load_first(sp, u, after=after):
                if after[0] == "ffn":
                    ffn_load_first(sp, p.w, u, lambda pair, f: a["up"][DEPTH + after[1], pair, f])
                else:
                    for j in range(RING):
                        p.w.load(sp, a["w2h" if after[0] == "hybrid" else "w2s"][j], u + j)

            p.load_first = load_first
            if kind == "ffn":
                ffn_stage(nc, p, a, n, f"ffn{n}", u0, last=after is None)
            elif kind == "hybrid":
                hybrid_stage(nc, p, a, u0)
            else:
                stick_stage(nc, p, a, u0)
            u0 += units[kind]


def program(nc, a, out):
    with ExitStack() as ctx:
        x = ctx.enter_context(nc.sbuf_tensor("x", [P, TT, D], F32))
        a["x_sb"] = x
        a["ring"] = Weights(nc, ctx.enter_context, ctx.enter_context(nc.sbuf_tensor("w_raw", [P, RING, UNIT], F32)),
                            *(ctx.enter_context(nc.sbuf_tensor(n, [P, RING, UNIT], F32R)) for n in ("w_hi", "w_lo")))
        block_one(nc, a)
        block_two(nc, a)
        with ExitStack() as c:
            stored = c.enter_context(nc.semaphore("stored"))
            with nc.Block() as block:
                @block.sync
                def _(sp):
                    sp.dma_start(out[0].rearrange("(t p) n -> p t n", p=P), x[:, :, :]).then_inc(stored, 16)
                    sp.wait_ge(stored, 16)


def _units_by_tiles(m):
    n = m.shape[1]
    return m.reshape(KT, P, n // 256, 2, P).transpose(2, 1, 3, 0, 4).reshape(n // 256, P, UNIT)


def _units_by_groups(m):
    n = m.shape[1]
    return m.reshape(2, 4, P, n // 512, 512).transpose(3, 0, 2, 1, 4).reshape(2 * (n // 512), P, UNIT)


def _units_of_ffn(up, down):
    u = up.reshape(KT, P, 2, FPAIRS, 2, P).transpose(3, 4, 1, 2, 0, 5).reshape(FPAIRS, 2, P, UNIT)
    d = down.reshape(FPAIRS, 2, P, D).transpose(0, 2, 1, 3).reshape(FPAIRS, P, UNIT)
    return u, d


def _columns(m):
    return np.ascontiguousarray(np.swapaxes(m.reshape(*m.shape[:-1], -1, P), -1, -2))


def _masks():
    i = np.arange(P)
    j = i[:, None]
    tri, strict = (j <= i), (j < i)
    levels = []
    for lv in range(7):
        s = 1 << lv
        row, col = i[:, None], i[None, :]
        levels.append((row // (2 * s) == col // (2 * s)) & (row // s % 2 == 1) & (col // s % 2 == 0))
    ident, ones = np.eye(P), np.ones((P, P))
    m1 = np.concatenate([ident, tri, strict, ones, levels[0].T, *levels[1:]], 1).astype(np.float32)
    causal = np.where(i[None, :] <= i[:, None], 0.0, -BIG)
    m2 = np.concatenate([ident, tri, strict, ones, -(j >= i).astype(np.float32), -ones, np.zeros((P, P)), causal], 1)
    return m1, m2.astype(np.float32)


def _lay_out(i):
    i = {k: np.asarray(v) for k, v in i.items()}
    w1, wg = [], []
    cuts = np.cumsum([512, 512, 1024, 1024, 4, 4, 3072, 1024, 8, 8, 1024, 1024])[:-1]
    for l in range(DEPTH):
        qa, ka, va, oa, ia, fa, qkv, zb, be, ab, ga, gb = np.split(i["w_in"][l], cuts, axis=1)

        def pairs(gate, branch):
            both = np.stack([gate.reshape(D, KT, P), branch.reshape(D, KT, P)], 2).reshape(D, 2 * D)
            return _units_by_tiles(both)

        w1.append(np.concatenate([
            _units_by_tiles(qkv), _units_by_tiles(qa), _units_by_tiles(ka), _units_by_groups(va), _units_by_tiles(oa),
            _units_by_tiles(zb), pairs(ga, i["w_branch_a"][l]), pairs(gb, i["w_branch_b"][l]),
            _units_by_groups(i["w_out"][l])]))
        wg.append(np.concatenate([ia, fa, be, ab], 1).reshape(KT, P, N_GATES).transpose(1, 0, 2).reshape(P, -1))
    assert w1[0].shape[0] == MIX1_UNITS
    pa = np.zeros((DEPTH, P, 129), np.float32)
    for l in range(DEPTH):
        pa[l, :, 0:96] = i["conv_w"][l].reshape(4, 24, P).transpose(2, 1, 0).reshape(P, 96)
        pa[l, :, 96:100] = i["b_igate"][l]
        pa[l, :, 100:104] = i["b_fgate"][l]
        pa[l, :, 112:120] = i["dt_bias"][l]
        pa[l, :, 120:128] = i["a_log"][l]
        pa[l, :, 128] = i["g_gdn_norm"][l]
    ffn = [_units_of_ffn(i["w_ffn_up"][l], i["w_ffn_down"][l]) for l in range(DEPTH)]
    ffn += [_units_of_ffn(i["ffn_w_in_2"][l, j], i["ffn_w_out_2"][l, j]) for l in range(DEPTH) for j in range(2)]
    up2 = ffn[DEPTH][0]
    first2 = np.stack([up2[0, 0], up2[0, 1], up2[1, 0]])
    hy = i["hy_w_in_2"][0]
    w2h = np.concatenate([_units_by_tiles(hy[:, 0:1024]), _units_by_groups(hy[:, 1024:2560]), _units_by_groups(i["hy_w_out_2"][0])])
    sbw = i["sb_w_qkv_2"][0]
    w2s = np.concatenate([_units_by_tiles(sbw[:, 0:2048]), _units_by_groups(sbw[:, 2048:]), _units_by_groups(i["sb_w_out_2"][0])])
    pp = np.concatenate([i["rg_conv_w_2"][0].reshape(4, 4, P).transpose(2, 1, 0).reshape(P, 16), _columns(i["rg_conv_b_2"][0]),
                         i["rg_gate_b_2"][0].reshape(8, P).T, _columns(i["rg_lambda_2"][0])], 1)
    gate_blocks = np.zeros((P, 2, 4, P), np.float32)
    for b in range(8):
        r = slice((b % 2) * HD, (b % 2 + 1) * HD)
        gate_blocks[r, :, b // 2, r] = i["rg_gate_w_2"][0, :, b].transpose(1, 0, 2)
    m1, m2 = _masks()
    sel = np.zeros((A_HEADS, A_HEADS, P), np.float32)
    for hd in range(A_HEADS):
        sel[hd, hd] = 1.0
    return {
        "x": i["x"], "first": np.stack([*(m[0:RING] for m in w1), first2]), "w1": np.stack([m[RING:] for m in w1]), "wg": np.stack(wg), "pa": pa, "g_mlstm": i["g_mlstm_norm"],
        "ln1_g": i["ln1_g"], "ln1_b": i["ln1_b"], "ln2_g": i["ln2_g"], "ln2_b": i["ln2_b"],
        "up": np.stack([f[0] for f in ffn]), "dn": np.stack([f[1] for f in ffn]), "w2h": w2h, "w2s": w2s,
        "wf": hy[:, 2560:].reshape(KT, P, FOX_HEADS).transpose(1, 0, 2).reshape(P, -1), "pp": pp,
        "gate_blocks": gate_blocks, "fox_fgate_b_2": i["fox_fgate_b_2"], "fox_qk_norm_2": i["fox_qk_norm_2"],
        "ffn_norm_2": _columns(i["ffn_norm_2"].reshape(4, D)), "mix_norm_2": _columns(i["mix_norm_2"]),
        "masks": m1, "masks2": m2, "sel": sel,
    }


def kernel(**inputs):
    import concourse.bacc as bacc
    from concourse.bass_utils import run_bass_kernel_spmd

    nc = bacc.Bacc("TRN2", target_bir_lowering=False, num_devices=1)
    arrays, aps = {}, {}
    for name, array in _lay_out(inputs).items():
        array = np.ascontiguousarray(array)
        arrays[f"in_{name}"] = array
        aps[name] = nc.dram_tensor(f"in_{name}", array.shape, mybir.dt.from_np(array.dtype), kind="ExternalInput").ap()
    out = nc.dram_tensor("out", (1, S, D), F32, kind="ExternalOutput").ap()
    program(nc, aps, out)
    r = run_bass_kernel_spmd(nc, [arrays], core_ids=[0])
    return r.results[0]["out"]
```
